# Optimizing a Trainium2 kernel written in Bass

```python
import jax, jax.numpy as jnp
from jax import lax
import numpy as np
import math

D_MODEL = 1024
BATCH = 1
SEQ = 256
DEPTH = 1

GRID_W = 64
CTX_LEN = 256
N_HEADS = 4
D_KEY = D_MODEL // 2
D_VAL = D_MODEL
HEAD_K = D_KEY // N_HEADS
HEAD_V = D_VAL // N_HEADS
DECAY_RANK = 16
DECAY_TAU = 16.0
CHUNK = 64
D_CONV = D_MODEL
CONV_W = 3
D_FF = ((-(-8 * D_MODEL // 3)) + 255) // 256 * 256
EPS = 1e-6
IN_SPLITS = (D_KEY, D_KEY, D_VAL, D_VAL, 2 * DECAY_RANK, D_CONV, D_CONV, D_CONV, D_MODEL, D_MODEL)
N_IN = sum(IN_SPLITS)


def rmsnorm(x, g):
    xf = x.astype(jnp.float32)
    y = xf * lax.rsqrt(jnp.mean(xf * xf, axis=-1, keepdims=True) + EPS)
    return (y * g.astype(jnp.float32)).astype(x.dtype)

def modulate(h, shift, scale):
    return h * (1.0 + scale[:, None, :]) + shift[:, None, :]

def gla_chunked(q, k, v, log_a, s0):
    Bn, H, T, K = q.shape
    V = v.shape[-1]
    N = T // CHUNK
    f = lambda t: t.astype(jnp.float32).reshape(Bn, H, N, CHUNK, t.shape[-1])
    q, k, v, log_a = f(q), f(k), f(v), f(log_a)
    q = q * (K ** -0.5)
    b = jnp.cumsum(log_a, axis=3)
    b_mid = b[:, :, :, CHUNK // 2 - 1:CHUNK // 2, :]
    b_last = b[:, :, :, CHUNK - 1:, :]
    causal = jnp.tril(jnp.ones((CHUNK, CHUNK), dtype=bool))
    scores = jnp.einsum('bhnik,bhnjk->bhnij', q * jnp.exp(b - b_mid), k * jnp.exp(b_mid - b))
    scores = jnp.where(causal, scores, 0.0)
    o_intra = jnp.einsum('bhnij,bhnjv->bhniv', scores, v)
    kv = jnp.einsum('bhnjk,bhnjv->nbhkv', k * jnp.exp(b_last - b), v)
    decay = jnp.moveaxis(jnp.exp(b_last[:, :, :, 0, :]), 2, 0)

    def step(s, inp):
        d, kv_n = inp
        return d[..., None] * s + kv_n, s

    s_final, s_before = lax.scan(step, s0.astype(jnp.float32), (decay, kv))
    o_inter = jnp.einsum('bhnik,nbhkv->bhniv', q * jnp.exp(b), s_before)
    return (o_intra + o_inter).reshape(Bn, H, T, V), s_final

def gla_bidir(q, k, v, la_f, la_b, s0_f, s0_b):
    o_f, s_f = gla_chunked(q, k, v, la_f, s0_f)
    flip = lambda t: jnp.flip(t, axis=2)
    o_b, s_b = gla_chunked(flip(q), flip(k), flip(v), flip(la_b), s0_b)
    return o_f + flip(o_b), s_f, s_b

def project(h, w_in, w_dec_up, b_dec):
    Bn, T, _ = h.shape
    z = h @ w_in
    q, k, v, g, dd, cb, cc, ch, ga, gb = jnp.split(z, np.cumsum(IN_SPLITS)[:-1].tolist(), axis=-1)
    dd = dd.reshape(Bn, T, 2, DECAY_RANK)
    zd = jnp.einsum('btdr,drk->dbtk', dd, w_dec_up) + b_dec[:, None, None, :]
    log_a = jax.nn.log_sigmoid(zd.astype(jnp.float32)) / DECAY_TAU
    heads = lambda t, hd: t.reshape(Bn, T, N_HEADS, hd).transpose(0, 2, 1, 3)
    return (heads(q, HEAD_K), heads(k, HEAD_K), heads(v, HEAD_V), g,
            heads(log_a[0], HEAD_K), heads(log_a[1], HEAD_K), cb, cc, ch, ga, gb)

def seq_conv(u, w):
    pad = CONV_W // 2
    T = u.shape[1]
    up = jnp.pad(u, ((0, 0), (pad, pad), (0, 0)))
    y = up[:, 0:T] * w[0]
    for j in range(1, CONV_W):
        y = y + up[:, j:j + T] * w[j]
    return y

def merge_branches(o, g, cb, cc, ch, ga, gb, rows, g_head, w_gla_out, w_conv, w_conv_out, w_mix_out):
    Bn, H, T, V = o.shape
    o = rmsnorm(o, g_head).transpose(0, 2, 1, 3).reshape(Bn, T, H * V).astype(g.dtype)
    y_gla = (o * jax.nn.silu(g)) @ w_gla_out
    u = cc * ch
    if rows is None:
        uc = seq_conv(u, w_conv)
    else:
        uc = seq_conv(u.reshape(Bn * rows, T // rows, -1), w_conv).reshape(Bn, T, -1)
    y_conv = (cb * uc) @ w_conv_out
    merged = jax.nn.sigmoid(ga) * y_gla + jax.nn.sigmoid(gb) * y_conv
    return merged @ w_mix_out

def swiglu(h, w_in, w_out):
    a, b = jnp.split(h @ w_in, 2, axis=-1)
    return (jax.nn.silu(a) * b) @ w_out

def first_inputs(seed: int = 0) -> dict:
    key = jax.random.key(seed)
    ks = jax.random.split(key, 20)
    nrm = lambda k, shape, s: jax.random.normal(k, shape, jnp.float32) * s
    return {
        "x": nrm(ks[0], (BATCH, SEQ, D_MODEL), 1.0),
        "c": nrm(ks[1], (BATCH, D_MODEL), 1.0),
        "ctx": nrm(ks[2], (BATCH, CTX_LEN, D_MODEL), 1.0),
        "c_ctx": nrm(ks[3], (D_MODEL,), 1.0),
        "w_ada": nrm(ks[4], (DEPTH, D_MODEL, 6 * D_MODEL), 0.5 * D_MODEL ** -0.5),
        "b_ada": nrm(ks[5], (DEPTH, 6 * D_MODEL), 0.01),
        "g_mix": 1.0 + nrm(ks[6], (DEPTH, D_MODEL), 0.02),
        "w_in": nrm(ks[7], (DEPTH, D_MODEL, N_IN), D_MODEL ** -0.5),
        "w_dec_up": nrm(ks[8], (DEPTH, 2, DECAY_RANK, D_KEY), DECAY_RANK ** -0.5),
        "b_dec": nrm(ks[9], (DEPTH, 2, D_KEY), 0.1),
        "g_head": 1.0 + nrm(ks[10], (DEPTH, HEAD_V), 0.02),
        "w_gla_out": nrm(ks[11], (DEPTH, D_VAL, D_MODEL), D_VAL ** -0.5),
        "w_conv": nrm(ks[12], (DEPTH, CONV_W, D_CONV), CONV_W ** -0.5),
        "w_conv_out": nrm(ks[13], (DEPTH, D_CONV, D_MODEL), D_CONV ** -0.5),
        "w_mix_out": nrm(ks[14], (DEPTH, D_MODEL, D_MODEL), D_MODEL ** -0.5),
        "g_ffn": 1.0 + nrm(ks[15], (DEPTH, D_MODEL), 0.02),
        "w_ffn_in": nrm(ks[16], (DEPTH, D_MODEL, 2 * D_FF), D_MODEL ** -0.5),
        "w_ffn_out": nrm(ks[17], (DEPTH, D_FF, D_MODEL), D_FF ** -0.5),
        "g_final": 1.0 + nrm(ks[18], (D_MODEL,), 0.02),
    }

def first_block(x, c, ctx, c_ctx, w_ada, b_ada, g_mix, w_in, w_dec_up, b_dec, g_head, w_gla_out,
              w_conv, w_conv_out, w_mix_out, g_ffn, w_ffn_in, w_ffn_out, g_final):
    rows = x.shape[1] // GRID_W
    bc = ctx.shape[0]
    zeros_state = jnp.zeros((bc, N_HEADS, HEAD_K, HEAD_V), jnp.float32)
    for l in range(DEPTH):
        last = l == DEPTH - 1
        mod_lat = jnp.split(jax.nn.silu(c) @ w_ada[l] + b_ada[l], 6, axis=-1)
        mod_ctx = jnp.split(jax.nn.silu(c_ctx)[None, :] @ w_ada[l] + b_ada[l], 6, axis=-1)
        sh1, sc1, gt1, sh2, sc2, gt2 = mod_lat
        sh1c, sc1c, gt1c, sh2c, sc2c, gt2c = mod_ctx

        pl = project(modulate(rmsnorm(x, g_mix[l]), sh1, sc1), w_in[l], w_dec_up[l], b_dec[l])
        pc = project(modulate(rmsnorm(ctx, g_mix[l]), sh1c, sc1c), w_in[l], w_dec_up[l], b_dec[l])
        o_c, s_cf, s_cb = gla_bidir(pc[0], pc[1], pc[2], pc[4], pc[5], zeros_state, zeros_state)
        o_l, _, _ = gla_bidir(pl[0], pl[1], pl[2], pl[4], pl[5], s_cf, s_cb)
        mix_l = merge_branches(o_l, pl[3], pl[6], pl[7], pl[8], pl[9], pl[10], rows, g_head[l],
                               w_gla_out[l], w_conv[l], w_conv_out[l], w_mix_out[l])
        x = x + gt1[:, None, :] * mix_l
        if not last:
            mix_c = merge_branches(o_c, pc[3], pc[6], pc[7], pc[8], pc[9], pc[10], None, g_head[l],
                                   w_gla_out[l], w_conv[l], w_conv_out[l], w_mix_out[l])
            ctx = ctx + gt1c[:, None, :] * mix_c

        x = x + gt2[:, None, :] * swiglu(modulate(rmsnorm(x, g_ffn[l]), sh2, sc2), w_ffn_in[l], w_ffn_out[l])
        if not last:
            ctx = ctx + gt2c[:, None, :] * swiglu(modulate(rmsnorm(ctx, g_ffn[l]), sh2c, sc2c),
                                                  w_ffn_in[l], w_ffn_out[l])
    return rmsnorm(x, g_final)


Q_BLOCK = 128
D_FF_2 = 2816
FFN_RES_WEIGHT = 0.5
ADA_SUBLAYERS = 3
ADA_WIDTH = ADA_SUBLAYERS * 3 * D_MODEL
MLA_HEADS = 8
MLA_Q_RANK = 256
MLA_KV_RANK = 128
MLA_NOPE = 64
MLA_ROPE = 32
MLA_V = 64
ROPE_THETA = 10000.0
CA_HEADS = 8
CA_HEAD_DIM = 64
CA_LEFT_CHUNKS = 8
CA_BAND = CA_LEFT_CHUNKS + 1
MAX_REL_DIST = 256
CA_WIDTH = CA_HEADS * CA_HEAD_DIM
MLA_OUT_WIDTH = MLA_HEADS * MLA_V
W_IN_COLS = MLA_Q_RANK + MLA_KV_RANK + MLA_ROPE + 3 * CA_WIDTH + 2 * D_MODEL
NEG_INF = -1e30


def rmsnorm_2(x, g):
    xf = x.astype(jnp.float32)
    y = xf * lax.rsqrt(jnp.mean(xf * xf, axis=-1, keepdims=True) + EPS)
    return (y * g.astype(jnp.float32)).astype(x.dtype)

def modulate_2(h, shift, scale):
    return h * (1 + scale[:, None, :]) + shift[:, None, :]

def swiglu_2(h, w_in, w_out):
    gu = h @ w_in
    g, u = jnp.split(gu, 2, axis=-1)
    return (jax.nn.silu(g) * u) @ w_out

def rope(x, cos, sin):
    half = x.shape[-1] // 2
    x1, x2 = x[..., :half], x[..., half:]
    return jnp.concatenate([x1 * cos - x2 * sin, x1 * sin + x2 * cos], axis=-1).astype(x.dtype)

def mla_attention(q_lat, kv_lat, k_pe_raw, positions, q_norm, w_uq, kv_norm, w_ukv):
    B, S = q_lat.shape[:2]
    cq = rmsnorm_2(q_lat, q_norm)
    q = (cq @ w_uq).reshape(B, S, MLA_HEADS, MLA_NOPE + MLA_ROPE)
    q_nope, q_pe = q[..., :MLA_NOPE], q[..., MLA_NOPE:]
    ckv = rmsnorm_2(kv_lat, kv_norm)
    kv = (ckv @ w_ukv).reshape(B, S, MLA_HEADS, MLA_NOPE + MLA_V)
    k_nope, v = kv[..., :MLA_NOPE], kv[..., MLA_NOPE:]

    inv_freq = ROPE_THETA ** (-jnp.arange(0, MLA_ROPE, 2, dtype=jnp.float32) / MLA_ROPE)
    ang = positions.astype(jnp.float32)[..., None] * inv_freq
    cos, sin = jnp.cos(ang), jnp.sin(ang)
    q_pe = rope(q_pe, cos[:, :, None, :], sin[:, :, None, :])
    k_pe = rope(k_pe_raw, cos, sin)

    scale = (MLA_NOPE + MLA_ROPE) ** -0.5
    key_chunk = jnp.arange(S) // CHUNK

    def block(qi):
        start = qi * Q_BLOCK
        qn = lax.dynamic_slice_in_dim(q_nope, start, Q_BLOCK, axis=1)
        qp = lax.dynamic_slice_in_dim(q_pe, start, Q_BLOCK, axis=1)
        s = (jnp.einsum('bqhd,bkhd->bhqk', qn, k_nope)
             + jnp.einsum('bqhd,bkd->bhqk', qp, k_pe)).astype(jnp.float32) * scale
        q_chunk = (start + jnp.arange(Q_BLOCK)) // CHUNK
        mask = key_chunk[None, :] <= q_chunk[:, None]
        s = jnp.where(mask[None, None], s, NEG_INF)
        p = jax.nn.softmax(s, axis=-1).astype(v.dtype)
        return jnp.einsum('bhqk,bkhd->bqhd', p, v)

    o = lax.map(block, jnp.arange(S // Q_BLOCK))
    return jnp.moveaxis(o, 0, 1).reshape(B, S, MLA_OUT_WIDTH)

def chunk_attention(q, k, v, rel_bias):
    B, S = q.shape[:2]
    NC = S // CHUNK
    KB = CA_BAND * CHUNK
    q = q.reshape(B, NC, CHUNK, CA_HEADS, CA_HEAD_DIM)
    pad = ((0, 0), (CA_LEFT_CHUNKS, 0), (0, 0), (0, 0), (0, 0))
    kpad = jnp.pad(k.reshape(B, NC, CHUNK, CA_HEADS, CA_HEAD_DIM), pad)
    vpad = jnp.pad(v.reshape(B, NC, CHUNK, CA_HEADS, CA_HEAD_DIM), pad)
    idx = jnp.arange(NC)[:, None] + jnp.arange(CA_BAND)[None, :]
    kb = kpad[:, idx].reshape(B, NC, KB, CA_HEADS, CA_HEAD_DIM)
    vb = vpad[:, idx].reshape(B, NC, KB, CA_HEADS, CA_HEAD_DIM)

    s = jnp.einsum('bnqhd,bnkhd->bnhqk', q, kb).astype(jnp.float32) * CA_HEAD_DIM ** -0.5
    rel = CA_LEFT_CHUNKS * CHUNK + jnp.arange(CHUNK)[:, None] - jnp.arange(KB)[None, :]
    rel = jnp.clip(rel, -MAX_REL_DIST, MAX_REL_DIST) + MAX_REL_DIST
    bias = jnp.transpose(rel_bias[rel], (2, 0, 1)).astype(jnp.float32)
    s = s + bias[None, None]
    key_chunk = jnp.arange(NC)[:, None] - CA_LEFT_CHUNKS + jnp.arange(KB)[None, :] // CHUNK
    valid = key_chunk >= 0
    s = jnp.where(valid[None, :, None, None, :], s, NEG_INF)
    p = jax.nn.softmax(s, axis=-1).astype(vb.dtype)
    o = jnp.einsum('bnhqk,bnkhd->bnqhd', p, vb)
    return o.reshape(B, S, CA_WIDTH)

def second_inputs(seed: int = 0) -> dict:
    key = jax.random.key(seed)
    ks = jax.random.split(key, 24)
    L, D = DEPTH, D_MODEL

    def w(k, shape, fan_in, mult=1.0):
        return jax.random.normal(k, shape, jnp.float32) * (mult * fan_in ** -0.5)

    def gain(k, shape):
        return 1.0 + 0.1 * jax.random.normal(k, shape, jnp.float32)

    offsets = jax.random.randint(ks[2], (BATCH, 1), 0, 64, dtype=jnp.int32) * CHUNK
    positions = offsets + jnp.arange(SEQ, dtype=jnp.int32)[None, :]
    return {
        "x": jax.random.normal(ks[0], (BATCH, SEQ, D), jnp.float32),
        "c": jax.random.normal(ks[1], (BATCH, D), jnp.float32),
        "positions": positions,
        "w_ada": w(ks[3], (L, D, ADA_WIDTH), D),
        "b_ada": 0.1 * jax.random.normal(ks[4], (L, ADA_WIDTH), jnp.float32),
        "ffn1_norm": gain(ks[5], (L, D)),
        "ffn1_w_in": w(ks[6], (L, D, 2 * D_FF_2), D),
        "ffn1_w_out": w(ks[7], (L, D_FF_2, D), D_FF_2),
        "mix_norm": gain(ks[8], (L, D)),
        "w_in": w(ks[9], (L, D, W_IN_COLS), D),
        "mla_q_norm": gain(ks[10], (L, MLA_Q_RANK)),
        "mla_w_uq": w(ks[11], (L, MLA_Q_RANK, MLA_HEADS * (MLA_NOPE + MLA_ROPE)), MLA_Q_RANK),
        "mla_kv_norm": gain(ks[12], (L, MLA_KV_RANK)),
        "mla_w_ukv": w(ks[13], (L, MLA_KV_RANK, MLA_HEADS * (MLA_NOPE + MLA_V)), MLA_KV_RANK),
        "rel_bias": 0.5 * jax.random.normal(ks[14], (L, 2 * MAX_REL_DIST + 1, CA_HEADS), jnp.float32),
        "w_branch_a": w(ks[15], (L, MLA_OUT_WIDTH, D), MLA_OUT_WIDTH),
        "w_branch_b": w(ks[16], (L, CA_WIDTH, D), CA_WIDTH),
        "w_out": w(ks[17], (L, D, D), D),
        "ffn2_norm": gain(ks[18], (L, D)),
        "ffn2_w_in": w(ks[19], (L, D, 2 * D_FF_2), D),
        "ffn2_w_out": w(ks[20], (L, D_FF_2, D), D_FF_2),
        "final_norm": gain(ks[21], (D,)),
    }

def second_block(x, c, positions, w_ada, b_ada, ffn1_norm, ffn1_w_in, ffn1_w_out,
              mix_norm, w_in, mla_q_norm, mla_w_uq, mla_kv_norm, mla_w_ukv, rel_bias,
              w_branch_a, w_branch_b, w_out, ffn2_norm, ffn2_w_in, ffn2_w_out, final_norm):
    c_act = jax.nn.silu(c)
    splits = []
    acc = 0
    for width in (MLA_Q_RANK, MLA_KV_RANK, MLA_ROPE, CA_WIDTH, CA_WIDTH, CA_WIDTH, D_MODEL):
        acc += width
        splits.append(acc)

    for l in range(DEPTH):
        ada = c_act @ w_ada[l] + b_ada[l]
        (sh1, sc1, g1, sh2, sc2, g2, sh3, sc3, g3) = jnp.split(ada, 3 * ADA_SUBLAYERS, axis=-1)

        h = modulate_2(rmsnorm_2(x, ffn1_norm[l]), sh1, sc1)
        x = x + FFN_RES_WEIGHT * g1[:, None, :] * swiglu_2(h, ffn1_w_in[l], ffn1_w_out[l])

        h = modulate_2(rmsnorm_2(x, mix_norm[l]), sh2, sc2)
        z = h @ w_in[l]
        q_lat, kv_lat, k_pe_raw, ca_q, ca_k, ca_v, gate_a, gate_b = jnp.split(z, splits, axis=-1)
        y_a = mla_attention(q_lat, kv_lat, k_pe_raw, positions, mla_q_norm[l], mla_w_uq[l],
                            mla_kv_norm[l], mla_w_ukv[l]) @ w_branch_a[l]
        B, S = ca_q.shape[:2]
        shp = (B, S, CA_HEADS, CA_HEAD_DIM)
        y_b = chunk_attention(ca_q.reshape(shp), ca_k.reshape(shp), ca_v.reshape(shp),
                              rel_bias[l]) @ w_branch_b[l]
        merged = jax.nn.sigmoid(gate_a) * y_a + jax.nn.sigmoid(gate_b) * y_b
        x = x + g2[:, None, :] * (merged @ w_out[l])

        h = modulate_2(rmsnorm_2(x, ffn2_norm[l]), sh3, sc3)
        x = x + FFN_RES_WEIGHT * g3[:, None, :] * swiglu_2(h, ffn2_w_in[l], ffn2_w_out[l])

    return rmsnorm_2(x, final_norm)


def setup_inputs(seed=0):
    out = dict(first_inputs(seed))
    for name, value in second_inputs(seed + 1).items():
        if name != "x":
            out[name + "_2"] = value
    return out


def reference(
    x, c, ctx, c_ctx, w_ada, b_ada, g_mix, w_in, w_dec_up, b_dec, g_head, w_gla_out, w_conv,
    w_conv_out, w_mix_out, g_ffn, w_ffn_in, w_ffn_out, g_final, c_2, positions_2, w_ada_2,
    b_ada_2, ffn1_norm_2, ffn1_w_in_2, ffn1_w_out_2, mix_norm_2, w_in_2, mla_q_norm_2,
    mla_w_uq_2, mla_kv_norm_2, mla_w_ukv_2, rel_bias_2, w_branch_a_2, w_branch_b_2, w_out_2,
    ffn2_norm_2, ffn2_w_in_2, ffn2_w_out_2, final_norm_2,
):
    x = first_block(
        x, c, ctx, c_ctx, w_ada, b_ada, g_mix, w_in, w_dec_up, b_dec, g_head, w_gla_out, w_conv,
        w_conv_out, w_mix_out, g_ffn, w_ffn_in, w_ffn_out, g_final,
    )
    return second_block(
        x, c_2, positions_2, w_ada_2, b_ada_2, ffn1_norm_2, ffn1_w_in_2, ffn1_w_out_2,
        mix_norm_2, w_in_2, mla_q_norm_2, mla_w_uq_2, mla_kv_norm_2, mla_w_ukv_2, rel_bias_2,
        w_branch_a_2, w_branch_b_2, w_out_2, ffn2_norm_2, ffn2_w_in_2, ffn2_w_out_2,
        final_norm_2,
    )


_drawn_inputs = setup_inputs


def setup_inputs(seed=0):
    import zlib

    import numpy as np

    out = dict(_drawn_inputs(seed))
    spreads = {}
    factors = {'ctx': 2.909,
     'c_ctx': 4.092,
     'b_ada': 4.261,
     'g_mix': 6.292,
     'w_dec_up': 3.168,
     'b_dec': 38.377,
     'g_head': 64.0,
     'g_ffn': 29.118,
     'g_final': 2.794,
     'mla_q_norm_2': 8.0,
     'mla_kv_norm_2': 3.252,
     'rel_bias_2': 4.617,
     'ffn2_norm_2': 3.999}
    for name, (base, spread) in spreads.items():
        noise = np.random.default_rng([zlib.crc32(name.encode()), seed]).standard_normal(out[name].shape)
        drawn = base * np.exp(spread * noise) if base else spread * noise
        out[name] = __import__('jax').numpy.asarray(drawn.astype(out[name].dtype))
    for name, factor in factors.items():
        out[name] = (out[name] * factor).astype(out[name].dtype)
    return out
```

```python
import math
from contextlib import ExitStack

import concourse.bass as bass
from concourse import mybir

F32 = mybir.dt.float32
F32R = mybir.dt.float32r
U32 = mybir.dt.uint32
I32 = mybir.dt.int32
ALU = mybir.AluOpType
ACT = mybir.ActivationFunctionType
AX = mybir.AxisListType

P = 128
D = 1024
T = 256
TT = T // P
KD = D // P
EPS = 1e-6
H1, HK, HV = 4, 128, 256
RANK = 16
CH = 64
NC = T // CH
DFF = 2816
NF = DFF // 256
H2 = 8
NOPE, ROPE, VD = 64, 32, 64
HR = ROPE // 2
QH = NOPE + ROPE
NEG = -1e30
QR, KVR = 256, 128
UC = 256
RING = 3

Q0, K0, V0, G0, DD0 = 0, 512, 1024, 2048, 3072
CB0, CC0, CHH0, GA0, GB0 = 3104, 4128, 5152, 6176, 7200
QL0, KL0, CQ0, CK0, CV0, SA0, SB0 = 0, 256, 416, 928, 1440, 1952, 2976

P1 = ([("dd", 0)] + [("k", n) for n in range(2)] + [("v", n) for n in range(4)] + [("q", n) for n in range(2)]
      + [(s, n) for n in range(4) for s in ("cb", "cc", "ch")] + [("conv_out", n) for n in range(4)]
      + [("g", n) for n in range(4)] + [(s, n) for s in ("ga", "gb") for n in range(4)]
      + [("gla_out", n) for n in range(4)] + [("mix_out", n) for n in range(4)])
P2 = ([("ql", 0), ("kl", 0), ("cq", 0), ("cq", 1), ("uq", 0), ("ck", 0), ("ck", 1), ("ukv", 0), ("cv", 0), ("cv", 1)]
      + [(s, n) for s in ("ga2", "gb2") for n in range(4)]
      + [("bra", n) for n in range(2)] + [("brb", n) for n in range(2)] + [("out2", n) for n in range(4)])
N1, N2, NFF = len(P1), len(P2), 3 * NF
BASE_P1 = 0
BASE_FFN = [N1, N1 + NFF, N1 + 2 * NFF + N2]
BASE_P2 = N1 + 2 * NFF
UNITS = N1 + 3 * NFF + N2
DUAL = ("dd", "k", "v")
GLA_U0, GLA_U1 = P1.index(("cb", 0)), P1.index(("conv_out", 3))
TOKEN_MAJOR = ("v", "g", "mix_out", "ql", "kl", "cv", "out2")


def unit_banks(base, plan):
    banks, held, before = [], {}, []
    for n, (kind, m) in enumerate(plan):
        if n == 0:
            b = [0, 7] if kind == "dd" else [0]
        elif kind in DUAL:
            b = [4, 5] if n % 2 == 0 else [6, 7]
        elif kind in ("uq", "ukv"):
            b = [0, 1, 2, 3]
        elif kind in ("bra", "brb"):
            b = [4, 5] if m % 2 == 0 else [6, 7]
        else:
            b = [4 + n % 2]
        before.append(sorted({held[x] for x in b if x in held}))
        for x in b:
            held[x] = n
        banks.append(b)
    return banks, before


BANKS1, BEFORE1 = unit_banks(0, P1)
BANKS2, BEFORE2 = unit_banks(0, P2)
DVE_EVACS = ("ch", "g", "gla_out", "mix_out", "bra", "brb", "out2")


def evac_counts(plan, start_act, start_dve):
    a, v, out = start_act, start_dve, []
    for kind, _ in plan:
        if kind in DVE_EVACS:
            v += 1
            out.append(("dve", v))
        else:
            a += 1
            out.append(("act", a))
    return out, a, v


EV1, A1, V1 = evac_counts(P1, 0, 0)
EV2, _, _ = evac_counts(P2, A1, V1)

JOBS = []
for _kind in ("mla", "ca"):
    JOBS += [(_kind, 0, (0, 2, 4, 6)), (_kind, 0, (1, 3, 5, 7))]
    JOBS += [(_kind, 1, hs) for hs in ((0, 2), (1, 3), (4, 6), (5, 7))]
NJ = len(JOBS)

ADA = []
for _blk, _col in ((0, 2), (0, 3), (0, 4), (1, 0), (1, 1),
                   (0, 5), (1, 2), (1, 3), (1, 4), (1, 5),
                   (1, 6), (1, 7), (1, 8)):
    ADA += [(_blk, _col * D + 256 * n) for n in range(4)]
NADA1, NADAF = 20, 10
ADA_P2 = NADA1 + 2 * NADAF


def ada_pos(n):
    return n if n < NADA1 else (n - NADA1) % 20


GATE_UNITS = [0, 20, 24, 36, 48]
NORM_UNITS = {2: (4, 8), 3: (12, 16), 4: (28, 32), 5: (40, 44)}
VEC = {"g_mix": 0, "g_ffn": 8, "ffn1_norm_2": 16, "mix_norm_2": 24, "ffn2_norm_2": 32,
       "b_dec": 40, "w_conv": 48, "mla_q_norm_2": 72, "mla_kv_norm_2": 74}
NVEC = 75
BROWS = 48 + 72
ADA1_STEP = {2 * n + 3: n for n in range(NADA1)}
ADA2_STEP = {2 * n + 1: n for n in range(12)}


def build(nc, a, out, stop=9):
    LIMIT = {1: N1 + 2, 2: N1 + NFF + 2, 3: BASE_P2 + 2, 4: BASE_P2 + N2 + 2}.get(stop, UNITS)
    with ExitStack() as ctx:
        def sb(name, shape, dt=F32):
            return ctx.enter_context(nc.sbuf_tensor(name, shape, dt))

        def sem(name):
            return ctx.enter_context(nc.semaphore(name))

        X = sb("X", [P, TT, D])
        raw = [sb(f"raw{i}", [P, KD * UC]) for i in range(RING)]
        whi = [sb(f"whi{i}", [P, KD * UC], F32R) for i in range(RING)]
        wlo = [sb(f"wlo{i}", [P, KD * UC], F32R) for i in range(RING)]
        ada_raw = sb("ada_raw", [P, KD, UC])
        A_hi = sb("A_hi", [P, KD, T], F32R)
        A_lo = sb("A_lo", [P, KD, T], F32R)
        B_hi = sb("B_hi", [P, KD, T], F32R)
        B_lo = sb("B_lo", [P, KD, T], F32R)
        KB = 256
        arena = sb("arena", [P, 87 * KB])
        ones = sb("ones", [P, P])
        bank = [ctx.enter_context(nc.psum_tensor(f"bank{i}", [P, 512], F32)) for i in range(8)]

        def at(kb, words):
            return arena[:, int(kb * KB):int(kb * KB) + words]

        def at3(kb, *shape):
            n = math.prod(shape)
            v = at(kb, n)
            if len(shape) == 2:
                return v.rearrange("p (a b) -> p a b", a=shape[0])
            if len(shape) == 3:
                return v.rearrange("p (a b c) -> p a b c", a=shape[0], b=shape[1])
            return v

        ident = at(85, P)
        small = int(85.5 * KB)
        used = [0]

        def cols(*shape):
            n = math.prod(shape)
            v = arena[:, small + used[0]:small + used[0] + n]
            used[0] += n
            assert used[0] <= 384
            return v if len(shape) == 1 else v.rearrange("p (a b) -> p a b", a=shape[0])

        vec = cols(80)
        bcol = cols(BROWS)
        c3 = cols(KD, 3)
        shift = cols(2, KD)
        scale = cols(2, KD)
        ss = cols(16)
        rstd = cols(16)
        oss = cols(8)
        orstd = cols(8)
        decay = cols(8)
        one = cols(1)
        mhalf = cols(4)
        cos = cols(TT, HR)
        sin = cols(TT, HR)

        acc = at(0, 20 * UC)
        GR = at(20, D)
        ada0 = [at3(8 * j, KD, UC) for j in range(8)]
        ctxX = at3(64, TT, D)
        craw = at3(81, 3, KD)
        vrows = at(82, P)
        brows = at(82.5, P)
        c_e = at3(83, 3, KD)
        arow = ada_raw[0:2, :, :].rearrange("p a b -> p (a b)")
        ddT = arena[0:RANK, 20 * KB:24 * KB].rearrange("p (s d t) -> p s d t", s=2, d=2)
        v_l = at3(24, TT, D)
        on = v_l
        v_c = at3(32, TT, D)
        sigb = at3(32, KD, T)
        qT1 = at3(40, H1, T)
        kT1 = at3(44, H1, T)
        siga = at3(40, KD, T)
        kTc = at3(48, H1, T)
        Bc = at(52, 512)
        Dm = at(54, 512)
        q_in = at(56, 512)
        k_in = at(58, 512)
        k_out = at(60, 512)
        q_out = at(62, 512)
        k_tok = at3(64, TT, 2, P)
        scT = at3(66, TT, 2, P)
        S = [at3(68, 2, HV), at3(70, 2, HV)]
        k_tokc = at3(54, TT, 2, P)
        Xr = at3(52, TT, D)
        msk64 = at(72, 512)
        ones256 = at(74, 256)
        causal = [at(75, P), at(75.5, P)]
        ghb = at(76, HV)
        wdec = arena[0:RANK, 77 * KB:81 * KB].rearrange("p (d n) -> p d n", d=2)
        T0, T1 = at(81, 512), at(83, 512)
        yT = X[:, :, :].rearrange("p t d -> p (t d)").rearrange("p (k t) -> p k t", k=KD)
        Xf = X[:, :, :].rearrange("p t d -> p (t d)")
        cbS, ccS, uS, yS = (Xf[:, 512 * n:512 * n + 512] for n in range(4))
        finrow = [at(52, D), at(56, D)]
        XN = at3(24, TT, D)
        HF = at3(32, KD, T)
        HF1 = [at3(0, KD, T), at3(8, KD, T)]
        sF = at(40, 512)
        hF = at(42, 512)
        yF = [at(44 + 2 * n, 512) for n in range(4)]
        qf = at3(24, TT, H2, QH)
        kf = at3(30, TT, H2, QH)
        vm = at3(36, TT, H2 * VD)
        qlS = at3(40, TT, QR)
        klS = at3(42, TT, KVR + ROPE)
        latF = at3(32, 3, T)
        Pb = [at(40, 512), at(42, 512)]
        qT2 = at3(44, H2, T)
        kT2 = at3(52, H2, T)
        caq = at3(60, 4, T)
        cak = at3(64, 4, T)
        k_ctx = at(64, 512)
        cav = at3(68, TT, 512)
        U = at(72, 2048)
        st2 = int(80 * KB)
        mx = arena[:, st2:st2 + 8].rearrange("p (a b) -> p a b", a=2)
        sm = arena[:, st2 + 8:st2 + 40].rearrange("p (a b) -> p a b", a=4)
        rin = arena[:, st2 + 40:st2 + 72].rearrange("p (a b) -> p a b", a=4)
        ss2 = arena[:, st2 + 72:st2 + 76]
        rs2 = arena[:, st2 + 76:st2 + 80]
        inv = arena[:, st2 + 80:st2 + 96]
        ang = arena[:, st2 + 96:st2 + 128]
        nrd = arena[:, st2 + 128:st2 + 160]
        posi = arena[:, st2 + 160:st2 + 162]
        posf = arena[:, st2 + 162:st2 + 164]
        siga2 = at3(24, KD, T)
        sigb2 = at3(44, KD, T)
        osb = at3(32, TT, 512)
        osb2 = at3(40, TT, 512)
        pT = [T0, T1]
        rot = [arena[:, (81 * KB) + 256 * n:(81 * KB) + 256 * n + 256].rearrange("p (t h r) -> p t h r", t=TT, h=H2)
               for n in range(4)]

        landed = [sem(f"landed{i}") for i in range(RING)]
        hi_ready = sem("hi_ready")
        lo_ready = sem("lo_ready")
        unit_used = sem("unit_used")
        act_evac = sem("act_evac")
        dve_evac = sem("dve_evac")
        act_chain = sem("act_chain")
        dve_chain = sem("dve_chain")
        pool_chain = sem("pool_chain")
        ada_landed = sem("ada_landed")
        ada_mac = sem("ada_mac")
        start_ada = [sem(f"start_ada{j}") for j in range(8)]
        c_in = sem("c_in")
        c_silu = sem("c_silu")
        vec_in = sem("vec_in")
        x_in = [sem("x_in0"), sem("x_in1")]
        dec_in = sem("dec_in")
        xr_in = sem("xr_in")
        u_in = sem("u_in")
        pos_in = sem("pos_in")
        gr_in = sem("gr_in")
        ident_done = sem("ident_done")
        ada0_mm = sem("ada0_mm")
        ada0_row = sem("ada0_row")
        consts = sem("consts")
        vec_tr = sem("vec_tr")
        vec_done = sem("vec_done")
        as_mm = sem("as_mm")
        as_done = sem("as_done")
        gr_mm = sem("gr_mm")
        gr_done = sem("gr_done")
        x_ready = sem("x_ready")
        sq_done = sem("sq_done")
        rstd_done = sem("rstd_done")
        xn_done = sem("xn_done")
        tr_done = sem("tr_done")
        h_done = sem("h_done")
        hhi_done = sem("hhi_done")
        hlo_done = sem("hlo_done")
        zd_mm = sem("zd_mm")
        z_abs = sem("z_abs")
        z_log = sem("z_log")
        z_min = sem("z_min")
        la_done = sem("la_done")
        scan_done = sem("scan_done")
        ex_done = sem("ex_done")
        kc_done = sem("kc_done")
        dm_done = sem("dm_done")
        eq_done = sem("eq_done")
        qk_done = sem("qk_done")
        kt_tr = sem("kt_tr")
        kt_sb = sem("kt_sb")
        s0_mm = sem("s0_mm")
        sc_mm = sem("sc_mm")
        s_ready = sem("s_ready")
        sc_ready = sem("sc_ready")
        kv_mm = sem("kv_mm")
        o_mm = sem("o_mm")
        osq_done = sem("osq_done")
        orstd_done = sem("orstd_done")
        on_done = sem("on_done")
        sig_done = sem("sig_done")
        uc_done = sem("uc_done")
        v_done = sem("v_done")
        vhi_done = sem("vhi_done")
        vlo_done = sem("vlo_done")
        yb_done = sem("yb_done")
        gt_done = sem("gt_done")
        ont_tr = sem("ont_tr")
        onhi_done = sem("onhi_done")
        onlo_done = sem("onlo_done")
        mg_done = sem("mg_done")
        mghi_done = sem("mghi_done")
        mglo_done = sem("mglo_done")
        silu_done = sem("silu_done")
        prod_done = sem("prod_done")
        half_down = sem("half_down")
        fhi_done = sem("fhi_done")
        flo_done = sem("flo_done")
        lat_rs = sem("lat_rs")
        lat_n = sem("lat_n")
        lat_tr = sem("lat_tr")
        lat_f = sem("lat_f")
        lat_hi = sem("lat_hi")
        lat_lo = sem("lat_lo")
        ang_done = sem("ang_done")
        trig_done = sem("trig_done")
        rope_done = sem("rope_done")
        qk_tr = sem("qk_tr")
        qk_sb = sem("qk_sb")
        js_mm = sem("js_mm")
        js_sb = sem("js_sb")
        jp_done = sem("jp_done")
        jt_mm = sem("jt_mm")
        jt_sb = sem("jt_sb")
        jo_mm = sem("jo_mm")
        osb_done = sem("osb_done")
        jx_done = sem("jx_done")
        ot_tr = sem("ot_tr")
        ohi_done = sem("ohi_done")
        olo_done = sem("olo_done")
        x_part = sem("x_part")
        y_added = sem("y_added")
        fsq_done = sem("fsq_done")
        frs_done = sem("frs_done")
        fin_in = sem("fin_in")
        inv_done = sem("inv_done")
        out_done = sem("out_done")
        gh_in = sem("gh_in")
        stored = sem("stored")

        evac_sem = {"act": act_evac, "dve": dve_evac}

        def ring(u):
            return u % RING

        def landings(u, i=0):
            return lin(16, i, 16 * (u // RING + 1))

        def lin(a, i, b):
            if isinstance(i, tuple):
                return i[0] * (3 * a) + (a * i[1] + b)
            return a * i + b

        def feed_forward_steps(eng, f, step):
            first = 1
            if f == 0:
                for i in range(1, 4):
                    step(i, i)
                first = 4
            end = NF - 1 if f < 2 else NF - 4
            with eng.Fori(0, (end - first) // 3) as j:
                for m in range(3):
                    step((j, first + m), first + m)
            for i in range(end, NF - 1):
                step(i, i)

        def cview(w, c0, n=UC):
            return w.rearrange("(k p) n -> p k n", p=P)[:, :, c0:c0 + n]

        def unit_source(kind, n):
            w1, w2 = a["w_in"][0], a["w_in_2"][0]
            first = {"dd": (w1, DD0), "k": (w1, K0), "v": (w1, V0), "q": (w1, Q0), "g": (w1, G0), "cb": (w1, CB0),
                     "cc": (w1, CC0), "ch": (w1, CHH0), "ga": (w1, GA0), "gb": (w1, GB0),
                     "conv_out": (a["w_conv_out"][0], 0), "gla_out": (a["w_gla_out"][0], 0),
                     "mix_out": (a["w_mix_out"][0], 0), "ql": (w2, QL0), "kl": (w2, KL0), "cq": (w2, CQ0),
                     "ck": (w2, CK0), "cv": (w2, CV0), "ga2": (w2, SA0), "gb2": (w2, SB0),
                     "out2": (a["w_out_2"][0], 0)}
            if kind in first:
                w, c0 = first[kind]
                return cview(w, c0 + UC * n), KD, UC
            if kind == "uq":
                return cview(a["mla_w_uq_2"][0], 0, 768), 2, 768
            if kind == "ukv":
                return cview(a["mla_w_ukv_2"][0], 0, 1024), 1, 1024
            w = a["w_branch_a_2"][0] if kind == "bra" else a["w_branch_b_2"][0]
            return cview(w, 512 * n, 512), 4, 512

        ffn_w = [(a["w_ffn_in"][0], a["w_ffn_out"][0]), (a["ffn1_w_in_2"][0], a["ffn1_w_out_2"][0]),
                 (a["ffn2_w_in_2"][0], a["ffn2_w_out_2"][0])]

        def ada_source(n):
            blk, c0 = ADA[n]
            w = a["w_ada"][0] if blk == 0 else a["w_ada_2"][0]
            return w.rearrange("(p k) n -> p k n", k=KD)[:, :, c0:c0 + UC]

        tok = "o (t p) d -> p (o t) d"
        block = ctx.enter_context(nc.Block())

        @block.sync
        def _(sp):
            def load_unit(u, kind, n):
                src, k, w = unit_source(kind, n)
                if u >= RING:
                    sp.wait_ge(lo_ready, u - RING + 1)
                dst = raw[ring(u)][:, 0:k * w].rearrange("p (k w) -> p k w", k=k)
                sp.dma_start(dst, src).then_inc(landed[ring(u)], 16)

            def load_ada(n):
                if n:
                    sp.wait_ge(ada_mac, KD * n)
                sp.dma_start(ada_raw[:], ada_source(n)).then_inc(ada_landed, 16)

            def load_ffn(f):
                w_in, w_out = ffn_w[f]
                u0 = BASE_FFN[f]
                w_in = w_in.rearrange("(k p) n -> p k n", p=P)
                w_out = w_out.rearrange("(k p) n -> p k n", p=P)

                def load(u, i, src, k):
                    sp.wait_ge(lo_ready, lin(3, i, u - RING + 1))
                    sp.dma_start(raw[ring(u)][:].rearrange("p (k w) -> p k w", k=k), src)\
                        .then_inc(landed[ring(u)], 16)

                def piece(a, i, b, n):
                    if isinstance(i, tuple):
                        return bass.ds(lin(a, i, b), n)
                    return slice(a * i + b, a * i + b + n)

                def step(i, m):
                    load(u0 + 2, i, w_in[:, :, piece(UC, i, UC, UC)], KD)
                    load(u0 + 3, i, w_in[:, :, piece(UC, i, DFF + UC, UC)], KD)
                    load(u0 + 4, i, w_out[:, piece(2, i, 0, 2), :], 2)
                    if f < 2:
                        n0 = NADA1 + NADAF * f
                        blk, c0 = ADA[n0 + m]
                        w = (a["w_ada"] if blk == 0 else a["w_ada_2"])[0].rearrange("(p k) n -> p k n", k=KD)
                        sp.wait_ge(ada_mac, lin(KD, i, KD * n0))
                        sp.dma_start(ada_raw[:], w[:, :, piece(UC, i, c0 - UC * m, UC)]).then_inc(ada_landed, 16)

                load(u0, 0, w_in[:, :, 0:UC], KD)
                load(u0 + 1, 0, w_in[:, :, DFF:DFF + UC], KD)
                step(0, 0)
                feed_forward_steps(sp, f, step)
                load(u0 + 3 * NF - 1, 0, w_out[:, 2 * (NF - 1):2 * NF, :], 2)

            for s, name in enumerate(("c", "c_ctx", "c_2")):
                src = a[name] if name == "c_ctx" else a[name].rearrange("o n -> (o n)")
                sp.dma_start(craw[:, s, :], src.rearrange("(p k) -> p k", k=KD)).then_inc(c_in, 16)
            for j in range(8):
                if j == 2:
                    for name, r0 in VEC.items():
                        v = a[name]
                        n = math.prod(v.shape) // P
                        src = bass.AP(tensor=v.tensor, offset=0, ap=[[P, n], [1, P]])
                        sp.dma_start(vrows[r0:r0 + n, :], src).then_inc(vec_in, 16)
                    for name, r0, n in (("b_ada", 0, 48), ("b_ada_2", 48, 72)):
                        src = bass.AP(tensor=a[name].tensor, offset=0, ap=[[P, n], [1, P]])
                        sp.dma_start(brows[r0:r0 + n, :], src).then_inc(vec_in, 16)
                sp.dma_start(ada0[j], a["w_ada"][0].rearrange("(p k) n -> p k n", k=KD)[:, :, UC * j:UC * j + UC])\
                    .then_inc(start_ada[j], 16)
                if j == 3:
                    sp.dma_start(ctxX, a["ctx"].rearrange(tok, p=P)).then_inc(x_in[0], 16)
                    sp.dma_start(X[:], a["x"].rearrange(tok, p=P)).then_inc(x_in[1], 16)
            for u, (kind, n) in enumerate(P1):
                load_unit(u, kind, n)
                if u == 3:
                    sp.wait_ge(as_mm, 1)
                    load_ada(0)
                if u >= 8 and u % 2 == 0 and (u - 6) // 2 < NADA1:
                    load_ada((u - 6) // 2)
                if (kind, n) == ("gla_out", 0):
                    sp.wait_ge(on_done, 8)
                    sp.dma_start(Xr, a["x"].rearrange(tok, p=P)).then_inc(xr_in, 16)
            if stop >= 2:
                load_ffn(0)
                sp.wait_ge(x_ready, 2)
                for q, name in enumerate(("g_final", "final_norm_2")):
                    if q == 0:
                        sp.dma_start(finrow[q], a[name].partition_broadcast(P)).then_inc(fin_in, 16)
                rb = a["rel_bias_2"]
                sp.dma_start(U, bass.AP(tensor=rb.tensor, offset=129 * H2, ap=[[H2, P], [1, T * H2]])).then_inc(u_in, 16)
                sp.dma_start(posi.bitcast(I32), a["positions_2"].rearrange("o (t p) -> p (o t)", p=P),
                             allow_slow_non_contiguous=True).then_inc(pos_in, 16)
            if stop >= 3:
                load_ffn(1)
            if stop >= 4:
                for n2, (kind, n) in enumerate(P2):
                    load_unit(BASE_P2 + n2, kind, n)
                    if n2 == 0:
                        load_ada(ADA_P2)
                    if n2 >= 6 and n2 % 2 == 0 and (n2 - 4) // 2 < 11:
                        load_ada(ADA_P2 + (n2 - 4) // 2)
                load_ada(ADA_P2 + 11)
            if stop >= 5:
                load_ffn(2)
                sp.wait_ge(x_ready, 8)
                sp.dma_start(finrow[1], a["final_norm_2"].partition_broadcast(P)).then_inc(fin_in, 16)
            if stop < 5:
                for u in range(LIMIT - 2, LIMIT):
                    load_unit(u, "q", 0)
            yv = out.rearrange(tok, p=P)
            for t in range(TT):
                if stop >= 5:
                    sp.wait_ge(out_done, t + 1)
                    sp.dma_start(yv[:, t, :], XN[:, t, :]).then_inc(stored, 16)
                else:
                    sp.wait_ge(x_ready, 2 * stop)
                    sp.dma_start(yv[:, t, :], X[:, t, :]).then_inc(stored, 16)
            sp.wait_ge(stored, 32)

        def hidden_part(v, m):
            return v[:, 2 * (m % 3):2 * (m % 3) + 2, :].rearrange("p a b -> p (a b)")

        def norm_source(n):
            return ctxX if n == 0 else X[:] if n == 1 else XN

        def norm_dest(n):
            return (B_hi, B_lo) if n == 0 else (A_hi, A_lo)

        def norm_bank(n, b):
            return {0: (4, 5, 6, 0), 1: (1, 2, 3, 4)}.get(n, (4, 5, 6, 7))[b]

        def norm_fp32(n):
            return HF1[n] if n < 2 else HF

        def head_group(n2, half):
            return {6: half, 7: 2 + half, 8: 4 + half, 9: 6 + half}.get(n2)

        def job_slot(n2, half):
            return 2 * (n2 - 10) + half if 10 <= n2 < 18 else None

        def gla_pass(g):
            d, p = divmod(g, 2)
            return d, p, [c if d == 0 else NC - 1 - c for c in range(NC)]

        def pair3(v):
            return v.rearrange("p (h t) -> p h t", h=2)

        @block.gpsimd
        def _(pool):
            n_chain = [0]

            def link(ins):
                n_chain[0] += 1
                ins.then_inc(pool_chain, 1)
                pool.wait_ge(pool_chain, n_chain[0])

            def root(dst, src, width):
                link(nc.gpsimd.tensor_scalar(dst, src, 1.0 / width, EPS, ALU.mult, ALU.add))
                return nc.gpsimd.tensor_tensor(dst, dst, mhalf[:, 0:dst.shape[1]], ALU.pow)

            def gate_bias(r):
                blk, c0 = ADA[GATE_UNITS[r]]
                b = a["b_ada"] if blk == 0 else a["b_ada_2"]
                pool.dma_start(GR, b[0, c0:c0 + D].partition_broadcast(P)).then_inc(gr_in, 16)

            def norm(n):
                for t in range(TT):
                    c = 2 * n + t
                    pool.wait_ge(sq_done, c + 1)
                    root(rstd[:, c:c + 1], ss[:, c:c + 1], D).then_inc(rstd_done, 1)

            def full_norm(q):
                for t in range(TT):
                    c = 12 + 2 * q + t
                    pool.wait_ge(fsq_done, 2 * q + t + 1)
                    root(rstd[:, c:c + 1], ss[:, c:c + 1], D).then_inc(frs_done, 1)

            nc.gpsimd.memset(mhalf, -0.5)
            link(nc.gpsimd.memset(ident, 0.0))
            nc.gpsimd.affine_select(out=ident, in_=ident, compare_op=ALU.not_equal, fill=1.0, base=0,
                                    pattern=[[-1, P]], channel_multiplier=1).then_inc(ident_done, 1)
            norm(0)
            norm(1)
            nc.gpsimd.memset(one, 1.0)
            nc.gpsimd.memset(ones[:], 1.0)
            nc.gpsimd.memset(ones256, 1.0)
            nc.gpsimd.memset(causal[0], 1.0)
            nc.gpsimd.memset(causal[1], 1.0)
            link(nc.gpsimd.memset(msk64, 1.0))
            for d, sgn in ((0, 1), (1, -1)):
                link(nc.gpsimd.affine_select(out=causal[d], in_=causal[d], compare_op=ALU.is_ge, fill=0.0, base=0,
                                             pattern=[[sgn, P]], channel_multiplier=-sgn))
            link(nc.gpsimd.affine_select(out=causal[0][:, CH:P], in_=causal[0][:, CH:P], compare_op=ALU.is_ge,
                                         fill=0.0, base=-CH, pattern=[[0, CH]], channel_multiplier=1))
            link(nc.gpsimd.affine_select(out=causal[1][:, 0:CH], in_=causal[1][:, 0:CH], compare_op=ALU.is_ge,
                                         fill=0.0, base=CH - 1, pattern=[[0, CH]], channel_multiplier=-1))
            nc.gpsimd.memset(msk64.rearrange("p (c j) -> p c j", j=CH)[:, :, 0:1], 0.0).then_inc(consts, 1)
            pool.dma_start(ghb, a["g_head"][0].partition_broadcast(P)).then_inc(gh_in, 16)
            pool.dma_start(wdec, a["w_dec_up"][0].rearrange("d r n -> r d n")).then_inc(dec_in, 16)
            for g in range(4):
                d, p, order = gla_pass(g)
                kc3, EX = kTc[:, 2 * p:2 * p + 2, :], pair3(k_ctx)
                pool.wait_ge(ex_done, g + 1)
                lo, edge = (slice(0, T - 1), slice(T - 1, T)) if d == 0 else (slice(1, T), slice(0, 1))
                nc.gpsimd.tensor_tensor(EX[:, :, lo], EX[:, :, lo], kc3[:, :, lo], ALU.mult)
                nc.gpsimd.tensor_copy(EX[:, :, edge], kc3[:, :, edge]).then_inc(kc_done, 1)
                pool.wait_ge(eq_done, 2 * g + 1)
                for dst, src in ((q_in, qT1), (k_in, kT1), (q_out, qT1)):
                    ins = nc.gpsimd.tensor_tensor(pair3(dst), pair3(dst), src[:, 2 * p:2 * p + 2, :], ALU.mult)
                ins.then_inc(qk_done, 1)
                pool.wait_ge(eq_done, 2 * g + 2)
                nc.gpsimd.tensor_tensor(pair3(k_out), pair3(k_out), kT1[:, 2 * p:2 * p + 2, :], ALU.mult)\
                    .then_inc(qk_done, 1)
            for t in range(TT):
                pool.wait_ge(osq_done, t + 1)
                root(orstd[:, 4 * t:4 * t + 4], oss[:, 4 * t:4 * t + 4], HV).then_inc(orstd_done, 1)
            pool.wait_ge(on_done, 8)
            gate_bias(0)
            for n in range(4):
                pool.wait_ge(act_evac, EV1[P1.index(("gb", n))][1])
                y = yT[:, 2 * n:2 * n + 2, :]
                nc.gpsimd.tensor_tensor(y, y, sigb[:, 2 * n:2 * n + 2, :], ALU.mult).then_inc(yb_done, 1)
            if stop >= 2:
                norm(2)
                gate_bias(1)
                full_norm(0)
            if stop >= 3:
                norm(3)
                gate_bias(2)
                for f in range(HR):
                    ins = nc.gpsimd.memset(inv[:, f:f + 1], float(10000.0 ** (-2.0 * f / ROPE)))
                ins.then_inc(inv_done, 1)
            if stop >= 4:
                norm(4)
                gate_bias(3)
                for j, w in ((0, QR), (1, KVR)):
                    pool.wait_ge(act_evac, EV2[j][1])
                    root(rs2[:, 2 * j:2 * j + 2], ss2[:, 2 * j:2 * j + 2], w).then_inc(lat_rs, 1)
            if stop >= 5:
                norm(5)
                gate_bias(4)
                full_norm(1)

        @block.scalar
        def _(act):
            n_chain = [0]

            def link(ins):
                n_chain[0] += 1
                ins.then_inc(act_chain, 1)
                act.wait_ge(act_chain, n_chain[0])

            def run(o, i, f=ACT.Copy, **kw):
                return nc.scalar.activation(o, i, f, **kw)

            def split(u, i=0):
                if isinstance(i, int) and u + 3 * i >= LIMIT:
                    return
                act.wait_ge(landed[ring(u)], landings(u, i))
                if not isinstance(i, int) or u + 3 * i >= RING:
                    act.wait_ge(unit_used, lin(3, i, u - RING + 1))
                run(whi[ring(u)][:], raw[ring(u)][:]).then_inc(hi_ready, 1)

            def squares(n):
                for t in range(TT):
                    if n < 2:
                        act.wait_ge(x_in[n], 16)
                        junk = wlo[1 + n][:, D * t:D * t + D]
                    else:
                        act.wait_ge(x_ready, 2 * (n - 2) + t + 1)
                        junk = XN[:, t, :]
                    src = (ctxX if n == 0 else X)[:, t, :]
                    run(junk, src, ACT.Square, accum_out=ss[:, 2 * n + t:2 * n + t + 1]).then_inc(sq_done, 1)

            def modulate(n):
                s = 1 if n == 0 else 0
                h, (hi, lo) = norm_fp32(n), norm_dest(n)
                act.wait_ge(as_done, max(1, n))
                for b in range(5):
                    g = 4 * n + b
                    if b < 4:
                        act.wait_ge(tr_done, g + 1)
                        for kk in range(2):
                            k = 2 * b + kk
                            ins = run(h[:, k, :], bank[norm_bank(n, b)][:, kk * T:kk * T + T], ACT.Identity,
                                      bias=shift[:, s, k:k + 1], scale=scale[:, s, k:k + 1])
                        ins.then_inc(h_done, 1)
                    if b:
                        act.wait_ge(h_done, g)
                        run(hi[:, 2 * b - 2:2 * b, :], h[:, 2 * b - 2:2 * b, :]).then_inc(hhi_done, 1)

            def evac1(u):
                kind, n = P1[u]
                eng, count = EV1[u]
                b = BANKS1[u]
                act.wait_ge(unit_used, u + 1)
                two = slice(2 * n, 2 * n + 2)
                b3 = [bank[x][:].rearrange("p (m t) -> p m t", m=2) for x in b]
                if kind == "dd":
                    run(ddT[:, 0], b3[0][0:RANK])
                    run(ddT[:, 1], b3[1][0:RANK]).then_inc(act_evac, 1)
                elif kind == "k":
                    run(kT1[:, two, :], b3[0])
                    run(kTc[:, two, :], b3[1]).then_inc(act_evac, 1)
                elif kind == "v":
                    run(v_l[:, :, UC * n:UC * n + UC], b3[0])
                    run(v_c[:, :, UC * n:UC * n + UC], b3[1]).then_inc(act_evac, 1)
                elif kind == "q":
                    run(qT1[:, two, :], b3[0], scale=float(HK) ** -0.5).then_inc(act_evac, 1)
                elif kind in ("cb", "cc"):
                    if n:
                        act.wait_ge(v_done, n)
                    run(cbS if kind == "cb" else ccS, bank[b[0]][:]).then_inc(act_evac, 1)
                elif kind == "ch":
                    act.wait_ge(v_done, n + 1)
                    run(B_hi[:, two, :], uS.rearrange("p (m t) -> p m t", m=2)).then_inc(vhi_done, 1)
                elif kind == "conv_out":
                    run(yT[:, two, :], b3[0]).then_inc(act_evac, 1)
                elif kind == "g":
                    if n:
                        act.wait_ge(dve_evac, EV1[u - 1][1])
                    run(T0, bank[b[0]][:], ACT.Sigmoid).then_inc(sig_done, 1)
                elif kind in ("ga", "gb"):
                    run((siga if kind == "ga" else sigb)[:, two, :], b3[0], ACT.Sigmoid).then_inc(act_evac, 1)
                    if kind == "ga":
                        act.wait_ge(ont_tr, n + 1)
                        run(B_hi[:, two, :], bank[6 + n % 2][:].rearrange("p (m t) -> p m t", m=2))\
                            .then_inc(onhi_done, 1)
                elif kind == "gla_out":
                    act.wait_ge(mg_done, n + 1)
                    run(A_hi[:, two, :], (T0, T1)[n % 2].rearrange("p (m t) -> p m t", m=2)).then_inc(mghi_done, 1)

            def gla(slot):
                g, r = divmod(slot, 8)
                if g >= 4:
                    return
                d, p, order = gla_pass(g)
                if r == 0:
                    for s, E in ((0, k_ctx), (1, k_out)):
                        act.wait_ge(zd_mm, 2 * g + s + 1)
                        for h in range(2):
                            col = VEC["b_dec"] + H1 * d + 2 * p + h
                            ins = run(E[:, T * h:T * h + T], bank[6 + s][:, T * h:T * h + T], ACT.Abs,
                                      bias=vec[:, col:col + 1])
                        ins.then_inc(z_abs, 1)
                        act.wait_ge(z_abs, 2 * g + s + 1)
                        link(run(E, E, ACT.Exp, scale=-1.0))
                        run(E, E, ACT.Ln, bias=1.0).then_inc(z_log, 1)
                if r == 1:
                    act.wait_ge(scan_done, 2 * g + 1)
                    R, E = pair3(Dm), pair3(k_ctx)
                    lo, hi = slice(0, T - 1), slice(1, T)
                    run(E[:, :, lo] if d == 0 else E[:, :, hi], R[:, :, hi] if d == 0 else R[:, :, lo], ACT.Exp,
                        scale=1.0 / 16).then_inc(ex_done, 1)
                    act.wait_ge(scan_done, 2 * g + 2)
                    last = CH - 1 if d == 0 else 0
                    B4 = Bc.rearrange("p (c j) -> p c j", j=CH)
                    run(decay.unsqueeze(2), B4[:, :, last:last + 1], ACT.Exp, scale=1.0 / 16)
                    run(q_out, Bc, ACT.Exp, scale=1.0 / 16)
                    act.wait_ge(dm_done, 2 * g + 1)
                    run(q_in, Dm, ACT.Exp, scale=1.0 / 16)
                    run(k_in, Dm, ACT.Exp, scale=-1.0 / 16).then_inc(eq_done, 1)
                if r == 2:
                    act.wait_ge(dm_done, 2 * g + 2)
                    run(k_out, Dm, ACT.Exp, scale=1.0 / 16).then_inc(eq_done, 1)
                if r == 3:
                    act.wait_ge(eq_done, 2 * g + 2)
                    for s, dst in ((0, k_tokc), (1, k_tok)):
                        act.wait_ge(kt_tr, 2 * g + s + 1)
                        run(dst.rearrange("p a b c -> p (a b c)"), bank[6 + s][:]).then_inc(kt_sb, 1)

            def head_squares():
                act.wait_ge(o_mm, 1)
                for t in range(TT):
                    for h in range(H1):
                        j = 4 * t + h
                        ins = run(at(52, 2048)[:, HV * j:HV * j + HV],
                                  bank[2 * t + h // 2][:, HV * (h % 2):HV * (h % 2) + HV], ACT.Square,
                                  accum_out=oss[:, j:j + 1])
                    ins.then_inc(osq_done, 1)

            def ffn(f):
                u0, n0 = BASE_FFN[f], NF * f

                def silu(i, u, b):
                    act.wait_ge(unit_used, lin(3, i, u + 1))
                    run(sF, bank[b][:], ACT.Silu).then_inc(silu_done, 1)

                def high(i, m):
                    act.wait_ge(prod_done, lin(1, i, n0 + 1))
                    run(hidden_part(B_hi, m), hF).then_inc(fhi_done, 1)

                def step(i, m):
                    silu(i, u0, 4) if m else silu(0, u0 + 1, 0)
                    split(u0 + 3, i)
                    high(i, m)
                    split(u0 + 4, i)
                    split(u0 + 5, i)

                split(u0 + 2)
                step(0, 0)
                feed_forward_steps(act, f, step)
                silu(NF - 1, u0, 4)
                split(u0 + 3 * NF)
                high(NF - 1, NF - 1)
                split(u0 + 3 * NF + 1)

            def second():
                act.wait_ge(ang_done, 1)
                f2 = "p t r -> p (t r)"
                run(sin.rearrange(f2), ang, ACT.Sin)
                run(cos.rearrange(f2), nrd, ACT.Sin).then_inc(trig_done, 1)

                def evac2(n2):
                    kind, n = P2[n2]
                    b = BANKS2[n2]
                    act.wait_ge(unit_used, BASE_P2 + n2 + 1)
                    two = slice(2 * n, 2 * n + 2)
                    b3 = bank[b[0]][:].rearrange("p (m t) -> p m t", m=2)
                    if kind == "ql":
                        for t in range(TT):
                            run(T0[:, QR * t:QR * t + QR], b3[:, t, :], ACT.Square, accum_out=ss2[:, t:t + 1])
                        run(qlS, b3).then_inc(act_evac, 1)
                    if kind == "kl":
                        for t in range(TT):
                            run(T1[:, KVR * t:KVR * t + KVR], b3[:, t, 0:KVR], ACT.Square,
                                accum_out=ss2[:, TT + t:TT + t + 1])
                        run(klS, b3[:, :, 0:KVR + ROPE]).then_inc(act_evac, 1)
                    if kind in ("cq", "ck"):
                        run((caq if kind == "cq" else cak)[:, two, :], b3).then_inc(act_evac, 1)
                    if kind == "cv":
                        run(cav[:, :, UC * n:UC * n + UC], b3).then_inc(act_evac, 1)
                    if kind == "uq":
                        for t in range(TT):
                            for x in range(2):
                                ins = run(qf[:, t, 4 * x:4 * x + 4, :],
                                          bank[2 * t + x][:, 0:384].rearrange("p (h d) -> p h d", h=4))
                        ins.then_inc(act_evac, 1)
                    if kind == "ukv":
                        for t in range(TT):
                            for x in range(2):
                                src = bank[2 * t + x][:].rearrange("p (h d) -> p h d", h=4)
                                run(kf[:, t, 4 * x:4 * x + 4, 0:NOPE], src[:, :, 0:NOPE])
                                dst = vm[:, t, 4 * x * VD:(4 * x + 4) * VD].rearrange("p (h d) -> p h d", h=4)
                                ins = run(dst, src[:, :, NOPE:NOPE + VD])
                        ins.then_inc(act_evac, 1)
                    if kind in ("ga2", "gb2"):
                        run((siga2 if kind == "ga2" else sigb2)[:, two, :], b3, ACT.Sigmoid).then_inc(act_evac, 1)
                    if kind == "brb":
                        for x in range(2):
                            act.wait_ge(mg_done, 4 + 2 * n + x + 1)
                            k = 4 * n + 2 * x
                            run(A_hi[:, k:k + 2, :], siga2[:, k:k + 2, :]).then_inc(mghi_done, 1)

                for n2 in range(N2):
                    if n2:
                        evac2(n2 - 1)
                    split(BASE_P2 + n2 + 2)
                    if n2 == 3:
                        act.wait_ge(lat_tr, 1)
                        for k in range(2):
                            c = VEC["mla_q_norm_2"] + k
                            run(latF[:, k, :], bank[6][:, T * k:T * k + T], scale=vec[:, c:c + 1])
                        act.wait_ge(lat_tr, 2)
                        c = VEC["mla_kv_norm_2"]
                        run(latF[:, 2, :], bank[7][:, 0:T], scale=vec[:, c:c + 1]).then_inc(lat_f, 1)
                        act.wait_ge(lat_f, 1)
                        run(B_hi[:, 0:3, :], latF).then_inc(lat_hi, 1)
                    for half in range(2):
                        g = head_group(n2, half)
                        if g is not None:
                            act.wait_ge(qk_tr, g + 1)
                            dst = (qT2 if g < 4 else kT2)[0:QH, 2 * (g % 4):2 * (g % 4) + 2, :]
                            run(dst, bank[6 + g % 2][0:QH, :].rearrange("p (h t) -> p h t", h=2)).then_inc(qk_sb, 1)
                        slot = job_slot(n2, half)
                        if slot is not None and slot < NJ:
                            j = slot
                            kind, t, heads = JOBS[j]
                            K = P * (t + 1)
                            act.wait_ge(jx_done, j + 1)
                            row = 2 * (kind == "ca") + t
                            for x, h in enumerate(heads):
                                v = Pb[j % 2][:, K * x:K * x + K]
                                ins = run(v, v, ACT.Exp, bias=mx[:, j % 2, x:x + 1], accum_out=sm[:, row, h:h + 1])
                            ins.then_inc(jp_done, 1)
                        if slot is not None and 2 <= slot < NJ + 2:
                            j = slot - 2
                            act.wait_ge(jt_mm, j + 1)
                            if j >= 2:
                                act.wait_ge(jo_mm, j - 1)
                            run(pT[j % 2], bank[7][:]).then_inc(jt_sb, 1)
                        if slot in (13, 14):
                            merge_high(0, slot - 13)
                    if P2[n2] == ("bra", 1):
                        merge_high(1, 0)
                        merge_high(1, 1)
                evac2(N2 - 1)

            def merge_high(kk, m):
                g = 2 * kk + m
                act.wait_ge(ot_tr, g + 1)
                k = 4 * kk + 2 * m
                b = bank[6] if kk == 0 else bank[m]
                run(B_hi[:, k:k + 2, :], b[:].rearrange("p (m t) -> p m t", m=2)).then_inc(ohi_done, 1)

            act.wait_ge(c_in, 48)
            run(c3.rearrange("p k s -> p s k"), craw, ACT.Silu).then_inc(c_silu, 1)
            act.wait_ge(vec_tr, 1)
            run(vec[:, 0:NVEC], bank[6][:, 0:NVEC])
            run(bcol, bank[6][:, P:P + BROWS]).then_inc(vec_done, 1)
            squares(0)
            act.wait_ge(ada0_mm, 1)
            run(arow[:, 0:512], bank[0][0:2, :]).then_inc(ada0_row, 1)
            squares(1)
            for b in range(1, 4):
                if b == 3:
                    split(0)
                    split(1)
                act.wait_ge(ada0_mm, b + 1)
                run(arow[:, 512 * b:512 * b + 512], bank[b][0:2, :]).then_inc(ada0_row, 1)
            modulate(0)
            modulate(1)
            for u in range(N1):
                if u:
                    evac1(u - 1)
                split(u + 2)
                if GLA_U0 <= u <= GLA_U1:
                    gla(2 * (u - GLA_U0))
                    gla(2 * (u - GLA_U0) + 1)
                if u == GLA_U1 + 1:
                    head_squares()
            evac1(N1 - 1)
            if stop >= 2:
                squares(2)
                modulate(2)
                ffn(0)
                for t in range(TT):
                    act.wait_ge(y_added, t + 1)
                    run(XN[:, t, :], X[:, t, :], ACT.Square, accum_out=ss[:, 12 + t:13 + t]).then_inc(fsq_done, 1)
            if stop >= 3:
                squares(3)
                modulate(3)
                ffn(1)
            if stop >= 4:
                squares(4)
                modulate(4)
                second()
            if stop >= 5:
                squares(5)
                modulate(5)
                ffn(2)
                for t in range(TT):
                    act.wait_ge(y_added, TT + t + 1)
                    run(XN[:, t, :], X[:, t, :], ACT.Square, accum_out=ss[:, 14 + t:15 + t]).then_inc(fsq_done, 1)

        @block.tensor
        def _(pe):
            def mm(o, l, r, start, stop, **kw):
                return nc.tensor.matmul(o, l, r, start=start, stop=stop, **kw)

            def three(o, w, x, n, stat_w, first, last, **kw):
                (wh, wl), (xh, xl) = w, x
                for j, (p, q) in enumerate(((wh, xh), (wh, xl), (wl, xh))):
                    l, r = (p, q) if stat_w else (q, p)
                    ins = mm(o, l, r, first and j == 0, last and j == 2, **kw)
                return ins

            def product(u, o, x, half, token_major, w0=None, parts=None):
                s = ring(u)
                wh = whi[s][:].rearrange("p (k w) -> p k w", k=KD)
                wl = wlo[s][:].rearrange("p (k w) -> p k w", k=KD)
                ms = slice(P * half, P * half + P)
                for k in range(KD):
                    if parts and k % 2 == 0:
                        pe.wait_ge(parts[0], parts[1] + k // 2 + 1)
                    if token_major:
                        w, xx = (wh[:, k, :], wl[:, k, :]), (x[0][:, k, ms], x[1][:, k, ms])
                    else:
                        ws = ms if w0 is None else slice(w0, w0 + P)
                        w, xx = (wh[:, k, ws], wl[:, k, ws]), (x[0][:, k, :], x[1][:, k, :])
                    ins = three(o, w, xx, k, not token_major, k == 0, k == KD - 1)
                return ins

            A, B = (A_hi, A_lo), (B_hi, B_lo)

            def norm(n):
                src = norm_source(n)
                for t in range(TT):
                    pe.wait_ge(xn_done, 2 * n + t + 1)
                    for b in range(4):
                        if n == 0 and t == 0 and b == 2:
                            pe.wait_ge(vec_done, 1)
                        if n == 0 and t == 0 and b == 3:
                            pe.wait_ge(ada0_row, 1)
                        if n == 1 and t == 0 and b == 3:
                            pe.wait_ge(h_done, 1)
                        for kk in range(2):
                            k = 2 * b + kk
                            c = T * kk + P * t
                            ins = nc.tensor.transpose(bank[norm_bank(n, b)][:, c:c + P], src[:, t, P * k:P * k + P],
                                                      ident)
                        if t == TT - 1:
                            ins.then_inc(tr_done, 1)

            def gate_and_columns(r, n, b, free=None):
                g0 = GATE_UNITS[r]
                pe.wait_ge(ada_mac, KD * (g0 + 4))
                pe.wait_ge(gr_in, 16 * (r + 1))
                for x in range(2):
                    c = UC * ada_pos(g0) + 512 * x
                    ins = mm(bank[6 + x][:], ones[:], acc[:, c:c + 512], True, True)
                ins.then_inc(gr_mm, 1)
                if n is not None:
                    if free:
                        pe.wait_ge(*free)
                    pe.wait_ge(ada_mac, KD * (NORM_UNITS[n][1] + 4))
                    for x in range(2):
                        for k in range(KD):
                            c = UC * ada_pos(NORM_UNITS[n][x]) + P * k
                            ins = mm(bank[b][:, KD * x + k:KD * x + k + 1], acc[:, c:c + P], one, True, True)
                    ins.then_inc(as_mm, 1)

            def wait_banks(u, before, ev):
                for v in before:
                    eng, count = ev[v]
                    pe.wait_ge(evac_sem[eng], count)

            def gla(slot):
                g, r = divmod(slot, 8)
                if r == 0 and g:
                    scan_step(g - 1, 3)
                if g >= 4:
                    return
                d, p, order = gla_pass(g)
                q3, k3, qo3 = pair3(q_in), pair3(k_in), pair3(q_out)
                if r == 0:
                    if g == 0:
                        pe.wait_ge(dec_in, 16)
                        pe.wait_ge(consts, 1)
                        pe.wait_ge(act_evac, EV1[6][1])
                    for s in range(2):
                        for h in range(2):
                            c = HK * (2 * p + h)
                            ins = mm(bank[6 + s][:, T * h:T * h + T], wdec[:, d, c:c + HK], ddT[:, 1 - s, d, :],
                                     True, True)
                        ins.then_inc(zd_mm, 1)
                if r == 3:
                    for s, src in ((0, pair3(k_ctx)), (1, pair3(k_out))):
                        if s == 0:
                            pe.wait_ge(kc_done, g + 1)
                        else:
                            pe.wait_ge(qk_done, 2 * g + 2)
                        for t in range(TT):
                            for h in range(2):
                                c = P * (2 * t + h)
                                ins = nc.tensor.transpose(bank[6 + s][:, c:c + P], src[:, h, P * t:P * t + P], ident)
                        ins.then_inc(kt_tr, 1)
                if r == 4:
                    pe.wait_ge(kt_sb, 2 * g + 1)
                    for h in range(2):
                        c = HV * (2 * p + h)
                        for t in range(TT):
                            ins = mm(bank[6][:, HV * h:HV * h + HV], k_tokc[:, t, h, :], v_c[:, t, c:c + HV],
                                     t == 0, t == TT - 1)
                    ins.then_inc(s0_mm, 1)
                    pe.wait_ge(kt_sb, 2 * g + 2)
                    for h in range(2):
                        for c in range(NC):
                            for x in range(2):
                                js = CH * c + CH // 2 * x
                                i0, ni = (CH * c, CH) if x == d else (js, CH // 2)
                                r0, c0 = js % P, P * (2 * (c // 2) + h) + i0 % P
                                ins = mm(bank[7][r0:r0 + CH // 2, c0:c0 + ni], k3[:, h, js:js + CH // 2],
                                         q3[:, h, i0:i0 + ni], True, True)
                    ins.then_inc(sc_mm, 1)
                if r == 5:
                    pe.wait_ge(sc_ready, g + 1)
                    for t in range(TT):
                        for h in range(2):
                            c = HV * (2 * p + h)
                            mm(bank[2 * t + p][:, HV * h:HV * h + HV], scT[:, t, h, :], v_l[:, t, c:c + HV],
                               d == 0 and h == 0, False, skip_group_check=True)
                if r >= 5:
                    scan_step(g, r - 5)

            def scan_step(g, n):
                d, p, order = gla_pass(g)
                c = order[n]
                t, off = c // 2, CH * (c % 2)
                rows = slice(off, off + CH)
                pe.wait_ge(s_ready, 4 * g + n + 1)
                for h in range(2):
                    ins = mm(bank[2 * t + p][rows, HV * h:HV * h + HV], pair3(q_out)[:, h, CH * c:CH * c + CH],
                             S[n % 2][:, h, :], False, True, skip_group_check=True)
                if g == 3 and n == 3:
                    ins.then_inc(o_mm, 1)
                if n < 3:
                    for h in range(2):
                        v0 = HV * (2 * p + h)
                        ins = mm(bank[6 + c % 2][:, HV * h:HV * h + HV], k_tok[rows, t, h, :],
                                 v_l[rows, t, v0:v0 + HV], True, True)
                    ins.then_inc(kv_mm, 1)

            def ffn(f):
                u0, n0 = BASE_FFN[f], NF * f

                def up(u, i, b, parts=None):
                    pe.wait_ge(lo_ready, lin(3, i, u + 1))
                    for half in range(2):
                        ins = product(u, bank[b][:, T * half:T * half + T], A, half, False, None,
                                      parts if half == 0 else None)
                    ins.then_inc(unit_used, 1)

                def down(u, i, m, first, last):
                    pe.wait_ge(lo_ready, lin(3, i, u + 1))
                    pe.wait_ge(flo_done, lin(1, i, n0 + 1))
                    s = ring(u)
                    wh = whi[s][:].rearrange("p (k w) -> p k w", k=2)
                    wl = wlo[s][:].rearrange("p (k w) -> p k w", k=2)
                    for t in range(TT):
                        for x in range(2):
                            for k in range(2):
                                ts, cs = slice(P * t, P * t + P), slice(512 * x, 512 * x + 512)
                                kb = 2 * (m % 3) + k
                                ins = three(bank[2 * t + x][:], (wh[:, k, cs], wl[:, k, cs]),
                                            (B_hi[:, kb, ts], B_lo[:, kb, ts]), k, False,
                                            first and k == 0, last and k == 1, skip_group_check=True)
                        if last and t == 0:
                            ins.then_inc(half_down, 1)
                    ins.then_inc(unit_used, 1)

                def step(i, m):
                    pe.wait_ge(prod_done, lin(1, i, n0 + 1))
                    up(u0 + 2, i, 4)
                    up(u0 + 3, i, 5)
                    down(u0 + 4, i, m, False, False)

                up(u0, 0, 0, (hlo_done, 4 * (2 + f + (f == 2))))
                up(u0 + 1, 0, 1)
                up(u0 + 2, 0, 4)
                up(u0 + 3, 0, 5)
                pe.wait_ge(prod_done, n0 + 1)
                down(u0 + 4, 0, 0, True, False)
                feed_forward_steps(pe, f, step)
                gate_and_columns((1, 2, 4)[f], (3, 4, None)[f], 4, (prod_done, n0 + NF))
                down(u0 + 2, NF - 1, NF - 1, False, True)

            def second():
                def job(slot):
                    if slot < NJ:
                        kind, t, heads = JOBS[slot]
                        K = P * (t + 1)
                        if slot:
                            pe.wait_ge(js_sb, slot)
                        for x, h in enumerate(heads):
                            if kind == "mla":
                                l, r = qT2[0:QH, h, P * t:P * t + P], kT2[0:QH, h, 0:K]
                            else:
                                rows = slice(64 * (h % 2), 64 * (h % 2) + 64)
                                l, r = caq[rows, h // 2, P * t:P * t + P], cak[rows, h // 2, 0:K]
                            ins = mm(bank[6][:, K * x:K * x + K], l, r, True, True)
                        ins.then_inc(js_mm, 1)
                    if 2 <= slot < NJ + 2:
                        j = slot - 2
                        pe.wait_ge(jp_done, j + 1)
                        if j:
                            pe.wait_ge(jt_sb, j)
                        for c in range(4):
                            ins = nc.tensor.transpose(bank[7][:, P * c:P * c + P], Pb[j % 2][:, P * c:P * c + P], ident)
                        ins.then_inc(jt_mm, 1)
                    if 3 <= slot < NJ + 3:
                        j = slot - 3
                        kind, t, heads = JOBS[j]
                        pe.wait_ge(jt_sb, j + 1)
                        o = bank[t + 2 * (kind == "ca")]
                        v = vm if kind == "mla" else cav
                        for x, h in enumerate(heads):
                            for kt in range(t + 1):
                                c = P * (x * (t + 1) + kt)
                                ins = mm(o[:, VD * h:VD * h + VD], pT[j % 2][:, c:c + P], v[:, kt, VD * h:VD * h + VD],
                                         kt == 0, kt == t)
                        ins.then_inc(jo_mm, 1)

                def out_group(kk, m):
                    pe.wait_ge(osb_done, kk + 1)
                    b = bank[6] if kk == 0 else bank[m]
                    if kk == 0 and m == 0:
                        pe.wait_ge(js_sb, NJ)
                    if kk == 0 and m == 1:
                        pe.wait_ge(olo_done, 1)
                    o = osb if kk == 0 else osb2
                    for x in range(2):
                        for t in range(TT):
                            f0 = P * (2 * m + x)
                            ins = nc.tensor.transpose(b[:, T * x + P * t:T * x + P * t + P], o[:, t, f0:f0 + P], ident)
                    ins.then_inc(ot_tr, 1)

                for n2, (kind, n) in enumerate(P2):
                    u = BASE_P2 + n2
                    b = BANKS2[n2]
                    s = ring(u)
                    pe.wait_ge(lo_ready, u + 1)
                    wait_banks(n2, BEFORE2[n2], EV2)
                    if kind in ("uq", "ukv"):
                        k0, nk, w = (0, 2, 768) if kind == "uq" else (2, 1, 1024)
                        pe.wait_ge(lat_lo, 1)
                        wh = whi[s][:, 0:nk * w].rearrange("p (k w) -> p k w", k=nk)
                        wl = wlo[s][:, 0:nk * w].rearrange("p (k w) -> p k w", k=nk)
                        for t in range(TT):
                            ts = slice(P * t, P * t + P)
                            for x in range(2):
                                cs = slice(x * w // 2, (x + 1) * w // 2)
                                for k in range(nk):
                                    ins = three(bank[2 * t + x][:, 0:w // 2], (wh[:, k, cs], wl[:, k, cs]),
                                                (B_hi[:, k0 + k, ts], B_lo[:, k0 + k, ts]), k, False,
                                                k == 0, k == nk - 1)
                        ins.then_inc(unit_used, 1)
                    elif kind in ("bra", "brb"):
                        kk = kind == "brb"
                        if n == 0 and not kk:
                            pe.wait_ge(jt_sb, NJ)
                        wh = whi[s][:].rearrange("p (k w) -> p k w", k=4)
                        wl = wlo[s][:].rearrange("p (k w) -> p k w", k=4)
                        for m in range(4):
                            for k in range(4):
                                if m == 0 and n == 0 and k % 2 == 0:
                                    pe.wait_ge(olo_done, 2 * kk + k // 2 + 1)
                                cs = slice(P * m, P * m + P)
                                ins = three(bank[b[m // 2]][:, T * (m % 2):T * (m % 2) + T],
                                            (wh[:, k, cs], wl[:, k, cs]),
                                            (B_hi[:, 4 * kk + k, :], B_lo[:, 4 * kk + k, :]), k, True,
                                            k == 0, k == 3)
                        ins.then_inc(unit_used, 1)
                    else:
                        for half in range(2):
                            first = {"ql": (hlo_done, 4 * 4), "out2": (mglo_done, 4)}
                            parts = first.get(kind) if n == 0 and half == 0 else None
                            ins = product(u, bank[b[0]][:, T * half:T * half + T], A, half, kind in TOKEN_MAJOR, None,
                                          parts)
                            if half:
                                ins.then_inc(unit_used, 1)
                            after_half(n2, half, job, out_group)
                    if kind == "ukv":
                        after_half(n2, 0, job, out_group)
                        after_half(n2, 1, job, out_group)
                    if n2 == 3:
                        pe.wait_ge(lat_n, 1)
                        for k in range(2):
                            for t in range(TT):
                                c = T * k + P * t
                                ins = nc.tensor.transpose(bank[6][:, c:c + P], qlS[:, t, P * k:P * k + P], ident)
                        ins.then_inc(lat_tr, 1)
                        pe.wait_ge(lat_n, 2)
                        for t in range(TT):
                            ins = nc.tensor.transpose(bank[7][:, P * t:P * t + P], klS[:, t, 0:KVR], ident)
                        ins.then_inc(lat_tr, 1)
                    if (kind, n) == ("bra", 1):
                        out_group(1, 0)
                        out_group(1, 1)
                    if (kind, n) == ("out2", 0):
                        pe.wait_ge(dve_evac, EV2[P2.index(("brb", 1))][1])
                        gate_and_columns(3, 5, 0)

            def after_half(n2, half, job, out_group):
                g = head_group(n2, half)
                if g is not None:
                    if g < 4:
                        pe.wait_ge(rope_done, 1)
                    else:
                        pe.wait_ge(rope_done, 2)
                        pe.wait_ge(act_evac, EV2[P2.index(("ukv", 0))][1])
                    if g >= 2:
                        pe.wait_ge(qk_sb, g - 1)
                    else:
                        pe.wait_ge(lat_hi, 1)
                    src = qf if g < 4 else kf
                    for h in range(2):
                        for t in range(TT):
                            c = P * (2 * h + t)
                            ins = nc.tensor.transpose(bank[6 + g % 2][0:QH, c:c + P], src[:, t, 2 * (g % 4) + h, :], ident)
                    ins.then_inc(qk_tr, 1)
                slot = job_slot(n2, half)
                if slot is not None:
                    if slot == 0:
                        pe.wait_ge(qk_sb, 8)
                        pe.wait_ge(act_evac, EV2[P2.index(("ukv", 0))][1])
                    job(slot)
                    if slot in (13, 14):
                        out_group(0, slot - 13)

            pe.wait_ge(c_silu, 1)
            for j in range(8):
                if j == 4:
                    pe.wait_ge(ident_done, 1)
                    pe.wait_ge(vec_in, 16 * (len(VEC) + 2))
                    nc.tensor.transpose(bank[6][:, 0:NVEC], vrows[0:NVEC, :], ident[0:NVEC, 0:NVEC])
                    nc.tensor.transpose(bank[6][:, P:P + BROWS], brows[0:BROWS, :], ident[0:BROWS, 0:BROWS])\
                        .then_inc(vec_tr, 1)
                if j == 6:
                    norm(0)
                pe.wait_ge(start_ada[j], 16)
                for k in range(KD):
                    ins = mm(bank[j // 2][0:2, UC * (j % 2):UC * (j % 2) + UC], c3[:, k, 0:2], ada0[j][:, k, :],
                             k == 0, k == KD - 1)
                if j % 2:
                    ins.then_inc(ada0_mm, 1)
            for k in range(16):
                if k % 4 == 0:
                    pe.wait_ge(ada0_row, k // 4 + 1)
                ins = nc.tensor.transpose(bank[7][:, 2 * k:2 * k + 2], arow[:, P * k:P * k + P], ident[0:2, 0:2])
            ins.then_inc(as_mm, 1)
            norm(1)
            for u, (kind, n) in enumerate(P1):
                b = BANKS1[u]
                if kind == "gla_out" and n == 0:
                    gate_and_columns(0, 2, 3)
                pe.wait_ge(lo_ready, u + 1)
                wait_banks(u, BEFORE1[u], EV1)
                x = B if kind in ("conv_out", "gla_out") else A
                if kind == "dd":
                    for x, low in ((1, 0), (0, 4)):
                        for half in range(2):
                            ins = product(u, bank[b[x]][:, T * half:T * half + T], (A, B)[x], half, False, RANK * half,
                                          (hlo_done, low))
                    ins.then_inc(unit_used, 1)
                    continue
                for half in range(2):
                    w0 = None
                    first = {"conv_out": (vlo_done, 0), "gla_out": (onlo_done, 0), "mix_out": (mglo_done, 0)}
                    parts = first.get(kind) if n == 0 and half == 0 else None
                    ins = product(u, bank[b[0]][:, T * half:T * half + T], x, half, kind in TOKEN_MAJOR, w0, parts)
                    if kind in DUAL:
                        ins = product(u, bank[b[1]][:, T * half:T * half + T], B, half, kind in TOKEN_MAJOR, w0)
                    if half:
                        ins.then_inc(unit_used, 1)
                    if GLA_U0 <= u <= GLA_U1:
                        gla(2 * (u - GLA_U0) + half)
                if u == GLA_U1:
                    gla(32)
                if kind == "ga":
                    pe.wait_ge(gt_done, n + 1)
                    if n >= 2:
                        pe.wait_ge(onlo_done, n - 1)
                    for m in range(2):
                        for t in range(TT):
                            c = T * m + P * t
                            f0 = HV * n + P * m
                            ins = nc.tensor.transpose(bank[6 + n % 2][:, c:c + P], on[:, t, f0:f0 + P], ident)
                    ins.then_inc(ont_tr, 1)
            if stop >= 2:
                norm(2)
                ffn(0)
            if stop >= 3:
                norm(3)
                ffn(1)
            if stop >= 4:
                norm(4)
                second()
            if stop >= 5:
                norm(5)
                ffn(2)

        @block.vector
        def _(dve):
            n_chain = [0]

            def link(ins):
                n_chain[0] += 1
                ins.then_inc(dve_chain, 1)
                dve.wait_ge(dve_chain, n_chain[0])

            def tt(o, x, y, op):
                return nc.vector.tensor_tensor(o, x, y, op)

            def ts(o, x, s1, s2, op0, op1=ALU.bypass):
                if s2 is None:
                    return nc.vector.tensor_scalar(o, x, s1, None, op0)
                return nc.vector.tensor_scalar(o, x, s1, s2, op0, op1)

            def stt(o, x, sc, y, op0, op1):
                return nc.vector.scalar_tensor_tensor(out=o, in0=x, scalar=sc, in1=y, op0=op0, op1=op1)

            def rest(o, x, hi):
                return tt(o, x, hi.bitcast(F32), ALU.subtract)

            def split(u, i=0):
                if isinstance(i, int) and u + 3 * i >= LIMIT:
                    return
                dve.wait_ge(hi_ready, lin(3, i, u + 1))
                rest(wlo[ring(u)][:], raw[ring(u)][:], whi[ring(u)][:]).then_inc(lo_ready, 1)

            def adapt(n, i, dst, blk):
                s = 0 if blk == 0 else 2
                dve.wait_ge(ada_landed, lin(16, i, 16 * (n + 1)))
                for k in range(KD):
                    if k:
                        dve.wait_ge(ada_mac, lin(KD, i, KD * n + k))
                        ins = stt(dst, ada_raw[:, k, :], c3[:, k, s:s + 1], dst, ALU.mult, ALU.add)
                    else:
                        ins = ts(dst, ada_raw[:, k, :], c3[:, k, s:s + 1], None, ALU.mult)
                    ins.then_inc(ada_mac, 1)

            def columns(n, b, gain, bias0, src):
                dve.wait_ge(as_mm, max(1, n))
                for s in src:
                    if n < 2:
                        v = bank[b][:, 0:32].rearrange("p (k s) -> p k s", s=2)
                        sh, sc = v[:, 0:KD, s], v[:, KD:2 * KD, s]
                    else:
                        sh, sc = bank[b][:, 0:KD], bank[b][:, KD:2 * KD]
                    tt(shift[:, s, :], sh, bcol[:, bias0:bias0 + KD], ALU.add)
                    link(tt(scale[:, s, :], sc, bcol[:, bias0 + KD:bias0 + 2 * KD], ALU.add))
                    ins = stt(scale[:, s, :], scale[:, s, :], 1.0, vec[:, gain:gain + KD], ALU.add, ALU.mult)
                ins.then_inc(as_done, 1)

            def gate_row(r):
                dve.wait_ge(gr_mm, r + 1)
                for x in range(2):
                    g = GR[:, 512 * x:512 * x + 512]
                    ins = tt(g, g, bank[6 + x][:], ALU.add)
                ins.then_inc(gr_done, 1)

            def norm(n):
                src, dst = (ctxX if n == 0 else X), norm_source(n)
                for t in range(TT):
                    c = 2 * n + t
                    dve.wait_ge(rstd_done, c + 1)
                    ts(dst[:, t, :], src[:, t, :], rstd[:, c:c + 1], None, ALU.mult).then_inc(xn_done, 1)

            def norm_low(n):
                h, (hi, lo) = norm_fp32(n), norm_dest(n)
                for b in range(4):
                    dve.wait_ge(hhi_done, 4 * n + b + 1)
                    k = slice(2 * b, 2 * b + 2)
                    rest(lo[:, k, :], h[:, k, :], hi[:, k, :]).then_inc(hlo_done, 1)

            def evac1(u):
                kind, n = P1[u]
                b = BANKS1[u]
                two = slice(2 * n, 2 * n + 2)
                b3 = bank[b[0]][:].rearrange("p (m t) -> p m t", m=2)
                if kind == "ch":
                    dve.wait_ge(unit_used, u + 1)
                    dve.wait_ge(act_evac, EV1[u - 1][1])
                    ins = tt(uS, ccS, bank[b[0]][:], ALU.mult)
                    ins.then_inc(dve_evac, 1)
                    dve.wait_ge(dve_evac, EV1[u][1])
                    def tap(j, m):
                        c = VEC["w_conv"] + KD * j + 2 * n + m
                        return vec[:, c:c + 1]

                    u4 = uS.rearrange("p (m r t) -> p m r t", m=2, t=CH)
                    y4 = yS.rearrange("p (m r t) -> p m r t", m=2, t=CH)
                    for m in range(2):
                        ins = ts(y4[:, m], u4[:, m], tap(1, m), None, ALU.mult)
                    link(ins)
                    for m in range(2):
                        y = y4[:, m, :, 1:CH]
                        ins = stt(y, u4[:, m, :, 0:CH - 1], tap(0, m), y, ALU.mult, ALU.add)
                    link(ins)
                    for m in range(2):
                        y = y4[:, m, :, 0:CH - 1]
                        ins = stt(y, u4[:, m, :, 1:CH], tap(2, m), y, ALU.mult, ALU.add)
                    link(ins)
                    tt(uS, cbS, yS, ALU.mult).then_inc(v_done, 1)
                    dve.wait_ge(vhi_done, n + 1)
                    rest(B_lo[:, two, :], uS.rearrange("p (m t) -> p m t", m=2), B_hi[:, two, :])\
                        .then_inc(vlo_done, 1)
                elif kind == "g":
                    dve.wait_ge(sig_done, n + 1)
                    if n:
                        dve.wait_ge(gt_done, n)
                    ins = tt(T1, T0, bank[b[0]][:], ALU.mult)
                    ins.then_inc(dve_evac, 1)
                    dve.wait_ge(dve_evac, EV1[u][1])
                    dve.wait_ge(on_done, 8)
                    o = on[:, :, HV * n:HV * n + HV]
                    tt(o, o, T1.rearrange("p (t d) -> p t d", t=TT), ALU.mult).then_inc(gt_done, 1)
                elif kind == "ga":
                    dve.wait_ge(onhi_done, n + 1)
                    rest(B_lo[:, two, :], bank[6 + n % 2][:].rearrange("p (m t) -> p m t", m=2), B_hi[:, two, :])\
                        .then_inc(onlo_done, 1)
                elif kind == "gla_out":
                    T = (T0, T1)[n % 2]
                    T3 = T.rearrange("p (m t) -> p m t", m=2)
                    dve.wait_ge(unit_used, u + 1)
                    tt(T3, b3, siga[:, two, :], ALU.mult).then_inc(dve_evac, 1)
                    dve.wait_ge(dve_evac, EV1[u][1])
                    dve.wait_ge(yb_done, n + 1)
                    tt(T3, T3, yT[:, two, :], ALU.add).then_inc(mg_done, 1)
                    dve.wait_ge(mghi_done, n + 1)
                    rest(A_lo[:, two, :], T3, A_hi[:, two, :]).then_inc(mglo_done, 1)
                elif kind == "mix_out":
                    residual(u, n, b[0], EV1[u][1], Xr)

            def residual(u, n, b, count, old):
                T = (T0, T1)[n % 2].rearrange("p (t d) -> p t d", t=TT)
                cs = slice(UC * n, UC * n + UC)
                dve.wait_ge(unit_used, u + 1)
                if n >= 2:
                    dve.wait_ge(x_part, n - 1 if old is Xr else n + 2)
                g = GR[:, cs].unsqueeze(1).to_broadcast([P, TT, UC])
                tt(T, bank[b][:].rearrange("p (t d) -> p t d", t=TT), g, ALU.mult).then_inc(dve_evac, 1)
                dve.wait_ge(dve_evac, count)
                if old is Xr and n == 0:
                    dve.wait_ge(xr_in, 16)
                ins = tt(X[:, :, cs], old[:, :, cs], T, ALU.add)
                ins.then_inc(x_part if n < 3 else x_ready, 1 if n < 3 else 2)

            def gla(slot):
                g, r = divmod(slot, 8)
                if g >= 4:
                    return
                d, p, order = gla_pass(g)
                if slot == 0:
                    dve.wait_ge(consts, 1)
                if r == 0:
                    for s, M, E in ((0, k_in, k_ctx), (1, q_out, k_out)):
                        dve.wait_ge(z_abs, 2 * g + s + 1)
                        for h in range(2):
                            col = VEC["b_dec"] + H1 * d + 2 * p + h
                            ts(M[:, T * h:T * h + T], bank[6 + s][:, T * h:T * h + T], vec[:, col:col + 1], 0.0,
                               ALU.add, ALU.min).then_inc(z_min, 1)
                        dve.wait_ge(z_min, 4 * g + 2 * s + 2)
                        dve.wait_ge(z_log, 2 * g + s + 1)
                        link(tt(M, M, E, ALU.subtract))
                        if s == 0:
                            M3, R3 = pair3(M), pair3(Dm)
                            for h in range(2):
                                if d == 0:
                                    ins = nc.vector.tensor_tensor_scan(R3[:, h, ::-1], ones256, M3[:, h, ::-1], 0.0,
                                                                       ALU.mult, ALU.add)
                                else:
                                    ins = nc.vector.tensor_tensor_scan(R3[:, h, :], ones256, M3[:, h, :], 0.0,
                                                                       ALU.mult, ALU.add)
                        elif d == 0:
                            ins = nc.vector.tensor_tensor_scan(Bc, msk64, M, 0.0, ALU.mult, ALU.add)
                        else:
                            ins = nc.vector.tensor_tensor_scan(Bc[:, ::-1], msk64, M[:, ::-1], 0.0, ALU.mult, ALU.add)
                        ins.then_inc(scan_done, 1)
                if r in (1, 2):
                    B3, D3 = (v.rearrange("p (c j) -> p c j", j=CH) for v in (Bc, Dm))
                    mid, last = (CH // 2 - 1, CH - 1) if d == 0 else (CH // 2, 0)
                if r == 1:
                    dve.wait_ge(scan_done, 2 * g + 2)
                    dve.wait_ge(ex_done, g + 1)
                    tt(D3, B3, B3[:, :, mid:mid + 1].to_broadcast([P, 8, CH]), ALU.subtract).then_inc(dm_done, 1)
                if r == 2:
                    dve.wait_ge(eq_done, 2 * g + 1)
                    tt(D3, B3[:, :, last:last + 1].to_broadcast([P, 8, CH]), B3, ALU.subtract).then_inc(dm_done, 1)
                if r == 4:
                    dve.wait_ge(s0_mm, g + 1)
                    nc.vector.tensor_copy(S[0].rearrange("p h d -> p (h d)"), bank[6][:]).then_inc(s_ready, 1)
                    dve.wait_ge(sc_mm, g + 1)
                    m = causal[d].bitcast(U32).unsqueeze(1).to_broadcast([P, 4, P])
                    s4 = scT.rearrange("p a b c -> p (a b) c")
                    if p == 0:
                        link(nc.vector.memset(scT.rearrange("p a b c -> p (a b c)"), 0.0))
                    nc.vector.copy_predicated(s4, m, bank[7][:].rearrange("p (a c) -> p a c", a=4))\
                        .then_inc(sc_ready, 1)
                if r >= 5:
                    n = r - 5
                    c = order[n]
                    dve.wait_ge(kv_mm, 3 * g + n + 1)
                    dve.wait_ge(s_ready, 4 * g + n + 1)
                    for h in range(2):
                        j = NC * h + c
                        ins = stt(S[(n + 1) % 2][:, h, :], S[n % 2][:, h, :], decay[:, j:j + 1],
                                  bank[6 + c % 2][:, HV * h:HV * h + HV], ALU.mult, ALU.add)
                    ins.then_inc(s_ready, 1)

            def norm_heads():
                dve.wait_ge(gh_in, 16)
                for t in range(TT):
                    dve.wait_ge(orstd_done, t + 1)
                    for h in range(H1):
                        stt(on[:, t, HV * h:HV * h + HV], bank[2 * t + h // 2][:, HV * (h % 2):HV * (h % 2) + HV],
                            orstd[:, 4 * t + h:4 * t + h + 1], ghb, ALU.mult, ALU.mult).then_inc(on_done, 1)

            def ffn(f):
                u0, n0 = BASE_FFN[f], NF * f

                def product(i, b):
                    dve.wait_ge(silu_done, lin(1, i, n0 + 1))
                    if i != 0 or n0:
                        dve.wait_ge(flo_done, lin(1, i, n0))
                    tt(hF, sF, bank[b][:], ALU.mult).then_inc(prod_done, 1)

                def low(i, m):
                    dve.wait_ge(fhi_done, lin(1, i, n0 + 1))
                    rest(hidden_part(B_lo, m), hF, hidden_part(B_hi, m)).then_inc(flo_done, 1)

                def step(i, m):
                    product(i, 5 if m else 1)
                    split(u0 + 3, i)
                    low(i, m)
                    split(u0 + 4, i)
                    if f < 2:
                        n1 = NADA1 + NADAF * f
                        if isinstance(i, int):
                            dst = acc[:, UC * (NADAF * f + i):UC * (NADAF * f + i) + UC]
                        else:
                            dst = acc[:, bass.ds(lin(UC, i, UC * NADAF * f), UC)]
                        adapt(n1, i, dst, ADA[n1 + m][0])
                    split(u0 + 5, i)

                split(u0 + 2)
                step(0, 0)
                feed_forward_steps(dve, f, step)
                product(NF - 1, 5)
                split(u0 + 3 * NF)
                low(NF - 1, NF - 1)
                r, n, q = ((1, 3, 0), (2, 4, None), (4, None, 1))[f]
                gate_row(r)
                if n is not None:
                    gain = VEC[{3: "ffn1_norm_2", 4: "mix_norm_2"}[n]]
                    columns(n, 4, gain, bias_col(n), (0,))
                dve.wait_ge(gr_done, r + 1)
                for t in range(TT):
                    if t == 0:
                        dve.wait_ge(half_down, f + 1)
                    else:
                        dve.wait_ge(unit_used, u0 + 3 * NF)
                    for x in range(2):
                        cs = slice(512 * x, 512 * x + 512)
                        ins = stt(yF[2 * t + x], bank[2 * t + x][:], 0.5 if f else 1.0, GR[:, cs], ALU.mult, ALU.mult)
                    link(ins)
                    for x in range(2):
                        cs = slice(512 * x, 512 * x + 512)
                        ins = tt(X[:, t, cs], X[:, t, cs], yF[2 * t + x], ALU.add)
                    if q is None:
                        ins.then_inc(x_ready, 1)
                    else:
                        ins.then_inc(y_added, 1)
                if q is not None:
                    dve.wait_ge(fin_in, 16 * (q + 1))
                    for t in range(TT):
                        c = 12 + 2 * q + t
                        dve.wait_ge(frs_done, 2 * q + t + 1)
                        if q == 0:
                            stt(X[:, t, :], X[:, t, :], rstd[:, c:c + 1], finrow[q], ALU.mult, ALU.mult)\
                                .then_inc(x_ready, 1)
                        else:
                            stt(XN[:, t, :], X[:, t, :], rstd[:, c:c + 1], finrow[q], ALU.mult, ALU.mult)\
                                .then_inc(out_done, 1)

            def bias_col(n):
                blk, c0 = ADA[NORM_UNITS[n][0]]
                return (0 if blk == 0 else 48) + c0 // P

            def second():
                dve.wait_ge(pos_in, 16)
                dve.wait_ge(inv_done, 1)
                link(nc.vector.tensor_copy(posf, posi.bitcast(I32)))
                for t in range(TT):
                    ins = ts(ang[:, HR * t:HR * t + HR], inv, posf[:, t:t + 1], None, ALU.mult)
                link(ins)
                magic = 12582912.0
                link(ts(nrd, ang, 1.0 / (2 * math.pi), magic, ALU.mult, ALU.add))
                link(ts(nrd, nrd, magic, None, ALU.subtract))
                for part in TURN:
                    link(stt(ang, nrd, -part, ang, ALU.mult, ALU.add))
                link(ts(ang, ang, 3.1415925, -3.1415925, ALU.min, ALU.max))
                link(stt(nrd, ang, -1.0, ang, ALU.mult, ALU.max))
                ts(nrd, nrd, -1.0, math.pi / 2, ALU.mult, ALU.add).then_inc(ang_done, 1)

                def evac2(n2):
                    kind, n = P2[n2]
                    u = BASE_P2 + n2
                    b = BANKS2[n2]
                    if kind == "uq":
                        dve.wait_ge(act_evac, EV2[n2][1])
                        dve.wait_ge(trig_done, 1)
                        rotate(qf[:, :, :, NOPE:NOPE + HR], qf[:, :, :, NOPE + HR:QH], H2, None)
                        rotate(klS[:, :, KVR:KVR + HR], klS[:, :, KVR + HR:KVR + ROPE], 1, kf)
                    if kind == "bra":
                        dve.wait_ge(unit_used, u + 1)
                        for x in range(2):
                            v = siga2[:, 4 * n + 2 * x:4 * n + 2 * x + 2, :]
                            ins = tt(v, bank[b[x]][:].rearrange("p (m t) -> p m t", m=2), v, ALU.mult)
                        ins.then_inc(dve_evac, 1)
                    if kind == "brb":
                        dve.wait_ge(unit_used, u + 1)
                        for x in range(2):
                            v = sigb2[:, 4 * n + 2 * x:4 * n + 2 * x + 2, :]
                            ins = tt(v, bank[b[x]][:].rearrange("p (m t) -> p m t", m=2), v, ALU.mult)
                        ins.then_inc(dve_evac, 1)
                        dve.wait_ge(dve_evac, EV2[n2][1])
                        for x in range(2):
                            k = slice(4 * n + 2 * x, 4 * n + 2 * x + 2)
                            tt(siga2[:, k, :], siga2[:, k, :], sigb2[:, k, :], ALU.add).then_inc(mg_done, 1)
                        for x in range(2):
                            k = slice(4 * n + 2 * x, 4 * n + 2 * x + 2)
                            dve.wait_ge(mghi_done, 4 + 2 * n + x + 1)
                            rest(A_lo[:, k, :], siga2[:, k, :], A_hi[:, k, :]).then_inc(mglo_done, 1)
                    if kind == "out2":
                        residual(u, n, b[0], EV2[n2][1], X)

                def rotate(x1, x2, heads, spread):
                    if spread is None:
                        r, c, s = rot, cos.unsqueeze(2).to_broadcast([P, TT, H2, HR]), \
                            sin.unsqueeze(2).to_broadcast([P, TT, H2, HR])
                    else:
                        r, c, s = [v[:, :, 0, :] for v in rot], cos, sin
                    tt(r[0], x1, c, ALU.mult)
                    tt(r[1], x2, s, ALU.mult)
                    tt(r[2], x1, s, ALU.mult)
                    link(tt(r[3], x2, c, ALU.mult))
                    if spread is None:
                        o1, o2 = x1, x2
                    else:
                        o1, o2 = spread[:, :, :, NOPE:NOPE + HR], spread[:, :, :, NOPE + HR:QH]
                        r = [v.unsqueeze(2).to_broadcast([P, TT, H2, HR]) for v in r]
                    tt(o1, r[0], r[1], ALU.subtract)
                    ins = tt(o2, r[2], r[3], ALU.add)
                    ins.then_inc(rope_done, 1)
                    dve.wait_ge(rope_done, 1 if spread is None else 2)

                def job(j):
                    kind, t, heads = JOBS[j]
                    K, nh = P * (t + 1), len(heads)
                    dve.wait_ge(js_mm, j + 1)
                    if j >= 2:
                        dve.wait_ge(jt_mm, j - 1)
                    s3 = Pb[j % 2].rearrange("p (h k) -> p h k", h=nh)
                    b3 = bank[6][:].rearrange("p (h k) -> p h k", h=nh)
                    if kind == "mla":
                        ins = ts(s3, b3, float(QH) ** -0.5, None, ALU.mult)
                    else:
                        bias = U.rearrange("p (k h) -> p h k", h=H2)[:, heads[0]:heads[0] + 2 * nh - 1:2, 0:K][:, :, ::-1]
                        ins = stt(s3, b3, float(VD) ** -0.5, bias, ALU.mult, ALU.add)
                    ins.then_inc(js_sb, 1)
                    dve.wait_ge(js_sb, j + 1)
                    link(nc.vector.memset(s3[0:CH, :, K - CH:K], NEG))
                    m = mx[:, j % 2, 0:nh]
                    link(nc.vector.tensor_reduce(m, s3, AX.X, ALU.max))
                    ts(m, m, -1.0, None, ALU.mult).then_inc(jx_done, 1)

                def heads_out(kk, o):
                    dve.wait_ge(jo_mm, 6 * kk + 6)
                    for t in range(TT):
                        ins = nc.vector.reciprocal(rin[:, 2 * kk + t, :], sm[:, 2 * kk + t, :])
                    link(ins)
                    for t in range(TT):
                        ins = tt(o[:, t, :].rearrange("p (h d) -> p h d", h=H2),
                                 bank[2 * kk + t][:].rearrange("p (h d) -> p h d", h=H2),
                                 rin[:, 2 * kk + t, :].unsqueeze(2).to_broadcast([P, H2, VD]), ALU.mult)
                    ins.then_inc(osb_done, 1)

                def merge_low(kk, m):
                    k = slice(4 * kk + 2 * m, 4 * kk + 2 * m + 2)
                    b = bank[6] if kk == 0 else bank[m]
                    dve.wait_ge(ohi_done, 2 * kk + m + 1)
                    rest(B_lo[:, k, :], b[:].rearrange("p (m t) -> p m t", m=2), B_hi[:, k, :]).then_inc(olo_done, 1)

                for n2 in range(N2):
                    if n2:
                        evac2(n2 - 1)
                    split(BASE_P2 + n2 + 2)
                    if n2 == 2:
                        for j, (v, w) in enumerate(((qlS, QR), (klS, KVR))):
                            dve.wait_ge(lat_rs, j + 1)
                            dve.wait_ge(act_evac, EV2[j][1])
                            for t in range(TT):
                                ins = ts(v[:, t, 0:w], v[:, t, 0:w], rs2[:, 2 * j + t:2 * j + t + 1], None, ALU.mult)
                            ins.then_inc(lat_n, 1)
                    if n2 == 3:
                        dve.wait_ge(lat_hi, 1)
                        rest(B_lo[:, 0:3, :], latF, B_hi[:, 0:3, :]).then_inc(lat_lo, 1)
                    for half in range(2):
                        slot = job_slot(n2, half)
                        if slot is not None and slot < NJ:
                            if slot == 6:
                                dve.wait_ge(u_in, 16)
                            job(slot)
                        if slot == 10:
                            heads_out(0, osb)
                        if slot in (13, 14):
                            merge_low(0, slot - 13)
                        if slot == 15:
                            heads_out(1, osb2)
                    if P2[n2] == ("bra", 1):
                        merge_low(1, 0)
                        merge_low(1, 1)
                    if P2[n2] == ("out2", 0):
                        gate_row(3)
                        columns(5, 0, VEC["ffn2_norm_2"], bias_col(5), (0,))
                        dve.wait_ge(gr_done, 4)
                    if n2 in ADA2_STEP:
                        n = ADA_P2 + ADA2_STEP[n2]
                        p = UC * ada_pos(n)
                        adapt(n, 0, acc[:, p:p + UC], ADA[n][0])
                evac2(N2 - 1)

            norm(0)
            norm(1)
            split(0)
            split(1)
            dve.wait_ge(vec_done, 1)
            columns(0, 7, VEC["g_mix"], 0, (0, 1))
            norm_low(0)
            norm_low(1)
            for u in range(N1):
                if u:
                    evac1(u - 1)
                split(u + 2)
                if GLA_U0 <= u <= GLA_U1:
                    gla(2 * (u - GLA_U0))
                    gla(2 * (u - GLA_U0) + 1)
                if u == GLA_U1 + 1:
                    norm_heads()
                if P1[u] == ("gla_out", 0):
                    gate_row(0)
                    columns(2, 3, VEC["g_ffn"], bias_col(2), (0,))
                    dve.wait_ge(gr_done, 1)
                if u in ADA1_STEP:
                    n = ADA1_STEP[u]
                    adapt(n, 0, acc[:, UC * n:UC * n + UC], ADA[n][0])
            evac1(N1 - 1)
            if stop >= 2:
                norm(2)
                norm_low(2)
                ffn(0)
            if stop >= 3:
                norm(3)
                split(BASE_FFN[1] + 1)
                norm_low(3)
                ffn(1)
            if stop >= 4:
                norm(4)
                split(BASE_P2 + 1)
                norm_low(4)
                second()
            if stop >= 5:
                norm(5)
                norm_low(5)
                ffn(2)


def turn_parts():
    left, parts = 2 * math.pi, []
    for _ in range(4):
        e = math.floor(math.log2(left))
        step = 2.0 ** (e - 7)
        p = math.floor(left / step) * step
        parts.append(p)
        left -= p
    return parts


TURN = turn_parts()

INS = ["x", "c", "ctx", "c_ctx", "w_ada", "b_ada", "g_mix", "w_in", "w_dec_up", "b_dec", "g_head", "w_gla_out",
       "w_conv", "w_conv_out", "w_mix_out", "g_ffn", "w_ffn_in", "w_ffn_out", "g_final", "c_2", "positions_2",
       "w_ada_2", "b_ada_2", "ffn1_norm_2", "ffn1_w_in_2", "ffn1_w_out_2", "mix_norm_2", "w_in_2", "mla_q_norm_2",
       "mla_w_uq_2", "mla_kv_norm_2", "mla_w_ukv_2", "rel_bias_2", "w_branch_a_2", "w_branch_b_2", "w_out_2",
       "ffn2_norm_2", "ffn2_w_in_2", "ffn2_w_out_2", "final_norm_2"]


STOP = 9


def kernel(**inputs):
    import numpy as np
    import concourse.bacc as bacc
    from concourse.bass_utils import run_bass_kernel_spmd as launch

    nc = bacc.Bacc("TRN2", target_bir_lowering=False, num_devices=1)
    arrays, args = {}, {}
    for name in INS:
        v = np.ascontiguousarray(inputs[name])
        arrays[f"in_{name}"] = v
        args[name] = nc.dram_tensor(f"in_{name}", v.shape, mybir.dt.from_np(v.dtype), kind="ExternalInput").ap()
    out = nc.dram_tensor("out_0", (1, T, D), F32, kind="ExternalOutput").ap()
    build(nc, args, out, STOP)
    r = launch(nc, [arrays], core_ids=[0])
    return r.results[0]["out_0"]
```

```python
import math
from contextlib import ExitStack

import concourse.bass as bass
from concourse import mybir

F32 = mybir.dt.float32
F32R = mybir.dt.float32r
U32 = mybir.dt.uint32
I32 = mybir.dt.int32
ALU = mybir.AluOpType
ACT = mybir.ActivationFunctionType
AX = mybir.AxisListType

P = 128
D = 1024
T = 256
TT = T // P
KD = D // P
EPS = 1e-6
H1, HK, HV = 4, 128, 256
RANK = 16
CH = 64
NC = T // CH
DFF = 2816
NF = DFF // 256
H2 = 8
NOPE, ROPE, VD = 64, 32, 64
HR = ROPE // 2
QH = NOPE + ROPE
NEG = -1e30
QR, KVR = 256, 128
UC = 256
WARM = (12, 5)
RING = 3

Q0, K0, V0, G0, DD0 = 0, 512, 1024, 2048, 3072
CB0, CC0, CHH0, GA0, GB0 = 3104, 4128, 5152, 6176, 7200
QL0, KL0, CQ0, CK0, CV0, SA0, SB0 = 0, 256, 416, 928, 1440, 1952, 2976

P1 = ([("dd", 0)] + [("k", n) for n in range(2)] + [("v", n) for n in range(4)] + [("q", n) for n in range(2)]
      + [(s, n) for n in range(4) for s in ("cb", "cc", "ch")] + [("conv_out", n) for n in range(4)]
      + [("g", n) for n in range(4)] + [(s, n) for s in ("ga", "gb") for n in range(4)]
      + [("gla_out", n) for n in range(4)] + [("mix_out", n) for n in range(4)])
P2 = ([("ql", 0), ("kl", 0), ("cq", 0), ("cq", 1), ("uq", 0), ("ck", 0), ("ck", 1), ("ukv", 0), ("cv", 0), ("cv", 1)]
      + [(s, n) for s in ("ga2", "gb2") for n in range(4)]
      + [("bra", n) for n in range(2)] + [("brb", n) for n in range(2)] + [("out2", n) for n in range(4)])
N1, N2, NFF = len(P1), len(P2), 3 * NF
BASE_FFN = [N1, N1 + NFF, N1 + 2 * NFF + N2]
BASE_P2 = N1 + 2 * NFF
UNITS = N1 + 3 * NFF + N2
DUAL = ("dd", "k", "v")
GLA_U0, GLA_U1 = P1.index(("cb", 0)), P1.index(("conv_out", 3))
TOKEN_MAJOR = ("v", "g", "mix_out", "ql", "kl", "cv", "out2")


def unit_banks(base, plan):
    banks, held, before = [], {}, []
    for n, (kind, m) in enumerate(plan):
        if n == 0:
            b = [0, 7] if kind == "dd" else [0]
        elif kind in DUAL:
            b = [4, 7] if n % 2 == 0 else [5, 6]
        elif kind == "q" and m == 0:
            b = [6]
        elif kind in ("uq", "ukv"):
            b = [0, 1, 2, 3]
        elif kind in ("bra", "brb"):
            b = [4, 5] if m % 2 == 0 else [6, 7]
        else:
            b = [4 + n % 2]
        before.append(sorted({held[x] for x in b if x in held}))
        for x in b:
            held[x] = n
        banks.append(b)
    return banks, before


BANKS1, BEFORE1 = unit_banks(0, P1)
BANKS2, BEFORE2 = unit_banks(0, P2)
DVE_EVACS = ("ch", "g", "gla_out", "mix_out", "bra", "brb", "out2")


def evac_counts(plan, start_act, start_dve):
    a, v, out = start_act, start_dve, []
    for kind, _ in plan:
        if kind in DVE_EVACS:
            v += 1
            out.append(("dve", v))
        else:
            a += 1
            out.append(("act", a))
    return out, a, v


EV1, A1, V1 = evac_counts(P1, 0, 0)
EV2, _, _ = evac_counts(P2, A1, V1)

JOBS = []
for _kind in ("mla", "ca"):
    JOBS += [(_kind, 0, (0, 2, 4, 6)), (_kind, 0, (1, 3, 5, 7))]
    JOBS += [(_kind, 1, hs) for hs in ((0, 2), (1, 3), (4, 6), (5, 7))]
NJ = len(JOBS)

ADA = []
for _blk, _col in ((0, 2), (0, 3), (0, 4), (0, 5),
                   (1, 0), (1, 1), (1, 2), (1, 3), (1, 4),
                   (1, 5), (1, 6), (1, 7),
                   (1, 8)):
    ADA += [(_blk, _col * D + 256 * n) for n in range(4)]
NADA1, NADAF, NADA2 = 16, 10, 12
ADA_P2 = NADA1 + 2 * NADAF
ADA_LAST = ADA_P2 + NADA2
ADA_FFN = [n for n in range(len(ADA)) if NADA1 <= n < ADA_P2 or n >= ADA_LAST]
ADA_MIX = [n for n in range(len(ADA)) if n not in ADA_FFN]
ADA_DVE = [n for n in range(len(ADA)) if n in ADA_FFN or ADA_P2 <= n < ADA_P2 + 4]
ADA_POOL = [n for n in range(len(ADA)) if n not in ADA_DVE]
LAST_STEPS = (0, NF - 4, NF - 3, NF - 2)


def ada_pos(n):
    return n if n < NADA1 else n - NADA1 if n < ADA_P2 else n - ADA_P2


GATE_UNITS = [0, 12, 24, 36, 48]
NORM_UNITS = {2: (4, 8), 3: (16, 20), 4: (28, 32), 5: (40, 44)}
VEC = {"g_mix": 0, "g_ffn": 8, "ffn1_norm_2": 16, "mix_norm_2": 24, "ffn2_norm_2": 32,
       "b_dec": 40, "w_conv": 48, "mla_q_norm_2": 72, "mla_kv_norm_2": 74}
NVEC = 75
PARTIAL = {2: 0, 5: 2}
BROWS = 48 + 72
ADA1_STEP = [2, 3, 4, 6, 7, 9, 11, 13, 15, 17, 20, 22, 25, 27, 30, 32]
ADA2_STEP = [1, 3, 5, 7]


def build(nc, a, out):
    with ExitStack() as ctx:
        def sb(name, shape, dt=F32):
            return ctx.enter_context(nc.sbuf_tensor(name, shape, dt))

        def sem(name):
            return ctx.enter_context(nc.semaphore(name))

        X = sb("X", [P, TT, D])
        raw = [sb(f"raw{i}", [P, KD * UC]) for i in range(RING)]
        whi = [sb(f"whi{i}", [P, KD * UC], F32R) for i in range(RING)]
        wlo = [sb(f"wlo{i}", [P, KD * UC], F32R) for i in range(RING)]
        ada_raw = sb("ada_raw", [P, KD, UC])
        A_hi = sb("A_hi", [P, KD, T], F32R)
        A_lo = sb("A_lo", [P, KD, T], F32R)
        B_hi = sb("B_hi", [P, KD, T], F32R)
        B_lo = sb("B_lo", [P, KD, T], F32R)
        KB = 256
        arena = sb("arena", [P, 87 * KB])
        ones = sb("ones", [P, P])
        bank = [ctx.enter_context(nc.psum_tensor(f"bank{i}", [P, 512], F32)) for i in range(8)]

        def at(kb, words):
            return arena[:, int(kb * KB):int(kb * KB) + words]

        def at3(kb, *shape):
            n = math.prod(shape)
            v = at(kb, n)
            if len(shape) == 2:
                return v.rearrange("p (a b) -> p a b", a=shape[0])
            if len(shape) == 3:
                return v.rearrange("p (a b c) -> p a b c", a=shape[0], b=shape[1])
            return v

        ident = at(85, P)
        small = int(85.5 * KB)
        used = [0]

        def cols(*shape):
            n = math.prod(shape)
            v = arena[:, small + used[0]:small + used[0] + n]
            used[0] += n
            assert used[0] <= 384
            return v if len(shape) == 1 else v.rearrange("p (a b) -> p a b", a=shape[0])

        vec = cols(80)
        bcol = cols(BROWS)
        c3 = cols(KD, 3)
        shift = cols(2, KD)
        scale = cols(2, KD)
        ss = cols(16)
        rstd = cols(16)
        oss = cols(8)
        orstd = cols(8)
        decay = cols(8)
        one = cols(1)
        mhalf = cols(4)
        cos = cols(TT, HR)
        sin = cols(TT, HR)

        acc = at(0, 20 * UC)
        GR = at(20, D)
        ada0 = [at3(8 * j, KD, UC) for j in range(8)]
        ctxX = at3(64, TT, D)
        craw = at3(81, 3, KD)
        vrows = at(82, P)
        brows = at(82.5, P)
        arow = ada_raw[0:2, :, :].rearrange("p a b -> p (a b)")
        ddT = arena[0:2 * RANK, 20 * KB:22 * KB].rearrange("p (s t) -> p s t", s=2)
        v_l = at3(24, TT, D)
        on = v_l
        v_c = at3(32, TT, D)
        sigb = at3(32, KD, T)
        qT1 = at3(40, H1, T)
        kT1 = at3(44, H1, T)
        siga = at3(40, KD, T)
        kTc = at3(48, H1, T)
        Bc = at(52, 512)
        Dm = at(54, 512)
        q_in = at(56, 512)
        k_in = at(58, 512)
        k_out = at(60, 512)
        q_out = at(62, 512)
        k_tok = at3(64, TT, 2, P)
        scT = at3(66, TT, 2, P)
        S = [at3(68, 2, HV), at3(70, 2, HV)]
        k_tokc = at3(54, TT, 2, P)
        Xr = at3(52, TT, D)
        msk64 = at(72, 512)
        ones256 = at(74, 256)
        causal = [at(75, P), at(75.5, P)]
        ghb = at(76, HV)
        wdec = arena[0:2 * RANK, 77 * KB:81 * KB].rearrange("p (d n) -> p d n", d=2)
        T0, T1 = at(81, 512), at(83, 512)
        yT = X[:, :, :].rearrange("p t d -> p (t d)").rearrange("p (k t) -> p k t", k=KD)
        Xf = X[:, :, :].rearrange("p t d -> p (t d)")
        cbS, ccS, uS, yS = (Xf[:, 512 * n:512 * n + 512] for n in range(4))
        finrow = [at(52, D), at(56, D)]
        XN = at3(24, TT, D)
        HF = at3(32, KD, T)
        HF1 = [at3(0, KD, T), at3(8, KD, T)]
        sF = at(40, 512)
        hF = at(42, 512)
        yF = [at(44 + 2 * n, 512) for n in range(4)]
        qf = at3(24, TT, H2, QH)
        kf = at3(30, TT, H2, QH)
        vm = at3(36, TT, H2 * VD)
        qlS = at3(40, TT, QR)
        klS = at3(42, TT, KVR + ROPE)
        latF = at3(32, 3, T)
        Pb = [at(40, 512), at(42, 512)]
        qT2 = at3(44, H2, T)
        kT2 = at3(52, H2, T)
        caq = at3(60, 4, T)
        cak = at3(64, 4, T)
        k_ctx = at(64, 512)
        cav = at3(68, TT, 512)
        U = at(72, 2048)
        st2 = int(80 * KB)
        mx = arena[:, st2:st2 + 8].rearrange("p (a b) -> p a b", a=2)
        sm = arena[:, st2 + 8:st2 + 40].rearrange("p (a b) -> p a b", a=4)
        rin = arena[:, st2 + 40:st2 + 72].rearrange("p (a b) -> p a b", a=4)
        ss2 = arena[:, st2 + 72:st2 + 76]
        rs2 = arena[:, st2 + 76:st2 + 80]
        inv = arena[:, st2 + 80:st2 + 96]
        ang = arena[:, st2 + 96:st2 + 128]
        nrd = arena[:, st2 + 128:st2 + 160]
        posi = arena[:, st2 + 160:st2 + 162]
        posf = arena[:, st2 + 162:st2 + 164]
        siga2 = at3(24, KD, T)
        sigb2 = at3(44, KD, T)
        osb = at3(32, TT, 512)
        osb2 = at3(40, TT, 512)
        pT = [T0, T1]
        rot = [arena[:, (81 * KB) + 256 * n:(81 * KB) + 256 * n + 256].rearrange("p (t h r) -> p t h r", t=TT, h=H2)
               for n in range(4)]

        landed = [sem(f"landed{i}") for i in range(RING)]
        hi_ready = sem("hi_ready")
        lo_ready = sem("lo_ready")
        unit_used = sem("unit_used")
        act_evac = sem("act_evac")
        dve_evac = sem("dve_evac")
        act_chain = sem("act_chain")
        dve_chain = sem("dve_chain")
        pool_chain = sem("pool_chain")
        ada_landed = sem("ada_landed")
        ada_landed_p = sem("ada_landed_p")
        ada_mac = sem("ada_mac")
        ada_sum = sem("ada_sum")
        start_ada = [sem(f"start_ada{j}") for j in range(8)]
        c_in = sem("c_in")
        c_silu = sem("c_silu")
        vec_in = sem("vec_in")
        x_in = [sem("x_in0"), sem("x_in1")]
        dec_in = sem("dec_in")
        xr_in = sem("xr_in")
        u_in = sem("u_in")
        pos_in = sem("pos_in")
        gr_in = sem("gr_in")
        ident_done = sem("ident_done")
        ada0_mm = sem("ada0_mm")
        ada0_row = sem("ada0_row")
        consts = sem("consts")
        vec_tr = sem("vec_tr")
        vec_done = sem("vec_done")
        as_mm = sem("as_mm")
        as_done = sem("as_done")
        gr_mm = sem("gr_mm")
        gr_done = sem("gr_done")
        x_ready = sem("x_ready")
        sq_done = sem("sq_done")
        rstd_done = sem("rstd_done")
        xn_done = sem("xn_done")
        tr_done = sem("tr_done")
        h_done = sem("h_done")
        h_dve = sem("h_dve")
        hhi_done = sem("hhi_done")
        hlo_done = sem("hlo_done")
        zd_mm = sem("zd_mm")
        z_abs = sem("z_abs")
        z_log = sem("z_log")
        z_min = sem("z_min")
        scan_done = sem("scan_done")
        ex_done = sem("ex_done")
        kc_done = sem("kc_done")
        dm_done = sem("dm_done")
        eq_done = sem("eq_done")
        qk_done = sem("qk_done")
        kt_tr = sem("kt_tr")
        kt_sb = sem("kt_sb")
        s0_mm = sem("s0_mm")
        sc_mm = sem("sc_mm")
        s_ready = sem("s_ready")
        sc_ready = sem("sc_ready")
        kv_mm = sem("kv_mm")
        o_mm = sem("o_mm")
        osq_done = sem("osq_done")
        orstd_done = sem("orstd_done")
        on_done = sem("on_done")
        sig_done = sem("sig_done")
        v_done = sem("v_done")
        vhi_done = sem("vhi_done")
        vlo_done = sem("vlo_done")
        yb_done = sem("yb_done")
        gt_done = sem("gt_done")
        ont_tr = sem("ont_tr")
        onhi_done = sem("onhi_done")
        onlo_done = sem("onlo_done")
        gates_done = sem("gates_done")
        mg_done = sem("mg_done")
        mghi_done = sem("mghi_done")
        mglo_done = sem("mglo_done")
        silu_done = sem("silu_done")
        prod_done = sem("prod_done")
        half_down = sem("half_down")
        fhi_done = sem("fhi_done")
        flo_done = sem("flo_done")
        lat_rs = sem("lat_rs")
        lat_n = sem("lat_n")
        lat_tr = sem("lat_tr")
        lat_f = sem("lat_f")
        lat_hi = sem("lat_hi")
        lat_lo = sem("lat_lo")
        ang_done = sem("ang_done")
        trig_done = sem("trig_done")
        rope_done = sem("rope_done")
        qk_tr = sem("qk_tr")
        qk_sb = sem("qk_sb")
        js_mm = sem("js_mm")
        js_sb = sem("js_sb")
        jp_done = sem("jp_done")
        jt_mm = sem("jt_mm")
        jt_sb = sem("jt_sb")
        jo_mm = sem("jo_mm")
        osb_done = sem("osb_done")
        jx_done = sem("jx_done")
        ot_tr = sem("ot_tr")
        ohi_done = sem("ohi_done")
        olo_done = sem("olo_done")
        x_part = sem("x_part")
        y_added = sem("y_added")
        fsq_done = sem("fsq_done")
        frs_done = sem("frs_done")
        fin_in = sem("fin_in")
        inv_done = sem("inv_done")
        out_done = sem("out_done")
        gh_in = sem("gh_in")
        stored = sem("stored")

        evac_sem = {"act": act_evac, "dve": dve_evac}

        def ring(u):
            return u % RING

        def landings(u, i=0):
            return lin(16, i, 16 * (u // RING + 1))

        def ada_order(n):
            return (ADA_DVE if n in ADA_DVE else ADA_POOL).index(n)

        def ada_done(n):
            if n in ADA_DVE:
                return ada_mac, KD * (ada_order(n) + 1)
            return ada_sum, ada_order(n) + 1

        def ada_landing(n):
            if n in ADA_FFN:
                return ada_landed, 16 * (ADA_FFN.index(n) + 1)
            return ada_landed_p, 16 * (ADA_MIX.index(n) + 1)

        def lin(a, i, b):
            if isinstance(i, tuple):
                return i[0] * (3 * a) + (a * i[1] + b)
            return a * i + b

        def feed_forward_steps(eng, f, step):
            end = NF - 1 if f < 2 else NF - 4
            with eng.Fori(0, (end - 1) // 3) as j:
                for m in range(1, 4):
                    step((j, m), m)
            for i in range(end, NF - 1):
                step(i, i)

        def cview(w, c0, n=UC):
            return w.rearrange("(k p) n -> p k n", p=P)[:, :, c0:c0 + n]

        def unit_source(kind, n):
            w1, w2 = a["w_in"][0], a["w_in_2"][0]
            first = {"dd": (w1, DD0), "k": (w1, K0), "v": (w1, V0), "q": (w1, Q0), "g": (w1, G0), "cb": (w1, CB0),
                     "cc": (w1, CC0), "ch": (w1, CHH0), "ga": (w1, GA0), "gb": (w1, GB0),
                     "conv_out": (a["w_conv_out"][0], 0), "gla_out": (a["w_gla_out"][0], 0),
                     "mix_out": (a["w_mix_out"][0], 0), "ql": (w2, QL0), "kl": (w2, KL0), "cq": (w2, CQ0),
                     "ck": (w2, CK0), "cv": (w2, CV0), "ga2": (w2, SA0), "gb2": (w2, SB0),
                     "out2": (a["w_out_2"][0], 0)}
            if kind in first:
                w, c0 = first[kind]
                return cview(w, c0 + UC * n), KD, UC
            if kind == "uq":
                return cview(a["mla_w_uq_2"][0], 0, 768), 2, 768
            if kind == "ukv":
                return cview(a["mla_w_ukv_2"][0], 0, 1024), 1, 1024
            w = a["w_branch_a_2"][0] if kind == "bra" else a["w_branch_b_2"][0]
            return cview(w, 512 * n, 512), 4, 512

        ffn_w = [(a["w_ffn_in"][0], a["w_ffn_out"][0]), (a["ffn1_w_in_2"][0], a["ffn1_w_out_2"][0]),
                 (a["ffn2_w_in_2"][0], a["ffn2_w_out_2"][0])]

        def ada_source(n):
            blk, c0 = ADA[n]
            w = a["w_ada"][0] if blk == 0 else a["w_ada_2"][0]
            return w.rearrange("(p k) n -> p k n", k=KD)[:, :, c0:c0 + UC]

        tok = "o (t p) d -> p (o t) d"
        block = ctx.enter_context(nc.Block())

        @block.sync
        def _(sp):
            def load_unit(u, kind, n):
                src, k, w = unit_source(kind, n)
                if u >= RING:
                    sp.wait_ge(lo_ready, u - RING + 1)
                dst = raw[ring(u)][:, 0:k * w].rearrange("p (k w) -> p k w", k=k)
                sp.dma_start(dst, src).then_inc(landed[ring(u)], 16)

            def load_ada(n):
                sp.wait_ge(*ada_done(n - 1))
                sp.dma_start(ada_raw[:], ada_source(n)).then_inc(ada_landed, 16)

            def load_ffn(f):
                w_in, w_out = ffn_w[f]
                u0 = BASE_FFN[f]
                w_in = w_in.rearrange("(k p) n -> p k n", p=P)
                w_out = w_out.rearrange("(k p) n -> p k n", p=P)

                def load(u, i, src, k):
                    sp.wait_ge(lo_ready, lin(3, i, u - RING + 1))
                    sp.dma_start(raw[ring(u)][:].rearrange("p (k w) -> p k w", k=k), src)\
                        .then_inc(landed[ring(u)], 16)

                def piece(a, i, b, n):
                    if isinstance(i, tuple):
                        return bass.ds(lin(a, i, b), n)
                    return slice(a * i + b, a * i + b + n)

                def step(i, m):
                    load(u0 + 2, i, w_in[:, :, piece(UC, i, UC, UC)], KD)
                    load(u0 + 3, i, w_in[:, :, piece(UC, i, DFF + UC, UC)], KD)
                    load(u0 + 4, i, w_out[:, piece(2, i, 0, 2), :], 2)
                    if f < 2:
                        n0 = NADA1 + NADAF * f
                        blk, c0 = ADA[n0 + m]
                        w = (a["w_ada"] if blk == 0 else a["w_ada_2"])[0].rearrange("(p k) n -> p k n", k=KD)
                        if n0 == NADA1 and m == 0:
                            sp.wait_ge(*ada_done(n0 - 1))
                        else:
                            sp.wait_ge(ada_mac, lin(KD, i, KD * ada_order(n0)))
                        sp.dma_start(ada_raw[:], w[:, :, piece(UC, i, c0 - UC * m, UC)]).then_inc(ada_landed, 16)
                    elif m in LAST_STEPS and i == m:
                        load_ada(ADA_LAST + LAST_STEPS.index(m))

                load(u0, 0, w_in[:, :, 0:UC], KD)
                load(u0 + 1, 0, w_in[:, :, DFF:DFF + UC], KD)
                step(0, 0)
                feed_forward_steps(sp, f, step)
                load(u0 + 3 * NF - 1, 0, w_out[:, 2 * (NF - 1):2 * NF, :], 2)

            for s, name in enumerate(("c", "c_ctx", "c_2")):
                src = a[name] if name == "c_ctx" else a[name].rearrange("o n -> (o n)")
                sp.dma_start(craw[:, s, :], src.rearrange("(p k) -> p k", k=KD)).then_inc(c_in, 16)
            for j in range(8):
                if j == 2:
                    for name, r0 in VEC.items():
                        v = a[name]
                        n = math.prod(v.shape) // P
                        src = bass.AP(tensor=v.tensor, offset=0, ap=[[P, n], [1, P]])
                        sp.dma_start(vrows[r0:r0 + n, :], src).then_inc(vec_in, 16)
                    for name, r0, n in (("b_ada", 0, 48), ("b_ada_2", 48, 72)):
                        src = bass.AP(tensor=a[name].tensor, offset=0, ap=[[P, n], [1, P]])
                        sp.dma_start(brows[r0:r0 + n, :], src).then_inc(vec_in, 16)
                sp.dma_start(ada0[j], a["w_ada"][0].rearrange("(p k) n -> p k n", k=KD)[:, :, UC * j:UC * j + UC])\
                    .then_inc(start_ada[j], 16)
                if j == 3:
                    sp.dma_start(ctxX, a["ctx"].rearrange(tok, p=P)).then_inc(x_in[0], 16)
                    sp.dma_start(X[:], a["x"].rearrange(tok, p=P)).then_inc(x_in[1], 16)
            for u, (kind, n) in enumerate(P1):
                load_unit(u, kind, n)
                if (kind, n) == ("gla_out", 0):
                    sp.wait_ge(on_done, 8)
                    sp.dma_start(Xr, a["x"].rearrange(tok, p=P)).then_inc(xr_in, 16)
            load_ffn(0)
            sp.wait_ge(x_ready, 2)
            for q, name in enumerate(("g_final", "final_norm_2")):
                if q == 0:
                    sp.dma_start(finrow[q], a[name].partition_broadcast(P)).then_inc(fin_in, 16)
            rb = a["rel_bias_2"]
            sp.dma_start(U, bass.AP(tensor=rb.tensor, offset=129 * H2, ap=[[H2, P], [1, T * H2]])).then_inc(u_in, 16)
            sp.dma_start(posi.bitcast(I32), a["positions_2"].rearrange("o (t p) -> p (o t)", p=P),
                         allow_slow_non_contiguous=True).then_inc(pos_in, 16)
            load_ffn(1)
            for n2, (kind, n) in enumerate(P2):
                load_unit(BASE_P2 + n2, kind, n)
            load_ffn(2)
            sp.wait_ge(x_ready, 8)
            sp.dma_start(finrow[1], a["final_norm_2"].partition_broadcast(P)).then_inc(fin_in, 16)
            yv = out.rearrange(tok, p=P)
            for t in range(TT):
                sp.wait_ge(out_done, t + 1)
                sp.dma_start(yv[:, t, :], XN[:, t, :]).then_inc(stored, 16)
            sp.wait_ge(stored, 32)

        def hidden_part(v, m):
            return v[:, 2 * (m % 3):2 * (m % 3) + 2, :].rearrange("p a b -> p (a b)")

        def norm_source(n):
            return ctxX if n == 0 else X[:] if n == 1 else XN

        def norm_dest(n):
            return (B_hi, B_lo) if n == 0 else (A_hi, A_lo)

        def norm_bank(n, b):
            return {0: (4, 5, 6, 0), 1: (1, 2, 3, 4)}.get(n, (4, 5, 6, 7))[b]

        def gate_bank(r):
            return 2 if r == 3 else 6

        def norm_fp32(n):
            return HF1[n] if n < 2 else HF

        def head_group(n2, half):
            return {6: half, 7: 2 + half, 8: 4 + half, 9: 6 + half}.get(n2)

        def score_bank(j):
            return 3 if j % 2 and j < NJ - 2 else 6

        def job_slot(n2, half):
            return 2 * (n2 - 10) + half if 10 <= n2 < 18 else None

        def gla_pass(g):
            d, p = divmod(g, 2)
            return d, p, [c if d == 0 else NC - 1 - c for c in range(NC)]

        def pair3(v):
            return v.rearrange("p (h t) -> p h t", h=2)

        @block.gpsimd
        def _(pool):
            n_chain = [0]

            def link(ins):
                n_chain[0] += 1
                ins.then_inc(pool_chain, 1)
                pool.wait_ge(pool_chain, n_chain[0])

            def root(dst, src, width):
                link(nc.gpsimd.tensor_scalar(dst, src, 1.0 / width, EPS, ALU.mult, ALU.add))
                return nc.gpsimd.tensor_tensor(dst, dst, mhalf[:, 0:dst.shape[1]], ALU.pow)

            def gate_bias(r):
                blk, c0 = ADA[GATE_UNITS[r]]
                b = a["b_ada"] if blk == 0 else a["b_ada_2"]
                pool.dma_start(GR, b[0, c0:c0 + D].partition_broadcast(P)).then_inc(gr_in, 16)

            def norm(n):
                for t in range(TT):
                    c = 2 * n + t
                    pool.wait_ge(sq_done, c + 1)
                    if n in PARTIAL:
                        part = ss[:, PARTIAL[n] + t:PARTIAL[n] + t + 1]
                        link(nc.gpsimd.tensor_tensor(part, part, ss[:, c:c + 1], ALU.add))
                        root(rstd[:, c:c + 1], part, D).then_inc(rstd_done, 1)
                        continue
                    root(rstd[:, c:c + 1], ss[:, c:c + 1], D).then_inc(rstd_done, 1)

            def full_norm(q):
                for t in range(TT):
                    c = 12 + 2 * q + t
                    pool.wait_ge(fsq_done, 2 * q + t + 1)
                    root(rstd[:, c:c + 1], ss[:, c:c + 1], D).then_inc(frs_done, 1)

            def load_ada(n):
                if n:
                    pool.wait_ge(*ada_done(n - 1))
                else:
                    pool.wait_ge(as_mm, 1)
                pool.dma_start(ada_raw[:], ada_source(n)).then_inc(ada_landed_p, 16)

            def adapt(n):
                s = 0 if ADA[n][0] == 0 else 2
                dst = acc[:, UC * ada_pos(n):UC * ada_pos(n) + UC]
                pool.wait_ge(*ada_landing(n))
                v = ada_raw
                link(nc.gpsimd.tensor_tensor(v[:], v[:], c3[:, :, s:s + 1].to_broadcast([P, KD, UC]), ALU.mult))
                link(nc.gpsimd.tensor_tensor(v[:, 0:4, :], v[:, 0:4, :], v[:, 4:8, :], ALU.add))
                link(nc.gpsimd.tensor_tensor(v[:, 0:2, :], v[:, 0:2, :], v[:, 2:4, :], ALU.add))
                nc.gpsimd.tensor_tensor(dst, v[:, 0, :], v[:, 1, :], ALU.add).then_inc(ada_sum, 1)

            nc.gpsimd.memset(mhalf, -0.5)
            link(nc.gpsimd.memset(ident, 0.0))
            nc.gpsimd.affine_select(out=ident, in_=ident, compare_op=ALU.not_equal, fill=1.0, base=0,
                                    pattern=[[-1, P]], channel_multiplier=1).then_inc(ident_done, 1)
            norm(0)
            norm(1)
            nc.gpsimd.memset(one, 1.0)
            nc.gpsimd.memset(ones[:], 1.0)
            nc.gpsimd.memset(ones256, 1.0)
            nc.gpsimd.memset(causal[0], 1.0)
            nc.gpsimd.memset(causal[1], 1.0)
            nc.gpsimd.memset(wdec, 0.0)
            link(nc.gpsimd.memset(msk64, 1.0))
            for d, sgn in ((0, 1), (1, -1)):
                link(nc.gpsimd.affine_select(out=causal[d], in_=causal[d], compare_op=ALU.is_ge, fill=0.0, base=0,
                                             pattern=[[sgn, P]], channel_multiplier=-sgn))
            link(nc.gpsimd.affine_select(out=causal[0][:, CH:P], in_=causal[0][:, CH:P], compare_op=ALU.is_ge,
                                         fill=0.0, base=-CH, pattern=[[0, CH]], channel_multiplier=1))
            link(nc.gpsimd.affine_select(out=causal[1][:, 0:CH], in_=causal[1][:, 0:CH], compare_op=ALU.is_ge,
                                         fill=0.0, base=CH - 1, pattern=[[0, CH]], channel_multiplier=-1))
            nc.gpsimd.memset(msk64.rearrange("p (c j) -> p c j", j=CH)[:, :, 0:1], 0.0).then_inc(consts, 1)
            pool.dma_start(ghb, a["g_head"][0].partition_broadcast(P)).then_inc(gh_in, 16)
            for d in range(2):
                pool.dma_start(wdec[RANK * d:RANK * d + RANK, d, :], a["w_dec_up"][0, d]).then_inc(dec_in, 16)
            load_ada(0)
            pool.wait_ge(hlo_done, 8)
            for u in range(N1):
                if GLA_U0 <= u <= GLA_U1 and (u - GLA_U0) % 4 == 0:
                    g = (u - GLA_U0) // 4
                    p = g % 2
                    for x, dsts in enumerate((((k_out, kT1),), ((k_in, kT1), (q_in, qT1)), ((q_out, qT1),))):
                        pool.wait_ge(eq_done, 3 * g + x + 1)
                        for dst, src in dsts:
                            ins = nc.gpsimd.tensor_tensor(pair3(dst), pair3(dst), src[:, 2 * p:2 * p + 2, :], ALU.mult)
                        ins.then_inc(qk_done, 1)
                if u == GLA_U1 + 1:
                    for t in range(TT):
                        pool.wait_ge(osq_done, t + 1)
                        root(orstd[:, 4 * t:4 * t + 4], oss[:, 4 * t:4 * t + 4], HV).then_inc(orstd_done, 1)
                for n in range(NADA1):
                    if ADA1_STEP[n] == u:
                        adapt(n)
                        if n + 1 < NADA1:
                            load_ada(n + 1)
            pool.wait_ge(on_done, 8)
            gate_bias(0)
            for n in range(4):
                pool.wait_ge(act_evac, EV1[P1.index(("gb", n))][1])
                y = yT[:, 2 * n:2 * n + 2, :]
                nc.gpsimd.tensor_tensor(y, y, sigb[:, 2 * n:2 * n + 2, :], ALU.mult).then_inc(yb_done, 1)
            norm(2)
            gate_bias(1)
            full_norm(0)
            norm(3)
            gate_bias(2)
            for f in range(HR):
                ins = nc.gpsimd.memset(inv[:, f:f + 1], float(10000.0 ** (-2.0 * f / ROPE)))
            ins.then_inc(inv_done, 1)
            norm(4)
            gate_bias(3)
            load_ada(ADA_P2)
            for j, w in ((0, QR), (1, KVR)):
                pool.wait_ge(act_evac, EV2[j][1])
                root(rs2[:, 2 * j:2 * j + 2], ss2[:, 2 * j:2 * j + 2], w).then_inc(lat_rs, 1)
            for n in range(ADA_P2, ADA_LAST):
                if n > ADA_P2:
                    load_ada(n)
                if n in ADA_POOL:
                    adapt(n)
            norm(5)
            gate_bias(4)
            full_norm(1)

        @block.scalar
        def _(act):
            n_chain = [0]

            def link(ins):
                n_chain[0] += 1
                ins.then_inc(act_chain, 1)
                act.wait_ge(act_chain, n_chain[0])

            def run(o, i, f=ACT.Copy, **kw):
                return nc.scalar.activation(o, i, f, **kw)

            def split(u, i=0):
                if isinstance(i, int) and u + 3 * i >= UNITS:
                    return
                act.wait_ge(landed[ring(u)], landings(u, i))
                if not isinstance(i, int) or u + 3 * i >= RING:
                    act.wait_ge(unit_used, lin(3, i, u - RING + 1))
                run(whi[ring(u)][:], raw[ring(u)][:]).then_inc(hi_ready, 1)

            def squares(n):
                for t in range(TT):
                    if n < 2:
                        act.wait_ge(x_in[n], 16)
                        junk = wlo[1 + n][:, D * t:D * t + D]
                    else:
                        act.wait_ge(x_ready, 2 * (n - 2) + t + 1)
                        junk = XN[:, t, :]
                    src = (ctxX if n == 0 else X)[:, t, :]
                    if n in PARTIAL:
                        src, junk = src[:, D - UC:D], junk[:, D - UC:D]
                    run(junk, src, ACT.Square, accum_out=ss[:, 2 * n + t:2 * n + t + 1]).then_inc(sq_done, 1)

            def partial_squares(n):
                act.wait_ge(x_part, 3 if n == 2 else 6)
                for t in range(TT):
                    run(XN[:, t, 0:D - UC], X[:, t, 0:D - UC], ACT.Square,
                        accum_out=ss[:, PARTIAL[n] + t:PARTIAL[n] + t + 1])

            def modulate(n):
                s = 1 if n == 0 else 0
                h, (hi, lo) = norm_fp32(n), norm_dest(n)
                act.wait_ge(as_done, max(1, n))
                def affine(b):
                    act.wait_ge(tr_done, 4 * n + b + 1)
                    for kk in range(2):
                        k = 2 * b + kk
                        ins = run(h[:, k, :], bank[norm_bank(n, b)][:, kk * T:kk * T + T], ACT.Identity,
                                  bias=shift[:, s, k:k + 1], scale=scale[:, s, k:k + 1])
                    ins.then_inc(h_done, 1)

                def high(b):
                    if n == 1:
                        act.wait_ge(h_dve, b + 1)
                    elif n >= 2 and b == 3:
                        act.wait_ge(h_dve, 4 + n - 1)
                    else:
                        act.wait_ge(h_done, (0 if n == 0 else 4 + 3 * (n - 2)) + b + 1)
                    run(hi[:, 2 * b:2 * b + 2, :], h[:, 2 * b:2 * b + 2, :]).then_inc(hhi_done, 1)

                if n == 1:
                    for b in range(4):
                        high(b)
                    return
                affine(0)
                high(0)
                affine(1)
                affine(2)
                high(1)
                if n == 0:
                    affine(3)
                high(2)
                high(3)

            def conv_high(n):
                act.wait_ge(v_done, n + 1)
                run(B_hi[:, 2 * n:2 * n + 2, :], uS.rearrange("p (m t) -> p m t", m=2)).then_inc(vhi_done, 1)

            def evac1(u):
                kind, n = P1[u]
                eng, count = EV1[u]
                b = BANKS1[u]
                act.wait_ge(unit_used, u + 1)
                two = slice(2 * n, 2 * n + 2)
                b3 = [bank[x][:].rearrange("p (m t) -> p m t", m=2) for x in b]
                if kind == "dd":
                    run(ddT[:, 0], b3[0][0:2 * RANK, 0])
                    run(ddT[:, 1], b3[1][0:2 * RANK, 0]).then_inc(act_evac, 1)
                elif kind == "k":
                    run(kT1[:, two, :], b3[0])
                    run(kTc[:, two, :], b3[1]).then_inc(act_evac, 1)
                elif kind == "v":
                    run(v_l[:, :, UC * n:UC * n + UC], b3[0])
                    run(v_c[:, :, UC * n:UC * n + UC], b3[1]).then_inc(act_evac, 1)
                elif kind == "q":
                    run(qT1[:, two, :], b3[0], scale=float(HK) ** -0.5).then_inc(act_evac, 1)
                elif kind in ("cb", "cc"):
                    if n:
                        act.wait_ge(v_done, n)
                    run(cbS if kind == "cb" else ccS, bank[b[0]][:]).then_inc(act_evac, 1)
                elif kind == "ch" and n == 3:
                    conv_high(n)
                elif kind == "conv_out":
                    run(yT[:, two, :], b3[0]).then_inc(act_evac, 1)
                elif kind == "g":
                    if n:
                        act.wait_ge(dve_evac, EV1[u - 1][1])
                    run(T0, bank[b[0]][:], ACT.Sigmoid).then_inc(sig_done, 1)
                elif kind in ("ga", "gb"):
                    run((siga if kind == "ga" else sigb)[:, two, :], b3[0], ACT.Sigmoid).then_inc(act_evac, 1)
                    if kind == "ga":
                        act.wait_ge(ont_tr, n + 1)
                        run(B_hi[:, two, :], bank[6 + n % 2][:].rearrange("p (m t) -> p m t", m=2))\
                            .then_inc(onhi_done, 1)
                elif kind == "gla_out":
                    act.wait_ge(mg_done, n + 1)
                    run(A_hi[:, two, :], (T0, T1)[n % 2].rearrange("p (m t) -> p m t", m=2)).then_inc(mghi_done, 1)

            def gla(slot):
                g, r = divmod(slot, 8)
                if g >= 4:
                    return
                d, p, order = gla_pass(g)
                if r == 0:
                    for s, E in ((0, k_ctx), (1, k_out)):
                        act.wait_ge(zd_mm, 2 * g + s + 1)
                        for h in range(2):
                            col = VEC["b_dec"] + H1 * d + 2 * p + h
                            ins = run(E[:, T * h:T * h + T], bank[6 + s][:, T * h:T * h + T], ACT.Abs,
                                      bias=vec[:, col:col + 1])
                        ins.then_inc(z_abs, 1)
                    act.wait_ge(z_abs, 2 * g + 2)
                    run(k_ctx, k_ctx, ACT.Exp, scale=-1.0)
                    link(run(k_out, k_out, ACT.Exp, scale=-1.0))
                    run(k_ctx, k_ctx, ACT.Ln, bias=1.0).then_inc(z_log, 1)
                    run(k_out, k_out, ACT.Ln, bias=1.0).then_inc(z_log, 1)
                if r == 1:
                    act.wait_ge(scan_done, 2 * g + 1)
                    R, E = pair3(Dm), pair3(k_ctx)
                    lo, hi = slice(0, T - 1), slice(1, T)
                    run(E[:, :, lo] if d == 0 else E[:, :, hi], R[:, :, hi] if d == 0 else R[:, :, lo], ACT.Exp,
                        scale=1.0 / 16).then_inc(ex_done, 1)
                    act.wait_ge(dm_done, 2 * g + 1)
                    run(k_out, k_out, ACT.Exp, scale=1.0 / 16).then_inc(eq_done, 1)
                    act.wait_ge(dm_done, 2 * g + 2)
                    link(run(k_in, q_in, ACT.Exp, scale=-1.0 / 16))
                    run(q_in, q_in, ACT.Exp, scale=1.0 / 16).then_inc(eq_done, 1)
                    last = CH - 1 if d == 0 else 0
                    B4 = Bc.rearrange("p (c j) -> p c j", j=CH)
                    run(decay.unsqueeze(2), B4[:, :, last:last + 1], ACT.Exp, scale=1.0 / 16)
                    run(q_out, Bc, ACT.Exp, scale=1.0 / 16).then_inc(eq_done, 1)
                if r == 3:
                    act.wait_ge(ex_done, g + 1)
                    for s, dst in ((0, k_tokc), (1, k_tok)):
                        act.wait_ge(kt_tr, 2 * g + s + 1)
                        run(dst.rearrange("p a b c -> p (a b c)"), bank[6 + s][:]).then_inc(kt_sb, 1)

            def head_squares():
                act.wait_ge(o_mm, 1)
                for t in range(TT):
                    for h in range(H1):
                        j = 4 * t + h
                        ins = run(at(52, 2048)[:, HV * j:HV * j + HV],
                                  bank[2 * t + h // 2][:, HV * (h % 2):HV * (h % 2) + HV], ACT.Square,
                                  accum_out=oss[:, j:j + 1])
                    ins.then_inc(osq_done, 1)

            def ffn(f):
                u0, n0 = BASE_FFN[f], NF * f

                def silu(i, u, b):
                    act.wait_ge(unit_used, lin(3, i, u + 1))
                    run(sF, bank[b][:], ACT.Silu).then_inc(silu_done, 1)

                def high(i, m):
                    act.wait_ge(prod_done, lin(1, i, n0 + 1))
                    run(hidden_part(B_hi, m), hF).then_inc(fhi_done, 1)

                def step(i, m):
                    silu(i, u0, 4) if m else silu(0, u0 + 1, 0)
                    split(u0 + 3, i)
                    high(i, m)
                    split(u0 + 4, i)
                    split(u0 + 5, i)

                split(u0 + 2)
                step(0, 0)
                feed_forward_steps(act, f, step)
                silu(NF - 1, u0, 4)
                split(u0 + 3 * NF)
                high(NF - 1, NF - 1)
                split(u0 + 3 * NF + 1)

            def second():
                act.wait_ge(ang_done, 1)
                f2 = "p t r -> p (t r)"
                run(sin.rearrange(f2), ang, ACT.Sin)
                run(cos.rearrange(f2), nrd, ACT.Sin).then_inc(trig_done, 1)

                def evac2(n2):
                    kind, n = P2[n2]
                    b = BANKS2[n2]
                    act.wait_ge(unit_used, BASE_P2 + n2 + 1)
                    two = slice(2 * n, 2 * n + 2)
                    b3 = bank[b[0]][:].rearrange("p (m t) -> p m t", m=2)
                    if kind == "ql":
                        for t in range(TT):
                            run(T0[:, QR * t:QR * t + QR], b3[:, t, :], ACT.Square, accum_out=ss2[:, t:t + 1])
                        run(qlS, b3).then_inc(act_evac, 1)
                    if kind == "kl":
                        for t in range(TT):
                            run(T1[:, KVR * t:KVR * t + KVR], b3[:, t, 0:KVR], ACT.Square,
                                accum_out=ss2[:, TT + t:TT + t + 1])
                        run(klS, b3[:, :, 0:KVR + ROPE]).then_inc(act_evac, 1)
                    if kind in ("cq", "ck"):
                        run((caq if kind == "cq" else cak)[:, two, :], b3).then_inc(act_evac, 1)
                    if kind == "cv":
                        run(cav[:, :, UC * n:UC * n + UC], b3).then_inc(act_evac, 1)
                    if kind == "uq":
                        for t in range(TT):
                            for x in range(2):
                                ins = run(qf[:, t, 4 * x:4 * x + 4, :],
                                          bank[2 * t + x][:, 0:384].rearrange("p (h d) -> p h d", h=4))
                        ins.then_inc(act_evac, 1)
                    if kind == "ukv":
                        for t in range(TT):
                            for x in range(2):
                                src = bank[2 * t + x][:].rearrange("p (h d) -> p h d", h=4)
                                run(kf[:, t, 4 * x:4 * x + 4, 0:NOPE], src[:, :, 0:NOPE])
                                dst = vm[:, t, 4 * x * VD:(4 * x + 4) * VD].rearrange("p (h d) -> p h d", h=4)
                                ins = run(dst, src[:, :, NOPE:NOPE + VD])
                        ins.then_inc(act_evac, 1)
                    if kind in ("ga2", "gb2"):
                        run((siga2 if kind == "ga2" else sigb2)[:, two, :], b3).then_inc(act_evac, 1)
                    if kind == "brb":
                        for x in range(2):
                            act.wait_ge(mg_done, 4 + 2 * n + x + 1)
                            k = 4 * n + 2 * x
                            run(A_hi[:, k:k + 2, :], siga2[:, k:k + 2, :]).then_inc(mghi_done, 1)

                for n2 in range(N2):
                    if P2[n2 - 1] == ("brb", 0):
                        split(BASE_P2 + n2 + 2)
                    if n2:
                        evac2(n2 - 1)
                    if P2[n2 - 1] != ("brb", 0):
                        split(BASE_P2 + n2 + 2)
                    if n2 == 3:
                        act.wait_ge(lat_tr, 1)
                        for k in range(2):
                            c = VEC["mla_q_norm_2"] + k
                            run(latF[:, k, :], bank[6][:, T * k:T * k + T], scale=vec[:, c:c + 1])
                        act.wait_ge(lat_tr, 2)
                        c = VEC["mla_kv_norm_2"]
                        run(latF[:, 2, :], bank[7][:, 0:T], scale=vec[:, c:c + 1]).then_inc(lat_f, 1)
                        act.wait_ge(lat_f, 1)
                        run(B_hi[:, 0:3, :], latF).then_inc(lat_hi, 1)
                    for half in range(2):
                        g = head_group(n2, half)
                        if g is not None:
                            act.wait_ge(qk_tr, g + 1)
                            dst = (qT2 if g < 4 else kT2)[0:QH, 2 * (g % 4):2 * (g % 4) + 2, :]
                            run(dst, bank[6 + g % 2][0:QH, :].rearrange("p (h t) -> p h t", h=2)).then_inc(qk_sb, 1)
                        slot = job_slot(n2, half)
                        if slot is not None and slot < NJ:
                            j = slot
                            kind, t, heads = JOBS[j]
                            K = P * (t + 1)
                            act.wait_ge(jx_done, j + 1)
                            row = 2 * (kind == "ca") + t
                            for x, h in enumerate(heads):
                                v = Pb[j % 2][:, K * x:K * x + K]
                                ins = run(v, v, ACT.Exp, bias=mx[:, j % 2, x:x + 1], accum_out=sm[:, row, h:h + 1])
                            ins.then_inc(jp_done, 1)
                        if slot is not None and 2 <= slot < NJ + 2:
                            j = slot - 2
                            act.wait_ge(jt_mm, j + 1)
                            if j >= 2:
                                act.wait_ge(jo_mm, j - 1)
                            run(pT[j % 2], bank[7][:]).then_inc(jt_sb, 1)
                        if slot in (13, 14):
                            merge_high(0, slot - 13)
                    if P2[n2] in (("bra", 0), ("bra", 1)):
                        v = (siga2, sigb2)[P2[n2][1]]
                        act.wait_ge(act_evac, EV2[n2 - 1][1] if n2 == P2.index(("bra", 0)) else EV2[n2 - 2][1])
                        run(v, v, ACT.Sigmoid).then_inc(gates_done, 1)
                    if P2[n2] == ("bra", 1):
                        merge_high(1, 0)
                        merge_high(1, 1)
                partial_squares(5)
                evac2(N2 - 1)

            def merge_high(kk, m):
                g = 2 * kk + m
                act.wait_ge(ot_tr, g + 1)
                k = 4 * kk + 2 * m
                b = bank[6] if kk == 0 else bank[m]
                run(B_hi[:, k:k + 2, :], b[:].rearrange("p (m t) -> p m t", m=2)).then_inc(ohi_done, 1)

            act.wait_ge(c_in, 48)
            run(c3.rearrange("p k s -> p s k"), craw, ACT.Silu).then_inc(c_silu, 1)
            act.wait_ge(vec_tr, 1)
            run(vec[:, 0:NVEC], bank[6][:, 0:NVEC])
            run(bcol, bank[6][:, P:P + BROWS]).then_inc(vec_done, 1)
            squares(0)
            act.wait_ge(ada0_mm, 1)
            run(arow[:, 0:512], bank[0][0:2, :]).then_inc(ada0_row, 1)
            squares(1)
            for b in range(1, 4):
                if b == 3:
                    split(0)
                    split(1)
                act.wait_ge(ada0_mm, b + 1)
                run(arow[:, 512 * b:512 * b + 512], bank[b][0:2, :]).then_inc(ada0_row, 1)
            modulate(0)
            modulate(1)
            for u in range(N1):
                if u:
                    evac1(u - 1)
                first = GLA_U0 <= u <= GLA_U1 and (u - GLA_U0) % 4 == 0
                if first:
                    gla(2 * (u - GLA_U0))
                split(u + 2)
                if GLA_U0 <= u <= GLA_U1:
                    if not first:
                        gla(2 * (u - GLA_U0))
                    gla(2 * (u - GLA_U0) + 1)
                if P1[u - 1][0] == "ch" and P1[u - 1][1] < 3:
                    conv_high(P1[u - 1][1])
                if u == GLA_U1 + 1:
                    head_squares()
            partial_squares(2)
            evac1(N1 - 1)
            squares(2)
            modulate(2)
            ffn(0)
            for t in range(TT):
                act.wait_ge(y_added, t + 1)
                run(XN[:, t, :], X[:, t, :], ACT.Square, accum_out=ss[:, 12 + t:13 + t]).then_inc(fsq_done, 1)
            squares(3)
            modulate(3)
            ffn(1)
            squares(4)
            modulate(4)
            second()
            squares(5)
            modulate(5)
            ffn(2)
            for t in range(TT):
                act.wait_ge(y_added, TT + t + 1)
                run(XN[:, t, :], X[:, t, :], ACT.Square, accum_out=ss[:, 14 + t:15 + t]).then_inc(fsq_done, 1)

        @block.tensor
        def _(pe):
            def mm(o, l, r, start, stop, **kw):
                return nc.tensor.matmul(o, l, r, start=start, stop=stop, **kw)

            def three(o, w, x, stat_w, first, last, **kw):
                (wh, wl), (xh, xl) = w, x
                for j, (p, q) in enumerate(((wh, xh), (wh, xl), (wl, xh))):
                    l, r = (p, q) if stat_w else (q, p)
                    ins = mm(o, l, r, first and j == 0, last and j == 2, **kw)
                return ins

            def step_product(u, o, x, half, token_major, k, start, w0=None, check=True):
                s = ring(u)
                wh = whi[s][:].rearrange("p (k w) -> p k w", k=KD)
                wl = wlo[s][:].rearrange("p (k w) -> p k w", k=KD)
                ms = slice(P * half, P * half + P)
                if token_major:
                    w, xx = (wh[:, k, :], wl[:, k, :]), (x[0][:, k, ms], x[1][:, k, ms])
                else:
                    ws = ms if w0 is None else slice(w0, w0 + P)
                    w, xx = (wh[:, k, ws], wl[:, k, ws]), (x[0][:, k, :], x[1][:, k, :])
                return three(o, w, xx, not token_major, start, k == KD - 1, skip_group_check=not check)

            def product(u, o, x, half, token_major, w0=None):
                for k in range(KD):
                    ins = step_product(u, o, x, half, token_major, k, k == 0, w0)
                return ins

            def first_product(u, o, x, halves, token_major, low, before, w0=None):
                for b in range(KD // 2):
                    pe.wait_ge(low, before + b + 1)
                    for half in range(halves):
                        for k in (2 * b, 2 * b + 1):
                            ins = step_product(u, o[:, T * half:T * half + T], x, half, token_major, k,
                                               k == 0 and half == 0, w0, False)
                return ins

            A, B = (A_hi, A_lo), (B_hi, B_lo)

            def keep_warm(b, count):
                for _ in range(count):
                    mm(bank[b][:, 0:P], ones[:], ones[:], True, True)

            def norm(n):
                src = norm_source(n)
                if n >= 2:
                    keep_warm(6, WARM[0])
                for t, groups in ((0, (0, 1, 2)), (1, (0, 1, 2)), (0, (3,)), (1, (3,))):
                    pe.wait_ge(xn_done, 2 * n + t + 1)
                    for b in groups:
                        if n >= 2 and t == 0 and b == 3:
                            pe.wait_ge(as_done, n)
                        if n == 0 and t == 0 and b == 2:
                            pe.wait_ge(vec_done, 1)
                        if n == 0 and t == 0 and b == 3:
                            pe.wait_ge(ada0_row, 1)
                        if n == 1 and t == 0 and b == 3:
                            pe.wait_ge(h_done, 1)
                        for kk in range(2):
                            k = 2 * b + kk
                            c = T * kk + P * t
                            ins = nc.tensor.transpose(bank[norm_bank(n, b)][:, c:c + P], src[:, t, P * k:P * k + P],
                                                      ident)
                        if t == TT - 1:
                            ins.then_inc(tr_done, 1)
                if n >= 2:
                    keep_warm(3, WARM[1])

            def gate(r):
                g0 = GATE_UNITS[r]
                pe.wait_ge(*ada_done(g0 + 3))
                pe.wait_ge(gr_in, 16 * (r + 1))
                for x in range(2):
                    c = UC * ada_pos(g0) + 512 * x
                    ins = mm(bank[gate_bank(r) + x][:], ones[:], acc[:, c:c + 512], True, True)
                ins.then_inc(gr_mm, 1)

            def shift_and_scale(n, b):
                pe.wait_ge(*ada_done(NORM_UNITS[n][1] + 3))
                for x in range(2):
                    for k in range(KD):
                        c = UC * ada_pos(NORM_UNITS[n][x]) + P * k
                        ins = mm(bank[b][:, KD * x + k:KD * x + k + 1], acc[:, c:c + P], one, True, True)
                ins.then_inc(as_mm, 1)

            def wait_banks(u, before, ev):
                for v in before:
                    eng, count = ev[v]
                    pe.wait_ge(evac_sem[eng], count)

            def gla(slot):
                g, r = divmod(slot, 8)
                if r == 0 and g:
                    scan_step(g - 1, 3)
                if g >= 4:
                    return
                d, p, order = gla_pass(g)
                q3, k3 = pair3(q_in), pair3(k_in)
                if r == 0:
                    if g == 0:
                        pe.wait_ge(dec_in, 32)
                        pe.wait_ge(consts, 1)
                        pe.wait_ge(act_evac, EV1[7][1])
                    for s in range(2):
                        for h in range(2):
                            c = HK * (2 * p + h)
                            ins = mm(bank[6 + s][:, T * h:T * h + T], wdec[:, d, c:c + HK], ddT[:, 1 - s, :],
                                     True, True)
                        ins.then_inc(zd_mm, 1)
                if r == 3:
                    for s, src in ((0, pair3(k_ctx)), (1, pair3(k_out))):
                        if s == 0:
                            pe.wait_ge(kc_done, g + 1)
                        else:
                            pe.wait_ge(qk_done, 3 * g + 1)
                        for t in range(TT):
                            for h in range(2):
                                c = P * (2 * t + h)
                                ins = nc.tensor.transpose(bank[6 + s][:, c:c + P], src[:, h, P * t:P * t + P], ident)
                        ins.then_inc(kt_tr, 1)
                if r == 4:
                    pe.wait_ge(kt_sb, 2 * g + 1)
                    for h in range(2):
                        c = HV * (2 * p + h)
                        for t in range(TT):
                            ins = mm(bank[6][:, HV * h:HV * h + HV], k_tokc[:, t, h, :], v_c[:, t, c:c + HV],
                                     t == 0, t == TT - 1)
                    ins.then_inc(s0_mm, 1)
                    pe.wait_ge(kt_sb, 2 * g + 2)
                    pe.wait_ge(qk_done, 3 * g + 2)
                    for h in range(2):
                        for c in range(NC):
                            for x in range(2):
                                js = CH * c + CH // 2 * x
                                i0, ni = (CH * c, CH) if x == d else (js, CH // 2)
                                r0, c0 = js % P, P * (2 * (c // 2) + h) + i0 % P
                                ins = mm(bank[7][r0:r0 + CH // 2, c0:c0 + ni], k3[:, h, js:js + CH // 2],
                                         q3[:, h, i0:i0 + ni], True, True)
                    ins.then_inc(sc_mm, 1)
                if r == 5:
                    pe.wait_ge(sc_ready, g + 1)
                    for t in range(TT):
                        for h in range(2):
                            c = HV * (2 * p + h)
                            mm(bank[2 * t + p][:, HV * h:HV * h + HV], scT[:, t, h, :], v_l[:, t, c:c + HV],
                               d == 0 and h == 0, False, skip_group_check=True)
                if r >= 5:
                    scan_step(g, r - 5)

            def scan_step(g, n):
                d, p, order = gla_pass(g)
                c = order[n]
                t, off = c // 2, CH * (c % 2)
                rows = slice(off, off + CH)
                if n == 0:
                    pe.wait_ge(qk_done, 3 * g + 3)
                pe.wait_ge(s_ready, 4 * g + n + 1)
                for h in range(2):
                    ins = mm(bank[2 * t + p][rows, HV * h:HV * h + HV], pair3(q_out)[:, h, CH * c:CH * c + CH],
                             S[n % 2][:, h, :], False, True, skip_group_check=True)
                if g == 3 and n == 3:
                    ins.then_inc(o_mm, 1)
                if n < 3:
                    for h in range(2):
                        v0 = HV * (2 * p + h)
                        ins = mm(bank[6 + c % 2][:, HV * h:HV * h + HV], k_tok[rows, t, h, :],
                                 v_l[rows, t, v0:v0 + HV], True, True)
                    ins.then_inc(kv_mm, 1)

            def ffn(f):
                u0, n0 = BASE_FFN[f], NF * f

                def up(u, i, b):
                    pe.wait_ge(lo_ready, lin(3, i, u + 1))
                    for half in range(2):
                        ins = product(u, bank[b][:, T * half:T * half + T], A, half, False)
                    ins.then_inc(unit_used, 1)

                def down(u, i, m, first, last):
                    pe.wait_ge(lo_ready, lin(3, i, u + 1))
                    pe.wait_ge(flo_done, lin(1, i, n0 + 1))
                    s = ring(u)
                    wh = whi[s][:].rearrange("p (k w) -> p k w", k=2)
                    wl = wlo[s][:].rearrange("p (k w) -> p k w", k=2)
                    for t in range(TT):
                        for x in range(2):
                            for k in range(2):
                                ts, cs = slice(P * t, P * t + P), slice(512 * x, 512 * x + 512)
                                kb = 2 * (m % 3) + k
                                ins = three(bank[2 * t + x][:], (wh[:, k, cs], wl[:, k, cs]),
                                            (B_hi[:, kb, ts], B_lo[:, kb, ts]), False,
                                            first and k == 0, last and k == 1, skip_group_check=True)
                        if last and t == 0:
                            ins.then_inc(half_down, 1)
                    ins.then_inc(unit_used, 1)

                def step(i, m):
                    pe.wait_ge(prod_done, lin(1, i, n0 + 1))
                    up(u0 + 2, i, 4)
                    up(u0 + 3, i, 5)
                    down(u0 + 4, i, m, False, False)

                pe.wait_ge(lo_ready, u0 + 1)
                first_product(u0, bank[0], A, 2, False, hlo_done, 4 * (2 + f + (f == 2))).then_inc(unit_used, 1)
                up(u0 + 1, 0, 1)
                up(u0 + 2, 0, 4)
                up(u0 + 3, 0, 5)
                pe.wait_ge(prod_done, n0 + 1)
                down(u0 + 4, 0, 0, True, False)
                feed_forward_steps(pe, f, step)
                gate((1, 2, 4)[f])
                down(u0 + 2, NF - 1, NF - 1, False, True)
                if f < 2:
                    pe.wait_ge(gr_done, (1, 2)[f] + 1)
                    shift_and_scale(3 + f, 7)

            def second():
                def job(slot):
                    if slot < NJ:
                        kind, t, heads = JOBS[slot]
                        K = P * (t + 1)
                        if slot >= 2:
                            pe.wait_ge(js_sb, slot if slot == NJ - 1 else slot - 1)
                        for x, h in enumerate(heads):
                            if kind == "mla":
                                l, r = qT2[0:QH, h, P * t:P * t + P], kT2[0:QH, h, 0:K]
                            else:
                                rows = slice(64 * (h % 2), 64 * (h % 2) + 64)
                                l, r = caq[rows, h // 2, P * t:P * t + P], cak[rows, h // 2, 0:K]
                            ins = mm(bank[score_bank(slot)][:, K * x:K * x + K], l, r, True, True)
                        ins.then_inc(js_mm, 1)
                    if 2 <= slot < NJ + 2:
                        j = slot - 2
                        pe.wait_ge(jp_done, j + 1)
                        if j:
                            pe.wait_ge(jt_sb, j)
                        for c in range(4):
                            ins = nc.tensor.transpose(bank[7][:, P * c:P * c + P], Pb[j % 2][:, P * c:P * c + P], ident)
                        ins.then_inc(jt_mm, 1)
                    if 3 <= slot < NJ + 3:
                        j = slot - 3
                        kind, t, heads = JOBS[j]
                        pe.wait_ge(jt_sb, j + 1)
                        o = bank[t + 2 * (kind == "ca")]
                        v = vm if kind == "mla" else cav
                        for x, h in enumerate(heads):
                            for kt in range(t + 1):
                                c = P * (x * (t + 1) + kt)
                                ins = mm(o[:, VD * h:VD * h + VD], pT[j % 2][:, c:c + P], v[:, kt, VD * h:VD * h + VD],
                                         kt == 0, kt == t)
                        ins.then_inc(jo_mm, 1)

                def out_group(kk, m):
                    pe.wait_ge(osb_done, kk + 1)
                    b = bank[6] if kk == 0 else bank[m]
                    if kk == 0 and m == 0:
                        pe.wait_ge(js_sb, NJ)
                    if kk == 0 and m == 1:
                        pe.wait_ge(olo_done, 1)
                    o = osb if kk == 0 else osb2
                    for x in range(2):
                        for t in range(TT):
                            f0 = P * (2 * m + x)
                            ins = nc.tensor.transpose(b[:, T * x + P * t:T * x + P * t + P], o[:, t, f0:f0 + P], ident)
                    ins.then_inc(ot_tr, 1)

                for n2, (kind, n) in enumerate(P2):
                    u = BASE_P2 + n2
                    b = BANKS2[n2]
                    s = ring(u)
                    if (kind, n) == ("out2", 0):
                        gate(3)
                    pe.wait_ge(lo_ready, u + 1)
                    wait_banks(n2, BEFORE2[n2], EV2)
                    if kind in ("uq", "ukv"):
                        k0, nk, w = (0, 2, 768) if kind == "uq" else (2, 1, 1024)
                        pe.wait_ge(lat_lo, 1)
                        wh = whi[s][:, 0:nk * w].rearrange("p (k w) -> p k w", k=nk)
                        wl = wlo[s][:, 0:nk * w].rearrange("p (k w) -> p k w", k=nk)
                        for t in range(TT):
                            ts = slice(P * t, P * t + P)
                            for x in range(2):
                                cs = slice(x * w // 2, (x + 1) * w // 2)
                                for k in range(nk):
                                    ins = three(bank[2 * t + x][:, 0:w // 2], (wh[:, k, cs], wl[:, k, cs]),
                                                (B_hi[:, k0 + k, ts], B_lo[:, k0 + k, ts]), False,
                                                k == 0, k == nk - 1)
                        ins.then_inc(unit_used, 1)
                    elif kind in ("bra", "brb"):
                        kk = kind == "brb"
                        if n == 0 and not kk:
                            pe.wait_ge(jt_sb, NJ)
                        wh = whi[s][:].rearrange("p (k w) -> p k w", k=4)
                        wl = wlo[s][:].rearrange("p (k w) -> p k w", k=4)
                        for m in range(4):
                            for k in range(4):
                                if m == 0 and n == 0 and k % 2 == 0:
                                    pe.wait_ge(olo_done, 2 * kk + k // 2 + 1)
                                cs = slice(P * m, P * m + P)
                                ins = three(bank[b[m // 2]][:, T * (m % 2):T * (m % 2) + T],
                                            (wh[:, k, cs], wl[:, k, cs]),
                                            (B_hi[:, 4 * kk + k, :], B_lo[:, 4 * kk + k, :]), True,
                                            k == 0, k == 3)
                        ins.then_inc(unit_used, 1)
                    else:
                        first = {"ql": (hlo_done, 4 * 4), "out2": (mglo_done, 4)}
                        if kind in first and n == 0:
                            first_product(u, bank[b[0]], A, 2, True, *first[kind]).then_inc(unit_used, 1)
                            continue
                        for half in range(2):
                            ins = product(u, bank[b[0]][:, T * half:T * half + T], A, half, kind in TOKEN_MAJOR)
                            if half:
                                ins.then_inc(unit_used, 1)
                            after_half(n2, half, job, out_group)
                    if (kind, n) == ("out2", 2):
                        shift_and_scale(5, 0)
                    if kind == "ukv":
                        after_half(n2, 0, job, out_group)
                        after_half(n2, 1, job, out_group)
                    if (kind, n) == ("bra", 1):
                        out_group(1, 0)
                        out_group(1, 1)

            def after_half(n2, half, job, out_group):
                if n2 == 3 and half == 0:
                    pe.wait_ge(lat_n, 1)
                    for k in range(2):
                        for t in range(TT):
                            c = T * k + P * t
                            ins = nc.tensor.transpose(bank[6][:, c:c + P], qlS[:, t, P * k:P * k + P], ident)
                    ins.then_inc(lat_tr, 1)
                    pe.wait_ge(lat_n, 2)
                    for t in range(TT):
                        ins = nc.tensor.transpose(bank[7][:, P * t:P * t + P], klS[:, t, 0:KVR], ident)
                    ins.then_inc(lat_tr, 1)
                g = head_group(n2, half)
                if g is not None:
                    if g < 4:
                        pe.wait_ge(rope_done, 1)
                    else:
                        pe.wait_ge(rope_done, 2)
                        pe.wait_ge(act_evac, EV2[P2.index(("ukv", 0))][1])
                    if g >= 2:
                        pe.wait_ge(qk_sb, g - 1)
                    else:
                        pe.wait_ge(lat_hi, 1)
                    src = qf if g < 4 else kf
                    for h in range(2):
                        for t in range(TT):
                            c = P * (2 * h + t)
                            ins = nc.tensor.transpose(bank[6 + g % 2][0:QH, c:c + P], src[:, t, 2 * (g % 4) + h, :],
                                                      ident)
                    ins.then_inc(qk_tr, 1)
                slot = job_slot(n2, half)
                if slot is not None:
                    if slot == 0:
                        pe.wait_ge(qk_sb, 8)
                        pe.wait_ge(act_evac, EV2[P2.index(("ukv", 0))][1])
                    job(slot)
                    if slot in (13, 14):
                        out_group(0, slot - 13)

            pe.wait_ge(c_silu, 1)
            for j in range(8):
                if j == 4:
                    pe.wait_ge(ident_done, 1)
                    pe.wait_ge(vec_in, 16 * (len(VEC) + 2))
                    nc.tensor.transpose(bank[6][:, 0:NVEC], vrows[0:NVEC, :], ident[0:NVEC, 0:NVEC])
                    nc.tensor.transpose(bank[6][:, P:P + BROWS], brows[0:BROWS, :], ident[0:BROWS, 0:BROWS])\
                        .then_inc(vec_tr, 1)
                if j == 6:
                    norm(0)
                pe.wait_ge(start_ada[j], 16)
                for k in range(KD):
                    ins = mm(bank[j // 2][0:2, UC * (j % 2):UC * (j % 2) + UC], c3[:, k, 0:2], ada0[j][:, k, :],
                             k == 0, k == KD - 1)
                if j % 2:
                    ins.then_inc(ada0_mm, 1)
            for k in range(16):
                if k % 4 == 0:
                    pe.wait_ge(ada0_row, k // 4 + 1)
                ins = nc.tensor.transpose(bank[7][:, 2 * k:2 * k + 2], arow[:, P * k:P * k + P], ident[0:2, 0:2])
            ins.then_inc(as_mm, 1)
            norm(1)
            for u, (kind, n) in enumerate(P1):
                b = BANKS1[u]
                if kind == "mix_out" and n == 0:
                    gate(0)
                    shift_and_scale(2, 3)
                pe.wait_ge(lo_ready, u + 1)
                wait_banks(u, BEFORE1[u], EV1)
                x = B if kind in ("conv_out", "gla_out") else A
                if kind == "dd":
                    for x, low in ((1, 0), (0, 4)):
                        ins = first_product(u, bank[b[x]], (A, B)[x], 1, False, hlo_done, low, 0)
                    ins.then_inc(unit_used, 1)
                    continue
                first = {"conv_out": (vlo_done, 0), "gla_out": (onlo_done, 0), "mix_out": (mglo_done, 0)}
                if kind in first and n == 0:
                    if kind == "conv_out":
                        gla(2 * (u - GLA_U0))
                    first_product(u, bank[b[0]], x, 2, kind in TOKEN_MAJOR, *first[kind]).then_inc(unit_used, 1)
                    if kind == "conv_out":
                        gla(2 * (u - GLA_U0) + 1)
                    continue
                for half in range(2):
                    ins = product(u, bank[b[0]][:, T * half:T * half + T], x, half, kind in TOKEN_MAJOR)
                    if kind in DUAL:
                        ins = product(u, bank[b[1]][:, T * half:T * half + T], B, half, kind in TOKEN_MAJOR)
                    if half:
                        ins.then_inc(unit_used, 1)
                    if GLA_U0 <= u <= GLA_U1:
                        gla(2 * (u - GLA_U0) + half)
                if u == GLA_U1:
                    gla(32)
                if kind == "ga":
                    pe.wait_ge(gt_done, n + 1)
                    if n >= 2:
                        pe.wait_ge(onlo_done, n - 1)
                    for m in range(2):
                        for t in range(TT):
                            c = T * m + P * t
                            f0 = HV * n + P * m
                            ins = nc.tensor.transpose(bank[6 + n % 2][:, c:c + P], on[:, t, f0:f0 + P], ident)
                    ins.then_inc(ont_tr, 1)
            norm(2)
            ffn(0)
            norm(3)
            ffn(1)
            norm(4)
            second()
            norm(5)
            ffn(2)

        @block.vector
        def _(dve):
            n_chain = [0]

            def link(ins):
                n_chain[0] += 1
                ins.then_inc(dve_chain, 1)
                dve.wait_ge(dve_chain, n_chain[0])

            def tt(o, x, y, op):
                return nc.vector.tensor_tensor(o, x, y, op)

            def ts(o, x, s1, s2, op0, op1=ALU.bypass):
                if s2 is None:
                    return nc.vector.tensor_scalar(o, x, s1, None, op0)
                return nc.vector.tensor_scalar(o, x, s1, s2, op0, op1)

            def stt(o, x, sc, y, op0, op1):
                return nc.vector.scalar_tensor_tensor(out=o, in0=x, scalar=sc, in1=y, op0=op0, op1=op1)

            def rest(o, x, hi):
                return tt(o, x, hi.bitcast(F32), ALU.subtract)

            def split(u, i=0):
                if isinstance(i, int) and u + 3 * i >= UNITS:
                    return
                dve.wait_ge(hi_ready, lin(3, i, u + 1))
                rest(wlo[ring(u)][:], raw[ring(u)][:], whi[ring(u)][:]).then_inc(lo_ready, 1)

            def adapt(n, i, dst, blk):
                s = 0 if blk == 0 else 2
                arrived, count = ada_landing(n)
                dve.wait_ge(arrived, lin(16, i, count))
                for k in range(KD):
                    if k:
                        dve.wait_ge(ada_mac, lin(KD, i, KD * ada_order(n) + k))
                        ins = stt(dst, ada_raw[:, k, :], c3[:, k, s:s + 1], dst, ALU.mult, ALU.add)
                    else:
                        ins = ts(dst, ada_raw[:, k, :], c3[:, k, s:s + 1], None, ALU.mult)
                    ins.then_inc(ada_mac, 1)

            def columns(n, b, gain, bias0, src):
                dve.wait_ge(as_mm, max(1, n))
                for s in src:
                    if n < 2:
                        v = bank[b][:, 0:32].rearrange("p (k s) -> p k s", s=2)
                        sh, sc = v[:, 0:KD, s], v[:, KD:2 * KD, s]
                    else:
                        sh, sc = bank[b][:, 0:KD], bank[b][:, KD:2 * KD]
                    tt(shift[:, s, :], sh, bcol[:, bias0:bias0 + KD], ALU.add)
                    link(tt(scale[:, s, :], sc, bcol[:, bias0 + KD:bias0 + 2 * KD], ALU.add))
                    ins = stt(scale[:, s, :], scale[:, s, :], 1.0, vec[:, gain:gain + KD], ALU.add, ALU.mult)
                ins.then_inc(as_done, 1)

            def gate_row(r):
                dve.wait_ge(gr_mm, r + 1)
                for x in range(2):
                    g = GR[:, 512 * x:512 * x + 512]
                    ins = tt(g, g, bank[gate_bank(r) + x][:], ALU.add)
                ins.then_inc(gr_done, 1)

            def norm(n):
                src, dst = (ctxX if n == 0 else X), norm_source(n)
                for t in range(TT):
                    c = 2 * n + t
                    dve.wait_ge(rstd_done, c + 1)
                    ts(dst[:, t, :], src[:, t, :], rstd[:, c:c + 1], None, ALU.mult).then_inc(xn_done, 1)

            def affine(n, b):
                h, s = norm_fp32(n), 0
                dve.wait_ge(as_done, max(1, n))
                dve.wait_ge(tr_done, 4 * n + b + 1)
                for kk in range(2):
                    k = 2 * b + kk
                    ins = ts(h[:, k, :], bank[norm_bank(n, b)][:, kk * T:kk * T + T], scale[:, s, k:k + 1],
                             shift[:, s, k:k + 1], ALU.mult, ALU.add)
                ins.then_inc(h_dve, 1)

            def low(n, b):
                h, (hi, lo) = norm_fp32(n), norm_dest(n)
                dve.wait_ge(hhi_done, 4 * n + b + 1)
                k = slice(2 * b, 2 * b + 2)
                rest(lo[:, k, :], h[:, k, :], hi[:, k, :]).then_inc(hlo_done, 1)

            def norm_low(n):
                if n >= 2:
                    affine(n, 3)
                for b in range(4):
                    low(n, b)

            def conv(n):
                def tap(j, m):
                    c = VEC["w_conv"] + KD * j + 2 * n + m
                    return vec[:, c:c + 1]

                u4 = uS.rearrange("p (m r t) -> p m r t", m=2, t=CH)
                y4 = yS.rearrange("p (m r t) -> p m r t", m=2, t=CH)
                for m in range(2):
                    ins = ts(y4[:, m], u4[:, m], tap(1, m), None, ALU.mult)
                link(ins)
                for m in range(2):
                    y = y4[:, m, :, 1:CH]
                    ins = stt(y, u4[:, m, :, 0:CH - 1], tap(0, m), y, ALU.mult, ALU.add)
                link(ins)
                for m in range(2):
                    y = y4[:, m, :, 0:CH - 1]
                    ins = stt(y, u4[:, m, :, 1:CH], tap(2, m), y, ALU.mult, ALU.add)
                link(ins)
                tt(uS, cbS, yS, ALU.mult).then_inc(v_done, 1)
                dve.wait_ge(vhi_done, n + 1)
                rest(B_lo[:, 2 * n:2 * n + 2, :], uS.rearrange("p (m t) -> p m t", m=2), B_hi[:, 2 * n:2 * n + 2, :])\
                    .then_inc(vlo_done, 1)

            def evac1(u):
                kind, n = P1[u]
                b = BANKS1[u]
                two = slice(2 * n, 2 * n + 2)
                b3 = bank[b[0]][:].rearrange("p (m t) -> p m t", m=2)
                if kind == "ch":
                    dve.wait_ge(unit_used, u + 1)
                    dve.wait_ge(act_evac, EV1[u - 1][1])
                    ins = tt(uS, ccS, bank[b[0]][:], ALU.mult)
                    ins.then_inc(dve_evac, 1)
                    dve.wait_ge(dve_evac, EV1[u][1])
                    if n == 3:
                        conv(n)
                elif kind == "g":
                    dve.wait_ge(sig_done, n + 1)
                    if n:
                        dve.wait_ge(gt_done, n)
                    ins = tt(T1, T0, bank[b[0]][:], ALU.mult)
                    ins.then_inc(dve_evac, 1)
                    dve.wait_ge(dve_evac, EV1[u][1])
                    dve.wait_ge(on_done, 8)
                    o = on[:, :, HV * n:HV * n + HV]
                    tt(o, o, T1.rearrange("p (t d) -> p t d", t=TT), ALU.mult).then_inc(gt_done, 1)
                elif kind == "ga":
                    dve.wait_ge(onhi_done, n + 1)
                    rest(B_lo[:, two, :], bank[6 + n % 2][:].rearrange("p (m t) -> p m t", m=2), B_hi[:, two, :])\
                        .then_inc(onlo_done, 1)
                elif kind == "gla_out":
                    T = (T0, T1)[n % 2]
                    T3 = T.rearrange("p (m t) -> p m t", m=2)
                    dve.wait_ge(unit_used, u + 1)
                    tt(T3, b3, siga[:, two, :], ALU.mult).then_inc(dve_evac, 1)
                    dve.wait_ge(dve_evac, EV1[u][1])
                    dve.wait_ge(yb_done, n + 1)
                    tt(T3, T3, yT[:, two, :], ALU.add).then_inc(mg_done, 1)
                    dve.wait_ge(mghi_done, n + 1)
                    rest(A_lo[:, two, :], T3, A_hi[:, two, :]).then_inc(mglo_done, 1)
                elif kind == "mix_out":
                    residual(u, n, b[0], EV1[u][1], Xr)

            def residual(u, n, b, count, old):
                T = (T0, T1)[n % 2].rearrange("p (t d) -> p t d", t=TT)
                cs = slice(UC * n, UC * n + UC)
                dve.wait_ge(unit_used, u + 1)
                if n >= 2:
                    dve.wait_ge(x_part, n - 1 if old is Xr else n + 2)
                g = GR[:, cs].unsqueeze(1).to_broadcast([P, TT, UC])
                tt(T, bank[b][:].rearrange("p (t d) -> p t d", t=TT), g, ALU.mult).then_inc(dve_evac, 1)
                dve.wait_ge(dve_evac, count)
                if old is Xr and n == 0:
                    dve.wait_ge(xr_in, 16)
                if n < 3:
                    tt(X[:, :, cs], old[:, :, cs], T, ALU.add).then_inc(x_part, 1)
                else:
                    for t in range(TT):
                        tt(X[:, t, cs], old[:, t, cs], T[:, t, :], ALU.add).then_inc(x_ready, 1)

            def gla(slot):
                g, r = divmod(slot, 8)
                if g >= 4:
                    return
                d, p, order = gla_pass(g)
                if slot == 0:
                    dve.wait_ge(consts, 1)
                if r == 0:
                    for s, M in ((0, k_in), (1, q_out)):
                        dve.wait_ge(z_abs, 2 * g + s + 1)
                        for h in range(2):
                            col = VEC["b_dec"] + H1 * d + 2 * p + h
                            ts(M[:, T * h:T * h + T], bank[6 + s][:, T * h:T * h + T], vec[:, col:col + 1], 0.0,
                               ALU.add, ALU.min).then_inc(z_min, 1)
                    for s, M, E in ((0, k_in, k_ctx), (1, q_out, k_out)):
                        dve.wait_ge(z_min, 4 * g + 2 * s + 2)
                        dve.wait_ge(z_log, 2 * g + s + 1)
                        link(tt(M, M, E, ALU.subtract))
                        if s == 0:
                            M3, R3 = pair3(M), pair3(Dm)
                            for h in range(2):
                                if d == 0:
                                    ins = nc.vector.tensor_tensor_scan(R3[:, h, ::-1], ones256, M3[:, h, ::-1], 0.0,
                                                                       ALU.mult, ALU.add)
                                else:
                                    ins = nc.vector.tensor_tensor_scan(R3[:, h, :], ones256, M3[:, h, :], 0.0,
                                                                       ALU.mult, ALU.add)
                        elif d == 0:
                            ins = nc.vector.tensor_tensor_scan(Bc, msk64, M, 0.0, ALU.mult, ALU.add)
                        else:
                            ins = nc.vector.tensor_tensor_scan(Bc[:, ::-1], msk64, M[:, ::-1], 0.0, ALU.mult, ALU.add)
                        ins.then_inc(scan_done, 1)
                    B3, K3, D3 = (v.rearrange("p (c j) -> p c j", j=CH) for v in (Bc, k_out, q_in))
                    mid, last = (CH // 2 - 1, CH - 1) if d == 0 else (CH // 2, 0)
                    dve.wait_ge(scan_done, 2 * g + 2)
                    tt(K3, B3[:, :, last:last + 1].to_broadcast([P, 8, CH]), B3, ALU.subtract).then_inc(dm_done, 1)
                    tt(D3, B3, B3[:, :, mid:mid + 1].to_broadcast([P, 8, CH]), ALU.subtract).then_inc(dm_done, 1)
                if r == 1:
                    dve.wait_ge(ex_done, g + 1)
                    kc3, EX = kTc[:, 2 * p:2 * p + 2, :], pair3(k_ctx)
                    lo, edge = (slice(0, T - 1), slice(T - 1, T)) if d == 0 else (slice(1, T), slice(0, 1))
                    tt(EX[:, :, lo], EX[:, :, lo], kc3[:, :, lo], ALU.mult)
                    nc.vector.tensor_copy(EX[:, :, edge], kc3[:, :, edge]).then_inc(kc_done, 1)
                if r == 4:
                    dve.wait_ge(s0_mm, g + 1)
                    nc.vector.tensor_copy(S[0].rearrange("p h d -> p (h d)"), bank[6][:]).then_inc(s_ready, 1)
                    dve.wait_ge(sc_mm, g + 1)
                    m = causal[d].bitcast(U32).unsqueeze(1).to_broadcast([P, 4, P])
                    s4 = scT.rearrange("p a b c -> p (a b) c")
                    if p == 0:
                        link(nc.vector.memset(scT.rearrange("p a b c -> p (a b c)"), 0.0))
                    nc.vector.copy_predicated(s4, m, bank[7][:].rearrange("p (a c) -> p a c", a=4))\
                        .then_inc(sc_ready, 1)
                if r >= 5:
                    n = r - 5
                    c = order[n]
                    if n == 0:
                        dve.wait_ge(eq_done, 3 * g + 3)
                    dve.wait_ge(kv_mm, 3 * g + n + 1)
                    dve.wait_ge(s_ready, 4 * g + n + 1)
                    for h in range(2):
                        j = NC * h + c
                        ins = stt(S[(n + 1) % 2][:, h, :], S[n % 2][:, h, :], decay[:, j:j + 1],
                                  bank[6 + c % 2][:, HV * h:HV * h + HV], ALU.mult, ALU.add)
                    ins.then_inc(s_ready, 1)

            def norm_heads():
                dve.wait_ge(gh_in, 16)
                for t in range(TT):
                    dve.wait_ge(orstd_done, t + 1)
                    for h in range(H1):
                        stt(on[:, t, HV * h:HV * h + HV], bank[2 * t + h // 2][:, HV * (h % 2):HV * (h % 2) + HV],
                            orstd[:, 4 * t + h:4 * t + h + 1], ghb, ALU.mult, ALU.mult).then_inc(on_done, 1)

            def ffn(f):
                u0, n0 = BASE_FFN[f], NF * f

                def product(i, b):
                    dve.wait_ge(silu_done, lin(1, i, n0 + 1))
                    if i != 0 or n0:
                        dve.wait_ge(flo_done, lin(1, i, n0))
                    tt(hF, sF, bank[b][:], ALU.mult).then_inc(prod_done, 1)

                def low(i, m):
                    dve.wait_ge(fhi_done, lin(1, i, n0 + 1))
                    rest(hidden_part(B_lo, m), hF, hidden_part(B_hi, m)).then_inc(flo_done, 1)

                def step(i, m):
                    product(i, 5 if m else 1)
                    split(u0 + 3, i)
                    low(i, m)
                    split(u0 + 4, i)
                    if f < 2:
                        n1 = NADA1 + NADAF * f
                        if isinstance(i, int):
                            dst = acc[:, UC * (NADAF * f + i):UC * (NADAF * f + i) + UC]
                        else:
                            dst = acc[:, bass.ds(lin(UC, i, UC * NADAF * f), UC)]
                        adapt(n1, i, dst, ADA[n1 + m][0])
                    elif m in LAST_STEPS and i == m:
                        n1 = ADA_LAST + LAST_STEPS.index(m)
                        adapt(n1, 0, acc[:, UC * ada_pos(n1):UC * ada_pos(n1) + UC], ADA[n1][0])
                    split(u0 + 5, i)

                split(u0 + 2)
                step(0, 0)
                feed_forward_steps(dve, f, step)
                product(NF - 1, 5)
                split(u0 + 3 * NF)
                low(NF - 1, NF - 1)
                r, n, q = ((1, 3, 0), (2, 4, None), (4, None, 1))[f]
                gate_row(r)
                dve.wait_ge(gr_done, r + 1)
                for t in range(TT):
                    if t == 0:
                        dve.wait_ge(half_down, f + 1)
                    else:
                        dve.wait_ge(unit_used, u0 + 3 * NF)
                    for x in range(2):
                        cs = slice(512 * x, 512 * x + 512)
                        ins = stt(yF[2 * t + x], bank[2 * t + x][:], 0.5 if f else 1.0, GR[:, cs], ALU.mult, ALU.mult)
                    link(ins)
                    for x in range(2):
                        cs = slice(512 * x, 512 * x + 512)
                        ins = tt(X[:, t, cs], X[:, t, cs], yF[2 * t + x], ALU.add)
                    if q is None:
                        ins.then_inc(x_ready, 1)
                    else:
                        ins.then_inc(y_added, 1)
                if q is not None:
                    dve.wait_ge(fin_in, 16 * (q + 1))
                    for t in range(TT):
                        c = 12 + 2 * q + t
                        dve.wait_ge(frs_done, 2 * q + t + 1)
                        if q == 0:
                            stt(X[:, t, :], X[:, t, :], rstd[:, c:c + 1], finrow[q], ALU.mult, ALU.mult)\
                                .then_inc(x_ready, 1)
                        else:
                            stt(XN[:, t, :], X[:, t, :], rstd[:, c:c + 1], finrow[q], ALU.mult, ALU.mult)\
                                .then_inc(out_done, 1)

            def bias_col(n):
                blk, c0 = ADA[NORM_UNITS[n][0]]
                return (0 if blk == 0 else 48) + c0 // P

            def second():
                dve.wait_ge(pos_in, 16)
                dve.wait_ge(inv_done, 1)
                link(nc.vector.tensor_copy(posf, posi.bitcast(I32)))
                for t in range(TT):
                    ins = ts(ang[:, HR * t:HR * t + HR], inv, posf[:, t:t + 1], None, ALU.mult)
                link(ins)
                magic = 12582912.0
                link(ts(nrd, ang, 1.0 / (2 * math.pi), magic, ALU.mult, ALU.add))
                link(ts(nrd, nrd, magic, None, ALU.subtract))
                for part in TURN:
                    link(stt(ang, nrd, -part, ang, ALU.mult, ALU.add))
                link(ts(ang, ang, 3.1415925, -3.1415925, ALU.min, ALU.max))
                link(stt(nrd, ang, -1.0, ang, ALU.mult, ALU.max))
                ts(nrd, nrd, -1.0, math.pi / 2, ALU.mult, ALU.add).then_inc(ang_done, 1)

                def evac2(n2):
                    kind, n = P2[n2]
                    u = BASE_P2 + n2
                    b = BANKS2[n2]
                    if kind == "uq":
                        dve.wait_ge(act_evac, EV2[n2][1])
                        dve.wait_ge(trig_done, 1)
                        rotate(qf[:, :, :, NOPE:NOPE + HR], qf[:, :, :, NOPE + HR:QH], H2, None)
                        rotate(klS[:, :, KVR:KVR + HR], klS[:, :, KVR + HR:KVR + ROPE], 1, kf)
                    if kind == "bra":
                        dve.wait_ge(gates_done, 1)
                        dve.wait_ge(unit_used, u + 1)
                        for x in range(2):
                            v = siga2[:, 4 * n + 2 * x:4 * n + 2 * x + 2, :]
                            ins = tt(v, bank[b[x]][:].rearrange("p (m t) -> p m t", m=2), v, ALU.mult)
                        ins.then_inc(dve_evac, 1)
                    if kind == "brb":
                        dve.wait_ge(gates_done, 2)
                        dve.wait_ge(unit_used, u + 1)
                        for x in range(2):
                            k = slice(4 * n + 2 * x, 4 * n + 2 * x + 2)
                            v = sigb2[:, k, :]
                            ins = tt(v, bank[b[x]][:].rearrange("p (m t) -> p m t", m=2), v, ALU.mult)
                            if x == 0:
                                link(ins)
                            else:
                                ins.then_inc(dve_evac, 1)
                                dve.wait_ge(dve_evac, EV2[n2][1])
                            tt(siga2[:, k, :], siga2[:, k, :], sigb2[:, k, :], ALU.add).then_inc(mg_done, 1)
                        if n == 0:
                            split(BASE_P2 + n2 + 3)
                        for x in range(2):
                            k = slice(4 * n + 2 * x, 4 * n + 2 * x + 2)
                            dve.wait_ge(mghi_done, 4 + 2 * n + x + 1)
                            rest(A_lo[:, k, :], siga2[:, k, :], A_hi[:, k, :]).then_inc(mglo_done, 1)
                    if kind == "out2":
                        residual(u, n, b[0], EV2[n2][1], X)

                def rotate(x1, x2, heads, spread):
                    if spread is None:
                        r, c, s = rot, cos.unsqueeze(2).to_broadcast([P, TT, H2, HR]), \
                            sin.unsqueeze(2).to_broadcast([P, TT, H2, HR])
                    else:
                        r, c, s = [v[:, :, 0, :] for v in rot], cos, sin
                    tt(r[0], x1, c, ALU.mult)
                    tt(r[1], x2, s, ALU.mult)
                    tt(r[2], x1, s, ALU.mult)
                    link(tt(r[3], x2, c, ALU.mult))
                    if spread is None:
                        o1, o2 = x1, x2
                    else:
                        o1, o2 = spread[:, :, :, NOPE:NOPE + HR], spread[:, :, :, NOPE + HR:QH]
                        r = [v.unsqueeze(2).to_broadcast([P, TT, H2, HR]) for v in r]
                    tt(o1, r[0], r[1], ALU.subtract)
                    ins = tt(o2, r[2], r[3], ALU.add)
                    ins.then_inc(rope_done, 1)
                    dve.wait_ge(rope_done, 1 if spread is None else 2)

                def job(j):
                    kind, t, heads = JOBS[j]
                    K, nh = P * (t + 1), len(heads)
                    dve.wait_ge(js_mm, j + 1)
                    if j >= 2:
                        dve.wait_ge(jt_mm, j - 1)
                    s3 = Pb[j % 2].rearrange("p (h k) -> p h k", h=nh)
                    b3 = bank[score_bank(j)][:].rearrange("p (h k) -> p h k", h=nh)
                    if kind == "mla":
                        ins = ts(s3, b3, float(QH) ** -0.5, None, ALU.mult)
                    else:
                        bias = U.rearrange("p (k h) -> p h k", h=H2)
                        bias = bias[:, heads[0]:heads[0] + 2 * nh - 1:2, 0:K][:, :, ::-1]
                        ins = stt(s3, b3, float(VD) ** -0.5, bias, ALU.mult, ALU.add)
                    ins.then_inc(js_sb, 1)
                    dve.wait_ge(js_sb, j + 1)
                    link(nc.vector.memset(s3[0:CH, :, K - CH:K], NEG))
                    m = mx[:, j % 2, 0:nh]
                    link(nc.vector.tensor_reduce(m, s3, AX.X, ALU.max))
                    ts(m, m, -1.0, None, ALU.mult).then_inc(jx_done, 1)

                def heads_out(kk, o):
                    dve.wait_ge(jo_mm, 6 * kk + 6)
                    for t in range(TT):
                        ins = nc.vector.reciprocal(rin[:, 2 * kk + t, :], sm[:, 2 * kk + t, :])
                    link(ins)
                    for t in range(TT):
                        ins = tt(o[:, t, :].rearrange("p (h d) -> p h d", h=H2),
                                 bank[2 * kk + t][:].rearrange("p (h d) -> p h d", h=H2),
                                 rin[:, 2 * kk + t, :].unsqueeze(2).to_broadcast([P, H2, VD]), ALU.mult)
                    ins.then_inc(osb_done, 1)

                def merge_low(kk, m):
                    k = slice(4 * kk + 2 * m, 4 * kk + 2 * m + 2)
                    b = bank[6] if kk == 0 else bank[m]
                    dve.wait_ge(ohi_done, 2 * kk + m + 1)
                    rest(B_lo[:, k, :], b[:].rearrange("p (m t) -> p m t", m=2), B_hi[:, k, :]).then_inc(olo_done, 1)

                for n2 in range(N2):
                    if n2:
                        evac2(n2 - 1)
                    if job_slot(n2, 0) is None and P2[n2 - 1] != ("brb", 0):
                        split(BASE_P2 + n2 + 2)
                    if n2 == 2:
                        for j, (v, w) in enumerate(((qlS, QR), (klS, KVR))):
                            dve.wait_ge(lat_rs, j + 1)
                            dve.wait_ge(act_evac, EV2[j][1])
                            for t in range(TT):
                                ins = ts(v[:, t, 0:w], v[:, t, 0:w], rs2[:, 2 * j + t:2 * j + t + 1], None, ALU.mult)
                            ins.then_inc(lat_n, 1)
                    if n2 == 3:
                        dve.wait_ge(lat_hi, 1)
                        rest(B_lo[:, 0:3, :], latF, B_hi[:, 0:3, :]).then_inc(lat_lo, 1)
                    for half in range(2):
                        slot = job_slot(n2, half)
                        if slot is not None and slot < NJ:
                            if slot == 6:
                                dve.wait_ge(u_in, 16)
                            job(slot)
                        if slot is not None and half == 0:
                            split(BASE_P2 + n2 + 2)
                        if slot == 10:
                            heads_out(0, osb)
                        if slot in (13, 14):
                            merge_low(0, slot - 13)
                        if slot == 15:
                            heads_out(1, osb2)
                    if P2[n2] == ("bra", 1):
                        merge_low(1, 0)
                        merge_low(1, 1)
                    if n2 in ADA2_STEP:
                        n = ADA_P2 + ADA2_STEP.index(n2)
                        adapt(n, 0, acc[:, UC * ada_pos(n):UC * ada_pos(n) + UC], ADA[n][0])
                    if P2[n2] == ("out2", 0):
                        gate_row(3)
                        dve.wait_ge(gr_done, 4)
                    if P2[n2] == ("out2", 3):
                        columns(5, 0, VEC["ffn2_norm_2"], bias_col(5), (0,))
                evac2(N2 - 1)

            norm(0)
            norm(1)
            split(0)
            dve.wait_ge(vec_done, 1)
            columns(0, 7, VEC["g_mix"], 0, (0, 1))
            for b in range(4):
                low(0, b)
                affine(1, b)
            norm_low(1)
            split(1)
            for u in range(N1):
                if u:
                    evac1(u - 1)
                part = (u - GLA_U0) % 4 if GLA_U0 <= u <= GLA_U1 else None
                if part in (0, 2, 3):
                    gla(2 * (u - GLA_U0))
                if part == 0:
                    gla(2 * (u - GLA_U0) + 1)
                split(u + 2)
                if part == 1:
                    gla(2 * (u - GLA_U0))
                if part in (1, 2, 3):
                    gla(2 * (u - GLA_U0) + 1)
                if P1[u - 1][0] == "ch" and P1[u - 1][1] < 3:
                    conv(P1[u - 1][1])
                if u == GLA_U1 + 1:
                    norm_heads()
                if P1[u] == ("mix_out", 0):
                    gate_row(0)
                    columns(2, 3, VEC["g_ffn"], bias_col(2), (0,))
                    dve.wait_ge(gr_done, 1)
            evac1(N1 - 1)
            norm(2)
            norm_low(2)
            ffn(0)
            norm(3)
            columns(3, 7, VEC["ffn1_norm_2"], bias_col(3), (0,))
            norm_low(3)
            split(BASE_FFN[1] + 1)
            ffn(1)
            norm(4)
            columns(4, 7, VEC["mix_norm_2"], bias_col(4), (0,))
            norm_low(4)
            split(BASE_P2 + 1)
            second()
            norm(5)
            norm_low(5)
            ffn(2)


def turn_parts():
    left, parts = 2 * math.pi, []
    for _ in range(4):
        e = math.floor(math.log2(left))
        step = 2.0 ** (e - 7)
        p = math.floor(left / step) * step
        parts.append(p)
        left -= p
    return parts


TURN = turn_parts()

INS = ["x", "c", "ctx", "c_ctx", "w_ada", "b_ada", "g_mix", "w_in", "w_dec_up", "b_dec", "g_head", "w_gla_out",
       "w_conv", "w_conv_out", "w_mix_out", "g_ffn", "w_ffn_in", "w_ffn_out", "g_final", "c_2", "positions_2",
       "w_ada_2", "b_ada_2", "ffn1_norm_2", "ffn1_w_in_2", "ffn1_w_out_2", "mix_norm_2", "w_in_2", "mla_q_norm_2",
       "mla_w_uq_2", "mla_kv_norm_2", "mla_w_ukv_2", "rel_bias_2", "w_branch_a_2", "w_branch_b_2", "w_out_2",
       "ffn2_norm_2", "ffn2_w_in_2", "ffn2_w_out_2", "final_norm_2"]


def kernel(**inputs):
    import numpy as np
    import concourse.bacc as bacc
    from concourse.bass_utils import run_bass_kernel_spmd as launch

    nc = bacc.Bacc("TRN2", target_bir_lowering=False, num_devices=1)
    arrays, args = {}, {}
    for name in INS:
        v = np.ascontiguousarray(inputs[name])
        arrays[f"in_{name}"] = v
        args[name] = nc.dram_tensor(f"in_{name}", v.shape, mybir.dt.from_np(v.dtype), kind="ExternalInput").ap()
    out = nc.dram_tensor("out_0", (1, T, D), F32, kind="ExternalOutput").ap()
    build(nc, args, out)
    r = launch(nc, [arrays], core_ids=[0])
    return r.results[0]["out_0"]
```
